# Optimizing a Trainium2 kernel written in Bass

```python
import jax
import jax.numpy as jnp
from jax import lax
import numpy as np

D_MODEL = 1024
BATCH = 1
SEQ = 2048
DEPTH = 1

N_MIXERS = 4
EPS = 1e-6
Q_BLOCK = 128
CHUNK = 64
ML_HEADS = 8
ML_DV = D_MODEL // ML_HEADS
ML_DQK = D_MODEL // (2 * ML_HEADS)
SB_HEADS = 16
SB_DH = D_MODEL // SB_HEADS
FX_HEADS = 16
FX_DH = D_MODEL // FX_HEADS
GLA_HEADS = 4
GLA_DK = D_MODEL // (2 * GLA_HEADS)
GLA_DV = D_MODEL // GLA_HEADS
GLA_RANK = 16
GLA_TAU = 16.0
D_FF = ((8 * D_MODEL + 3 * 256 - 1) // (3 * 256)) * 256
ML_IN = 2 * ML_HEADS * ML_DQK + 2 * ML_HEADS * ML_DV + 2 * ML_HEADS
SB_IN = 3 * SB_HEADS * SB_DH
FX_IN = 4 * FX_HEADS * FX_DH + FX_HEADS
GLA_IN = 2 * GLA_HEADS * GLA_DK + 2 * GLA_HEADS * GLA_DV + GLA_RANK

kernel_name = 'hybrid_mlstm_stickbreak_fox_gla_trunk'

def _rms(t):
    tf = t.astype(jnp.float32)
    return (tf * lax.rsqrt(jnp.mean(tf * tf, axis=-1, keepdims=True) + EPS)).astype(t.dtype)

def rmsnorm(t, g):
    return _rms(t) * g

def split_heads(t, n_heads):
    b, s, w = t.shape
    return t.reshape(b, s, n_heads, w // n_heads).transpose(0, 2, 1, 3)

def merge_heads(t):
    b, h, s, d = t.shape
    return t.transpose(0, 2, 1, 3).reshape(b, s, h * d)

def to_blocks(t, size):
    b, h, s = t.shape[:3]
    return jnp.moveaxis(t.reshape(b, h, s // size, size, *t.shape[3:]), 2, 0)

def from_blocks(t):
    nb, b, h, size = t.shape[:4]
    return jnp.moveaxis(t, 0, 2).reshape(b, h, nb * size, *t.shape[4:])

def mlstm_mixer(u, w_in, b_if, norm_g, w_out):
    nq = ML_HEADS * ML_DQK
    nv = ML_HEADS * ML_DV
    q, k, v, o_pre, if_pre = jnp.split(u @ w_in, [nq, 2 * nq, 2 * nq + nv, 2 * nq + 2 * nv], axis=-1)
    q = split_heads(q, ML_HEADS)
    k = split_heads(k, ML_HEADS) * (ML_DQK ** -0.5)
    v = split_heads(v, ML_HEADS)
    gates = (if_pre + b_if).astype(jnp.float32).transpose(0, 2, 1)
    log_i = gates[:, :ML_HEADS]
    log_f = jax.nn.log_sigmoid(gates[:, ML_HEADS:])
    causal = jnp.tril(jnp.ones((CHUNK, CHUNK), dtype=bool))
    b = u.shape[0]

    def step(carry, inp):
        c_st, n_st, m_st = carry
        qc, kc, vc, li, lf = inp
        cum_f = jnp.cumsum(lf, axis=-1)
        tot_f = cum_f[..., -1]
        log_d = jnp.where(causal, cum_f[..., :, None] - cum_f[..., None, :] + li[..., None, :], -jnp.inf)
        log_inter = cum_f + m_st[..., None]
        m_t = jnp.maximum(log_inter, jnp.max(log_d, axis=-1))
        w_inter = jnp.exp(log_inter - m_t)
        scores = jnp.einsum('bhtd,bhsd->bhts', qc, kc) * jnp.exp(log_d - m_t[..., None])
        num = w_inter[..., None] * jnp.einsum('bhtd,bhde->bhte', qc, c_st) + jnp.einsum('bhts,bhse->bhte', scores, vc)
        den = w_inter * jnp.einsum('bhtd,bhd->bht', qc, n_st) + jnp.sum(scores, axis=-1)
        h = num / jnp.maximum(jnp.abs(den), jnp.exp(-m_t))[..., None]
        log_w = tot_f[..., None] - cum_f + li
        m_new = jnp.maximum(tot_f + m_st, jnp.max(log_w, axis=-1))
        decay = jnp.exp(tot_f + m_st - m_new)
        w_k = jnp.exp(log_w - m_new[..., None])[..., None] * kc
        c_st = decay[..., None, None] * c_st + jnp.einsum('bhsd,bhse->bhde', w_k, vc)
        n_st = decay[..., None] * n_st + jnp.sum(w_k, axis=2)
        return (c_st, n_st, m_new), h

    init = (jnp.zeros((b, ML_HEADS, ML_DQK, ML_DV), jnp.float32),
            jnp.zeros((b, ML_HEADS, ML_DQK), jnp.float32),
            jnp.zeros((b, ML_HEADS), jnp.float32))
    _, h = lax.scan(step, init, (to_blocks(q, CHUNK), to_blocks(k, CHUNK), to_blocks(v, CHUNK),
                                 to_blocks(log_i, CHUNK), to_blocks(log_f, CHUNK)))
    h = merge_heads(_rms(from_blocks(h))).astype(u.dtype) * norm_g
    return (h * jax.nn.sigmoid(o_pre)) @ w_out

def stick_breaking_mixer(u, w_in, w_out):
    q, k, v = jnp.split(u @ w_in, 3, axis=-1)
    q, k, v = split_heads(q, SB_HEADS), split_heads(k, SB_HEADS), split_heads(v, SB_HEADS)
    s = u.shape[1]
    k_pos = jnp.arange(s)
    scale = SB_DH ** -0.5

    def block(args):
        q_blk, blk = args
        z = jnp.einsum('bhtd,bhsd->bhts', q_blk, k).astype(jnp.float32) * scale
        q_pos = blk * Q_BLOCK + jnp.arange(Q_BLOCK)
        mask = k_pos[None, :] < q_pos[:, None]
        log_1m = jnp.where(mask, -jax.nn.softplus(z), 0.0)
        log_keep = lax.cumsum(log_1m, axis=3, reverse=True) - log_1m
        a = jnp.where(mask, jnp.exp(jax.nn.log_sigmoid(z) + log_keep), 0.0)
        return jnp.einsum('bhts,bhsd->bhtd', a.astype(v.dtype), v)

    out = lax.map(block, (to_blocks(q, Q_BLOCK), jnp.arange(s // Q_BLOCK)))
    return merge_heads(from_blocks(out)) @ w_out

def forgetting_attn_mixer(u, w_in, b_f, q_norm_g, k_norm_g, w_out):
    w = FX_HEADS * FX_DH
    q, k, v, o_pre, f_pre = jnp.split(u @ w_in, [w, 2 * w, 3 * w, 4 * w], axis=-1)
    q = rmsnorm(split_heads(q, FX_HEADS), q_norm_g)
    k = rmsnorm(split_heads(k, FX_HEADS), k_norm_g)
    v = split_heads(v, FX_HEADS)
    log_f = jax.nn.log_sigmoid((f_pre + b_f).astype(jnp.float32)).transpose(0, 2, 1)
    cum_f = jnp.cumsum(log_f, axis=-1)
    s = u.shape[1]
    k_pos = jnp.arange(s)
    scale = FX_DH ** -0.5

    def block(args):
        q_blk, cf_blk, blk = args
        logits = (jnp.einsum('bhtd,bhsd->bhts', q_blk, k).astype(jnp.float32) * scale
                  + cf_blk[..., :, None] - cum_f[..., None, :])
        q_pos = blk * Q_BLOCK + jnp.arange(Q_BLOCK)
        mask = k_pos[None, :] <= q_pos[:, None]
        p = jax.nn.softmax(jnp.where(mask, logits, -jnp.inf), axis=-1)
        return jnp.einsum('bhts,bhsd->bhtd', p.astype(v.dtype), v)

    out = lax.map(block, (to_blocks(q, Q_BLOCK), to_blocks(cum_f, Q_BLOCK), jnp.arange(s // Q_BLOCK)))
    o = merge_heads(from_blocks(out)) * jax.nn.sigmoid(o_pre)
    return o @ w_out

def gla_mixer(u, w_in, w_gate_up, b_gate, norm_g, w_out):
    nk = GLA_HEADS * GLA_DK
    nv = GLA_HEADS * GLA_DV
    q, k, v, r, g_low = jnp.split(u @ w_in, [nk, 2 * nk, 2 * nk + nv, 2 * nk + 2 * nv], axis=-1)
    q = split_heads(q, GLA_HEADS) * (GLA_DK ** -0.5)
    k = split_heads(k, GLA_HEADS)
    v = split_heads(v, GLA_HEADS)
    log_a = jax.nn.log_sigmoid((g_low @ w_gate_up + b_gate).astype(jnp.float32)) / GLA_TAU
    log_a = split_heads(log_a, GLA_HEADS)
    causal = jnp.tril(jnp.ones((CHUNK, CHUNK), dtype=bool))
    b = u.shape[0]

    def step(state, inp):
        qc, kc, vc, la = inp
        cum_a = jnp.cumsum(la, axis=2)
        tot_a = cum_a[:, :, -1]
        inter = jnp.einsum('bhtd,bhde->bhte', qc * jnp.exp(cum_a), state)
        rel = jnp.where(causal[:, :, None], cum_a[:, :, :, None, :] - cum_a[:, :, None, :, :], -jnp.inf)
        scores = jnp.einsum('bhtd,bhsd,bhtsd->bhts', qc, kc, jnp.exp(rel))
        h = inter + jnp.einsum('bhts,bhse->bhte', scores, vc)
        state = (jnp.exp(tot_a)[..., None] * state
                 + jnp.einsum('bhsd,bhse->bhde', kc * jnp.exp(tot_a[:, :, None] - cum_a), vc))
        return state, h

    init = jnp.zeros((b, GLA_HEADS, GLA_DK, GLA_DV), jnp.float32)
    _, h = lax.scan(step, init, (to_blocks(q, CHUNK), to_blocks(k, CHUNK), to_blocks(v, CHUNK),
                                 to_blocks(log_a, CHUNK)))
    h = merge_heads(_rms(from_blocks(h))).astype(u.dtype) * norm_g
    return (h * jax.nn.silu(r)) @ w_out

def swiglu(u, w_gate, w_up, w_down):
    return (jax.nn.silu(u @ w_gate) * (u @ w_up)) @ w_down

def setup_inputs(seed: int = 0) -> dict:
    key = jax.random.key(seed)
    keys = jax.random.split(key, 26)
    f32 = jnp.float32

    def nrm(i, shape, scale):
        return jax.random.normal(keys[i], shape, f32) * scale

    n_ml = len(range(0, DEPTH, N_MIXERS))
    n_sb = len(range(1, DEPTH, N_MIXERS))
    n_fx = len(range(2, DEPTH, N_MIXERS))
    n_gla = len(range(3, DEPTH, N_MIXERS))
    d = D_MODEL
    ml_b_if = jnp.concatenate([
        jnp.broadcast_to(nrm(10, (n_ml, ML_HEADS), 0.1), (n_ml, ML_HEADS)),
        jnp.linspace(3.0, 6.0, ML_HEADS, dtype=f32)[None, :] + nrm(11, (n_ml, ML_HEADS), 0.1)], axis=-1)
    return {
        'x': nrm(0, (BATCH, SEQ, d), 1.0),
        'mix_norm_g': 1.0 + nrm(1, (DEPTH, d), 0.05),
        'ffn_norm_g': 1.0 + nrm(2, (DEPTH, d), 0.05),
        'ffn_w_gate': nrm(3, (DEPTH, d, D_FF), d ** -0.5),
        'ffn_w_up': nrm(4, (DEPTH, d, D_FF), d ** -0.5),
        'ffn_w_down': nrm(5, (DEPTH, D_FF, d), D_FF ** -0.5),
        'ml_w_in': nrm(6, (n_ml, d, ML_IN), d ** -0.5),
        'ml_b_if': ml_b_if,
        'ml_norm_g': 1.0 + nrm(7, (n_ml, ML_HEADS * ML_DV), 0.05),
        'ml_w_out': nrm(8, (n_ml, ML_HEADS * ML_DV, d), (ML_HEADS * ML_DV) ** -0.5),
        'sb_w_in': nrm(9, (n_sb, d, SB_IN), d ** -0.5),
        'sb_w_out': nrm(12, (n_sb, SB_HEADS * SB_DH, d), (SB_HEADS * SB_DH) ** -0.5),
        'fx_w_in': nrm(13, (n_fx, d, FX_IN), d ** -0.5),
        'fx_b_f': jnp.linspace(2.0, 5.0, FX_HEADS, dtype=f32)[None, :] + nrm(14, (n_fx, FX_HEADS), 0.1),
        'fx_q_norm_g': 1.0 + nrm(15, (n_fx, FX_DH), 0.05),
        'fx_k_norm_g': 1.0 + nrm(16, (n_fx, FX_DH), 0.05),
        'fx_w_out': nrm(17, (n_fx, FX_HEADS * FX_DH, d), (FX_HEADS * FX_DH) ** -0.5),
        'gla_w_in': nrm(18, (n_gla, d, GLA_IN), d ** -0.5),
        'gla_w_gate_up': nrm(19, (n_gla, GLA_RANK, GLA_HEADS * GLA_DK), GLA_RANK ** -0.5),
        'gla_b_gate': nrm(20, (n_gla, GLA_HEADS * GLA_DK), 0.1),
        'gla_norm_g': 1.0 + nrm(21, (n_gla, GLA_HEADS * GLA_DV), 0.05),
        'gla_w_out': nrm(22, (n_gla, GLA_HEADS * GLA_DV, d), (GLA_HEADS * GLA_DV) ** -0.5),
    }

def reference(x, mix_norm_g, ffn_norm_g, ffn_w_gate, ffn_w_up, ffn_w_down,
              ml_w_in, ml_b_if, ml_norm_g, ml_w_out,
              sb_w_in, sb_w_out,
              fx_w_in, fx_b_f, fx_q_norm_g, fx_k_norm_g, fx_w_out,
              gla_w_in, gla_w_gate_up, gla_b_gate, gla_norm_g, gla_w_out):
    h = x
    for layer in range(DEPTH):
        kind = layer % N_MIXERS
        j = layer // N_MIXERS
        u = rmsnorm(h, mix_norm_g[layer])
        if kind == 0:
            y = mlstm_mixer(u, ml_w_in[j], ml_b_if[j], ml_norm_g[j], ml_w_out[j])
        elif kind == 1:
            y = stick_breaking_mixer(u, sb_w_in[j], sb_w_out[j])
        elif kind == 2:
            y = forgetting_attn_mixer(u, fx_w_in[j], fx_b_f[j], fx_q_norm_g[j], fx_k_norm_g[j], fx_w_out[j])
        else:
            y = gla_mixer(u, gla_w_in[j], gla_w_gate_up[j], gla_b_gate[j], gla_norm_g[j], gla_w_out[j])
        h = h + y.astype(h.dtype)
        u = rmsnorm(h, ffn_norm_g[layer])
        h = h + swiglu(u, ffn_w_gate[layer], ffn_w_up[layer], ffn_w_down[layer]).astype(h.dtype)
    return h


_drawn_inputs = setup_inputs


def setup_inputs(seed=0):
    import zlib

    import numpy as np

    out = dict(_drawn_inputs(seed))
    spreads = {}
    factors = {}
    for name, (base, spread) in spreads.items():
        noise = np.random.default_rng([zlib.crc32(name.encode()), seed]).standard_normal(out[name].shape)
        drawn = base * np.exp(spread * noise) if base else spread * noise
        out[name] = jnp.asarray(drawn.astype(out[name].dtype))
    for name, factor in factors.items():
        out[name] = (out[name] * factor).astype(out[name].dtype)
    return out
```

```python
from contextlib import ExitStack

import concourse.bass as bass
from concourse import mybir

F32 = mybir.dt.float32
F32R = mybir.dt.float32r
BF16 = mybir.dt.bfloat16
ALU = mybir.AluOpType
ACT = mybir.ActivationFunctionType
AX_X = mybir.AxisListType.X

P = 128
D = 1024
SEQ = 2048
HEADS = 8
DV = D // HEADS
DQK = D // (2 * HEADS)
FF = 2816
EPS = 1e-6
KD = D // P
HALVES = 2
TOK = SEQ // HALVES
TILES = TOK // P
NB = 512
TBS = TOK // NB
VW = DV + 1
QK_BLOCKS = 8
V_END = 16
BLOCKS = 24
PIECES = 4
GROUPS = FF // (2 * P)
MASKED = -1e30

XT = 2 * TILES
PJ = 2 * BLOCKS
SP_ = BLOCKS + PIECES + 4 * GROUPS
GU = 4 * GROUPS
DN = 16 * GROUPS
RAW = BLOCKS // 4 + PIECES // 2 + GROUPS
OUT0 = BLOCKS
FF0 = BLOCKS + PIECES


def mlstm_layer(nc, x, mix_norm_g, ffn_norm_g, w_gate, w_up, w_down, w_in, b_if, norm_g, w_out, out):
    x_rows = x[0].rearrange("(t p) d -> t p d", p=P)
    out_rows = out[0].rearrange("(t p) d -> t p d", p=P)
    w_in_k = w_in[0].rearrange("(k p) n -> p k n", p=P)
    w_out_k = w_out[0].rearrange("(k p) n -> p k n", p=P)
    w_gate_k = w_gate[0].rearrange("(k p) n -> p k n", p=P)
    w_up_k = w_up[0].rearrange("(k p) n -> p k n", p=P)
    w_down_k = w_down[0].rearrange("(k p) n -> k p n", p=P)

    with ExitStack() as ctx:
        def sem(name):
            return ctx.enter_context(nc.semaphore(name))

        base = -(-nc.sbuf_base // 32) * 32
        top = [base]

        def region(nbytes):
            at = top[0]
            top[0] += -(-nbytes // 32) * 32
            return at

        def place(name, at, shape, dt):
            return nc.alloc_sbuf_tensor_at(name, shape, dt, offset=at)

        def small(name, shape, dt=F32):
            n = 1
            for s in shape[1:]:
                n *= s
            return place(name, region(n * (2 if dt == BF16 else 4)), shape, dt)

        KB = 1024
        r_u = region(64 * KB)
        u_hi = place("u_hi", r_u, [P, KD, TOK], F32R)
        u_lo = place("u_lo", r_u + 32 * KB, [P, KD, TOK], F32R)

        r_v = region(TILES * HEADS * VW * 4)
        v1 = place("v1", r_v, [P, TILES, HEADS, VW], F32)
        res = place("res", r_v, [P, TILES, D], F32)

        r_q = region(32 * KB)
        qk = place("qk", r_q, [P, QK_BLOCKS, TOK], F32)
        hg = place("hg", r_q, [P, KD, TOK], F32)
        wo1 = [place("wo1_hi", r_q, [P, KD, NB], F32R), place("wo1_lo", r_q + 16 * KB, [P, KD, NB], F32R)]
        dn_hi = place("dn_hi", r_q, [P, 2, D], F32R)
        dn_lo = place("dn_lo", r_q + 8 * KB, [P, 2, D], F32R)
        dn_raw = place("dn_raw", r_q + 16 * KB, [P, 2, D], F32)
        sg = place("sg", r_q + 24 * KB, [P, 2, NB], F32)
        x_in = [place("x_in0", r_q + 28 * KB, [P, D], F32), place("x_in1", r_q + 24 * KB, [P, D], F32)]

        r_a = region(16 * KB)
        wp_hi = [place(f"wp_hi{s}", r_a + 8 * KB * s, [P, KD, P], F32R) for s in range(2)]
        wp_lo = [place(f"wp_lo{s}", r_a + 8 * KB * s + 4 * KB, [P, KD, P], F32R) for s in range(2)]
        gain2 = place("gain2", r_a, [P, D], F32)
        xn2 = [place(f"xn2_{s}", r_a + 4 * KB * (s + 1), [P, D], F32) for s in range(2)]
        g_hi = [[place(f"g_hi{f}{t}", r_a + 2 * KB * (2 * f + t), [P, NB], F32R) for t in range(2)] for f in range(2)]
        g_lo = [[place(f"g_lo{f}{t}", r_a + 2 * KB * (4 + 2 * f + t), [P, NB], F32R) for t in range(2)] for f in range(2)]

        r_b = region(16 * KB)
        raw = [place(f"raw{s}", r_b + 8 * KB * s, [P, KD, 2 * P], F32) for s in range(2)]
        raw_wo = [place(f"raw_wo{s}", r_b + 8 * KB * s, [P, KD // 2, NB], F32) for s in range(2)]

        r_c = region(28 * KB + HEADS * VW * 4)
        cols = place("cols", r_c, [P, TOK], F32)
        negm = place("negm", r_c + 4 * KB, [P, TOK], F32R)
        wint = place("wint", r_c + 8 * KB, [P, TOK], F32R)
        t0 = place("t0", r_c + 12 * KB, [HEADS, TOK], F32)
        t1 = place("t1", r_c + 16 * KB, [HEADS, TOK], F32)
        t2 = place("t2", r_c + 20 * KB, [HEADS, TOK], F32)
        t3 = place("t3", r_c + 24 * KB, [HEADS, TOK], F32)
        t4 = place("t4", r_c + 28 * KB, [HEADS, TOK], F32)
        if_hi = place("if_hi", r_c + 12 * KB, [P, KD, P], F32R)
        if_lo = place("if_lo", r_c + 16 * KB, [P, KD, P], F32R)
        xn1 = [place(f"xn1_{s}", r_c + (20 + 4 * s) * KB, [P, D], F32) for s in range(2)]
        gain1 = place("gain1", r_c + 28 * KB, [P, D], F32)
        v_st = place("v_st", r_c + 12 * KB, [P, TBS, NB], F32)
        dmat = place("dmat", r_c + 12 * KB, [P, HEADS, P], F32)
        hrow = place("hrow", r_c + 16 * KB, [P, HEADS, DV], F32)
        qkc = place("qkc", r_c + 20 * KB, [P, QK_BLOCKS, P], F32)
        kw = place("kw", r_c + 24 * KB, [P, HEADS, DQK], F32)
        qw = place("qw", r_c + 26 * KB, [P, 4, P], F32)
        num = place("num", r_c + 28 * KB, [P, HEADS, VW], F32)
        wo0 = [place("wo0_hi", r_c, [P, KD, NB], F32R), place("wo0_lo", r_c + 16 * KB, [P, KD, NB], F32R)]
        gu_hi = [place(f"gu_hi{f}", r_c + 16 * KB * f, [P, 2, KD, P], F32R) for f in range(2)]
        gu_lo = [place(f"gu_lo{f}", r_c + 16 * KB * f + 8 * KB, [P, 2, KD, P], F32R) for f in range(2)]
        wo = [wo0, wo1]

        state = small("state", [P, 4, 2 * VW])
        colt = small("colt", [P, TILES, 72])
        ident = small("ident", [P, P])
        ident_b = small("ident_b", [P, P], BF16)
        pick = small("pick", [P, HEADS, P], F32R)
        mask = small("mask", [P, 4, P], BF16)
        not_first = small("not_first", [HEADS, TOK], BF16)
        if_raw = small("if_raw", [P, KD, 2 * HEADS])
        bias_i = small("bias_i", [HEADS, 1])
        bias_f = small("bias_f", [64, 1])
        head_g = small("head_g", [P, HEADS])
        m_end = small("m_end", [HEADS, 1])
        m_prev = small("m_prev", [HEADS, TILES])
        nm_end = small("nm_end", [HEADS, TILES])
        dec = small("dec", [P, 4])
        nv = small("nv", [P, 2, 8])
        hv = small("hv", [P, 10, HEADS])
        assert top[0] <= nc.sbuf_usable_end, (top[0], nc.sbuf_usable_end)
        pick_src = place("pick_src", r_q, [P, HEADS, P], F32)

        ps = ctx.enter_context(nc.psum_tensor("ps", [P, 8, NB], F32))

        def banks(b, n=1):
            return ps[:, b:b + n, :].rearrange("p b n -> p (b n)")

        x_loaded = [sem(f"x_loaded{s}") for s in range(2)]
        gain_loaded = sem("gain_loaded")
        if_loaded = sem("if_loaded")
        raw_loaded = [sem(f"raw_loaded{s}") for s in range(2)]
        dn_loaded = [sem(f"dn_loaded{s}") for s in range(2)]
        res_loaded = [sem(f"res_loaded{s}") for s in range(4)]
        bias_loaded = sem("bias_loaded")
        out_stored = sem("out_stored")
        const_pool = sem("const_pool")
        const_dve = sem("const_dve")
        prep_done = sem("prep_done")
        pool_passed = sem("pool_passed")
        dve_passed = sem("dve_passed")
        pe_passed = sem("pe_passed")
        ssq_done = sem("ssq_done")
        var_done = sem("var_done")
        lnv_done = sem("lnv_done")
        rstd0_done = sem("rstd0_done")
        rstd_step = sem("rstd_step")
        xn_done = sem("xn_done")
        xt_done = sem("xt_done")
        uhi_done = sem("uhi_done")
        ulo_done = sem("ulo_done")
        split_hi = sem("split_hi")
        split_lo = sem("split_lo")
        if_hi_done = sem("if_hi_done")
        if_lo_done = sem("if_lo_done")
        dn_hi_done = sem("dn_hi_done")
        dn_lo_done = sem("dn_lo_done")
        if_done = sem("if_done")
        proj_done = sem("proj_done")
        qk_kept = sem("qk_kept")
        v_staged = sem("v_staged")
        vt_done = sem("vt_done")
        v_kept = sem("v_kept")
        gate_dve = sem("gate_dve")
        gate_act = sem("gate_act")
        colt_turned = sem("colt_turned")
        colt_kept = sem("colt_kept")
        qkc_ready = sem("qkc_ready")
        wint_spread = sem("wint_spread")
        darg_done = sem("darg_done")
        k_turned = sem("k_turned")
        dmat_done = sem("dmat_done")
        dec_done = sem("dec_done")
        qw_done = sem("qw_done")
        kw_done = sem("kw_done")
        s_done = sem("s_done")
        sd_done = sem("sd_done")
        upd_done = sem("upd_done")
        n_done = sem("n_done")
        num_kept = sem("num_kept")
        state_done = sem("state_done")
        sq_done = sem("sq_done")
        post_step = sem("post_step")
        hln_done = sem("hln_done")
        hrs_done = sem("hrs_done")
        h_done = sem("h_done")
        h_turned = sem("h_turned")
        ht_kept = sem("ht_kept")
        oexp_done = sem("oexp_done")
        o1_done = sem("o1_done")
        hg_done = sem("hg_done")
        hghi_done = sem("hghi_done")
        hglo_done = sem("hglo_done")
        outp_done = sem("outp_done")
        res_added = sem("res_added")
        gu_done = sem("gu_done")
        silu_done = sem("silu_done")
        gf_done = sem("gf_done")
        ghi_done = sem("ghi_done")
        glo_done = sem("glo_done")
        dn_done = sem("dn_done")
        dn_added = sem("dn_added")

        def past(count):
            return count + 1

        def start_at_one(engine, *counters):
            for counter in counters:
                engine.sem_inc(counter, 1)

        block = ctx.enter_context(nc.Block())

        def head_values(c):
            return v1[:, c, :, 0:DV]

        @block.sync
        def _(sp):
            sp.dma_start(bias_i[:, :], b_if[0, 0:HEADS].rearrange("(p a) -> p a", a=1)).then_inc(bias_loaded, 16)
            sp.dma_start(bias_f[32:32 + HEADS, :], b_if[0, HEADS:2 * HEADS].rearrange("(p a) -> p a", a=1))\
                .then_inc(bias_loaded, 16)
            sp.dma_start(head_g[:, :], norm_g[0].rearrange("(h p) -> p h", p=P),
                         allow_slow_non_contiguous=True).then_inc(bias_loaded, 16)

            def load_pair(h, p, s):
                sp.dma_start(raw[s][:, :, :], w_in_k[:, :, bass.ds(p * 2 * P, 2 * P)]).then_inc(raw_loaded[s], 16)

            def load_down(n, f):
                sp.dma_start(dn_raw[:, f, :], w_down_k[2 * n + f]).then_inc(dn_loaded[f], 16)

            def load_gate_up(n, s):
                w = w_gate_k if s == 0 else w_up_k
                sp.dma_start(raw[s][:, :, :], w[:, :, bass.ds(n * 2 * P, 2 * P)]).then_inc(raw_loaded[s], 16)

            with sp.Fori(0, HALVES) as h:
                sp.wait_ge(outp_done, past(h * 16))
                sp.dma_start(x_in[0][:, :], x_rows[h * TILES]).then_inc(x_loaded[0], 16)
                sp.wait_ge(glo_done, past(h * GU))
                sp.dma_start(x_in[1][:, :], x_rows[h * TILES + 1]).then_inc(x_loaded[1], 16)
                sp.wait_ge(gu_done, past(h * GU))
                sp.dma_start(gain1[:, :], mix_norm_g[0:1, :].partition_broadcast(P)).then_inc(gain_loaded, 16)
                sp.wait_ge(if_lo_done, past(h))
                sp.wait_ge(split_lo, past(h * SP_))
                sp.dma_start(if_raw[:, :, :], w_in_k[:, :, BLOCKS * P:BLOCKS * P + 2 * HEADS]).then_inc(if_loaded, 16)
                with sp.Fori(1, TILES // 2) as j:
                    for s in range(2):
                        sp.wait_ge(xn_done, h * XT + 2 * j + s - 1)
                        sp.dma_start(x_in[s][:, :], x_rows[h * TILES + 2 * j + s]).then_inc(x_loaded[s], 16)
                load_pair(h, 0, 0)
                load_pair(h, 1, 1)
                with sp.Fori(1, BLOCKS // 4) as j:
                    for s in range(2):
                        sp.wait_ge(split_lo, past(h * SP_ + 4 * j + 2 * s - 2))
                        load_pair(h, 2 * j + s, s)
                for q in range(PIECES):
                    sp.wait_ge(split_lo, past(h * SP_ + (OUT0 - 2 + 2 * q if q < 2 else OUT0 + q - 1)))
                    sp.dma_start(raw_wo[q % 2][:, :, :],
                                 w_out_k[:, 4 * (q % 2):4 * (q % 2) + 4, NB * (q // 2):NB * (q // 2) + NB])\
                        .then_inc(raw_loaded[q % 2], 16)
                sp.wait_ge(proj_done, past(h * PJ + PJ))
                sp.dma_start(gain2[:, :], ffn_norm_g[0:1, :].partition_broadcast(P)).then_inc(gain_loaded, 16)
                for s in range(2):
                    sp.wait_ge(split_lo, past(h * SP_ + FF0 - 1 + s))
                    load_gate_up(0, s)
                sp.wait_ge(outp_done, past(h * 16 + 16))
                load_down(0, 0)
                load_down(0, 1)
                with sp.Fori(1, GROUPS) as n:
                    for s in range(2):
                        sp.wait_ge(split_lo, past(h * SP_ + n * 4 + (FF0 - 1 + s)))
                        load_gate_up(n, s)
                    for f in range(2):
                        sp.wait_ge(dn_lo_done, h * (2 * GROUPS) + n * 2 + (f - 1))
                        load_down(n, f)

        @block.gpsimd
        def _(pool):
            nc.gpsimd.memset(ident[:, :], 0.0).then_inc(const_pool, 1)
            nc.gpsimd.memset(mask[:, :, :], 0.0).then_inc(const_pool, 1)
            nc.gpsimd.memset(pick_src[:, :, :], 0.0).then_inc(const_pool, 1)
            pool.wait_ge(const_pool, 3)
            nc.gpsimd.affine_select(out=ident[:, :], in_=ident[:, :], compare_op=ALU.not_equal, fill=1.0, base=0,
                                    pattern=[[-1, P]], channel_multiplier=1).then_inc(const_pool, 1)
            nc.gpsimd.affine_select(out=mask[:, :, :], in_=mask[:, :, :], compare_op=ALU.is_ge, fill=MASKED, base=0,
                                    pattern=[[0, 4], [1, P]], channel_multiplier=-1).then_inc(const_pool, 1)
            nc.gpsimd.affine_select(out=pick_src[:, :, :], in_=pick_src[:, :, :], compare_op=ALU.not_equal, fill=1.0,
                                    base=0, pattern=[[-1, HEADS], [0, P]], channel_multiplier=1)\
                .then_inc(const_pool, 1)
            pool.wait_ge(const_pool, 6)
            nc.gpsimd.affine_select(out=pick_src[:, :, :], in_=pick_src[:, :, :], compare_op=ALU.not_equal, fill=1.0,
                                    base=-32, pattern=[[-1, HEADS], [0, P]], channel_multiplier=1)\
                .then_inc(const_pool, 1)
            nc.gpsimd.memset(state[:, :, :], 0.0).then_inc(const_pool, 1)
            nc.gpsimd.memset(m_end[:, :], 0.0).then_inc(const_pool, 1)
            nc.gpsimd.memset(not_first[:, :], 1.0).then_inc(const_pool, 1)
            pool.wait_ge(const_pool, 10)
            nc.gpsimd.memset(not_first[:, :].rearrange("p (c t) -> p c t", t=P)[:, :, 0:1], 0.0)\
                .then_inc(const_pool, 1)

            def clear_rows():
                for tile in (if_hi, if_lo):
                    nc.gpsimd.memset(tile[:, :, :].bitcast(F32), 0.0).then_inc(prep_done, 1)
                nc.gpsimd.memset(cols[:, :], 0.0).then_inc(prep_done, 1)
                for tile in (negm, wint):
                    nc.gpsimd.memset(tile[:, :].bitcast(F32), 0.0).then_inc(prep_done, 1)

            def set_ones():
                nc.gpsimd.memset(v1[:, :, :, DV:VW], 1.0).then_inc(prep_done, 1)

            clear_rows()
            set_ones()
            with pool.Fori(0, HALVES) as h:
                def copy_qk(c):
                    nc.gpsimd.tensor_copy(qkc[:, :, :], qk[:, :, bass.ds(c * P, P)]).then_inc(qkc_ready, 1)

                def squares(c):
                    pool.wait_ge(num_kept, h * 32 + c * 4 + 4)
                    pool.wait_ge(h_turned, past(h * 8 + c))
                    nc.gpsimd.tensor_tensor(hrow[:, :, :], num[:, :, 0:DV], num[:, :, 0:DV], ALU.mult)\
                        .then_inc(sq_done, 1)

                pool.wait_ge(qk_kept, past(h * 16 + 16))
                pool.wait_ge(gate_dve, h * 13 + 13)
                pool.wait_ge(gate_act, h * 7 + 7)
                pool.sem_inc(pool_passed, 1)
                copy_qk(0)
                with pool.Fori(1, TILES) as c:
                    pool.wait_ge(s_done, h * 16 + c * 2)
                    pool.wait_ge(qw_done, h * 8 + c)
                    pool.sem_inc(pool_passed, 1)
                    copy_qk(c)
                    squares(c - 1)
                squares(TILES - 1)
                pool.wait_ge(hg_done, past(h * 16 + 16))
                pool.sem_inc(pool_passed, 1)
                for q in range(4):
                    pool.dma_start(res[:, 2 * q:2 * q + 2, :],
                                   x_rows[bass.ds(h * TILES + 2 * q, 2)].rearrange("t p d -> p t d"))\
                        .then_inc(res_loaded[q], 16)
                for i in range(TILES):
                    pool.wait_ge(dn_added, past(h * DN + (DN - 16 + 2 * i + 2)))
                    pool.sem_inc(pool_passed, 1)
                    pool.dma_start(out_rows[h * TILES + i], res[:, i, :]).then_inc(out_stored, 16)
                pool.wait_ge(gu_done, past(h * GU + GU))
                pool.sem_inc(pool_passed, 1)
                clear_rows()
                pool.wait_ge(out_stored, h * (16 * TILES) + 16 * TILES)
                pool.sem_inc(pool_passed, 1)
                set_ones()
            pool.wait_ge(out_stored, HALVES * 16 * TILES)

        @block.scalar
        def _(act):
            def norm_sum(i, src, junk):
                s = nv[:, i[1], :]
                nc.scalar.activation(junk, src, ACT.Square, accum_out=s[:, 0:1]).then_inc(ssq_done, 1)
                act.wait_ge(var_done, i[0] + 1)
                nc.scalar.activation(s[:, 2:3], s[:, 1:2], ACT.Ln).then_inc(lnv_done, 1)
                act.wait_ge(lnv_done, i[0] + 1)
                nc.scalar.activation(s[:, 3:4], s[:, 2:3], ACT.Exp, scale=-0.5).then_inc(rstd0_done, 1)

            def norm_hi(i, cols_, bank):
                act.wait_ge(xt_done, past(i + 1))
                nc.scalar.copy(u_hi[:, :, cols_], banks(bank, 2).rearrange("p (k t) -> p k t", k=KD))\
                    .then_inc(uhi_done, 1)

            def split_block(h, b):
                act.wait_ge(proj_done, past(h * PJ + max(0, 2 * (b - 1))))
                act.wait_ge(raw_loaded[(b // 2) % 2], h * (16 * RAW) + 16 * (b // 4 + 1))
                nc.scalar.copy(wp_hi[b % 2][:, :, :], raw[(b // 2) % 2][:, :, (b % 2) * P:(b % 2) * P + P])\
                    .then_inc(split_hi, 1)

            def split_piece(h, q):
                act.wait_ge(raw_loaded[q % 2], h * (16 * RAW) + 16 * (BLOCKS // 4 + q // 2 + 1))
                nc.scalar.copy(wo[q // 2][0][:, 4 * (q % 2):4 * (q % 2) + 4, :], raw_wo[q % 2][:, :, :])\
                    .then_inc(split_hi, 1)

            def split_gate_up(h, n, f):
                for s in range(2):
                    act.wait_ge(raw_loaded[s], h * (16 * RAW) + n * 16 + 16 * (BLOCKS // 4 + PIECES // 2 + 1))
                    nc.scalar.copy(gu_hi[f][:, s, :, :], raw[s][:, :, f * P:f * P + P]).then_inc(split_hi, 1)

            start_at_one(act, qk_kept, v_staged, ht_kept)
            act.wait_ge(const_pool, 11)
            act.wait_ge(bias_loaded, 48)

            with act.Fori(0, HALVES) as h:
                act.wait_ge(gu_done, past(h * GU))
                with act.Fori(0, TILES // 2) as j:
                    for s in range(2):
                        act.wait_ge(x_loaded[s], h * (8 * TILES) + j * 16 + 16)
                        act.wait_ge(xt_done, past(h * XT + j * 2))
                        norm_sum((h * XT + j * 2 + s, s), x_in[s][:, :], xn1[s][:, :])
                    for s in range(2):
                        norm_hi(h * XT + j * 2 + s, bass.ds(j * (2 * P) + s * P, P), 2 * s)

                act.wait_ge(if_loaded, h * 16 + 16)
                act.wait_ge(prep_done, h * 6 + 2)
                nc.scalar.copy(if_hi[:, :, :].rearrange("p k (a c) -> p k a c", c=32)[:, :, 0:2, 0:HEADS],
                               if_raw[:, :, :].rearrange("p k (a c) -> p k a c", a=2)).then_inc(if_hi_done, 1)
                act.wait_ge(dn_done, past(h * DN))
                split_block(h, 0)

                def gate_part(b):
                    if b == 1:
                        act.wait_ge(gate_dve, h * 13 + 3)
                        nc.scalar.activation(t2[:, :], t2[:, :], ACT.Exp).then_inc(gate_act, 1)
                        act.wait_ge(gate_act, h * 7 + 1)
                        nc.scalar.activation(t2[:, :], t2[:, :], ACT.Ln, bias=1.0).then_inc(gate_act, 1)
                    if b == 3:
                        act.wait_ge(gate_dve, h * 13 + 8)
                        nc.scalar.activation(cols[64:64 + HEADS, :], t3[:, :], ACT.Exp, scale=-1.0)\
                            .then_inc(gate_act, 1)
                        nc.scalar.copy(negm[0:HEADS, :], t4[:, :]).then_inc(gate_act, 1)
                        act.wait_ge(gate_dve, h * 13 + 11)
                        nc.scalar.activation(t2[:, :], t2[:, :], ACT.Exp).then_inc(gate_act, 1)
                        nc.scalar.activation(cols[32:32 + HEADS, :], t0[:, :], ACT.Exp).then_inc(gate_act, 1)
                        act.wait_ge(gate_act, h * 7 + 5)
                        nc.scalar.copy(wint[0:HEADS, :], t2[:, :]).then_inc(gate_act, 1)

                for b in range(QK_BLOCKS):
                    split_block(h, b + 1)
                    gate_part(b)
                    for t in range(TBS):
                        act.wait_ge(proj_done, past(h * PJ + 2 * b + t + 1))
                        nc.scalar.mul(qk[:, b, t * NB:t * NB + NB], banks(2 * (b % 2) + t),
                                      1.0 if b < 4 else float(DQK) ** -0.5).then_inc(qk_kept, 1)

                act.wait_ge(colt_turned, h + 1)
                act.wait_ge(gate_dve, h * 13 + 13)
                for b in range(QK_BLOCKS, V_END):
                    split_block(h, b + 1)
                    for t in range(TBS):
                        act.wait_ge(proj_done, past(h * PJ + 2 * b + t + 1))
                        act.wait_ge(vt_done, past(h * 16 + max(0, 2 * (b - QK_BLOCKS - 1) + t + 1)))
                        nc.scalar.copy(v_st[:, t, :], banks(2 * (b % 2) + t)).then_inc(v_staged, 1)

                def decay_matrix(c):
                    act.wait_ge(darg_done, h * 8 + c + 1)
                    for i in range(HEADS):
                        nc.scalar.activation(dmat[:, i, :], ps[:, 1 + i // 4, (i % 4) * P:(i % 4) * P + P], ACT.Exp,
                                             bias=colt[:, c, i:i + 1]).then_inc(dmat_done, 1)

                def head_rstd(c):
                    act.wait_ge(post_step, h * 88 + c * 11 + 7)
                    nc.scalar.activation(hv[:, 6, :], hv[:, 5, :], ACT.Ln).then_inc(hln_done, 1)
                    act.wait_ge(hln_done, h * 8 + c + 1)
                    nc.scalar.activation(hv[:, 7, :], hv[:, 6, :], ACT.Exp, scale=-0.5).then_inc(hrs_done, 1)

                def keep_num(c):
                    act.wait_ge(h_done, past(h * 8 + c))
                    for g in range(4):
                        act.wait_ge(n_done, h * 32 + c * 4 + g + 1)
                        nc.scalar.copy(num[:, 2 * g:2 * g + 2, :],
                                       ps[:, 4 + g % 2, 0:2 * VW].rearrange("p (a n) -> p a n", a=2))\
                            .then_inc(num_kept, 1)

                def keep_turned(c):
                    act.wait_ge(h_turned, past(h * 8 + c + 1))
                    nc.scalar.copy(head_values(c), banks(1, 2).rearrange("p (k t) -> p k t", k=HEADS))\
                        .then_inc(ht_kept, 1)

                act.wait_ge(vt_done, past(h * 16 + 16))
                act.wait_ge(colt_kept, h + 1)
                decay_matrix(0)
                keep_num(0)
                with act.Fori(1, TILES) as c:
                    decay_matrix(c)
                    head_rstd(c - 1)
                    keep_num(c)
                    keep_turned(c - 1)
                head_rstd(TILES - 1)
                keep_turned(TILES - 1)

                for b in range(V_END, BLOCKS):
                    if b + 1 < BLOCKS:
                        split_block(h, b + 1)
                    if b >= BLOCKS - 2:
                        split_piece(h, b - (BLOCKS - 2))
                    for t in range(TBS):
                        act.wait_ge(proj_done, past(h * PJ + 2 * b + t + 1))
                        nc.scalar.activation(banks(2 * (b % 2) + t), banks(2 * (b % 2) + t), ACT.Exp, scale=-1.0)\
                            .then_inc(oexp_done, 1)

                act.wait_ge(hg_done, past(h * 16 + 16))
                for i in range(TILES):
                    nc.scalar.copy(u_hi[:, :, i * P:i * P + P], hg[:, :, i * P:i * P + P]).then_inc(hghi_done, 1)
                act.wait_ge(hglo_done, h * 8 + 8)
                split_piece(h, 2)
                split_piece(h, 3)
                act.wait_ge(outp_done, past(h * 16 + 8))
                split_gate_up(h, 0, 0)
                for i in range(TILES):
                    act.wait_ge(res_added, h * 16 + 8 + i + 1)
                    if i >= 2:
                        act.wait_ge(xt_done, past(h * XT + TILES + i - 1))
                    norm_sum((h * XT + TILES + i, i % 2), res[:, i, :], xn2[i % 2][:, :])
                    if i >= 2:
                        norm_hi(h * XT + TILES + i - 2, slice((i - 2) * P, (i - 1) * P), 4 + 2 * (i % 2))
                for i in range(TILES - 2, TILES):
                    norm_hi(h * XT + TILES + i, slice(i * P, i * P + P), 4 + 2 * (i % 2))

                def silu(n, o):
                    act.wait_ge(gu_done, past(h * GU + n * 4 + o + 1))
                    act.wait_ge(glo_done, past(h * GU + n * 4 + o - 1 if o >= 2 else h * GU + n * 4))
                    nc.scalar.activation(sg[:, o % 2, :], banks(2 * (o % 2)), ACT.Silu).then_inc(silu_done, 1)

                def hidden_hi(n, o):
                    act.wait_ge(gf_done, past(h * GU + n * 4 + o + 1))
                    act.wait_ge(dn_done, past(h * DN + n * 16 + (-8 if o < 2 else 0) if n is not first else h * DN))
                    nc.scalar.copy(g_hi[o % 2][o // 2][:, :], sg[:, o % 2, :]).then_inc(ghi_done, 1)

                def ffn_group(n, last):
                    act.wait_ge(gu_done, past(h * GU + n * 4))
                    split_gate_up(h, n, 1)
                    silu(n, 0)
                    if n is first:
                        act.wait_ge(xt_done, past(h * XT + XT))
                    hidden_hi(n, 0)
                    act.wait_ge(dn_done, past(h * DN + n * 16))
                    for f in range(2):
                        act.wait_ge(dn_loaded[f], h * (16 * GROUPS) + n * 16 + 16)
                        nc.scalar.copy(dn_hi[:, f, :], dn_raw[:, f, :]).then_inc(dn_hi_done, 1)
                    silu(n, 1)
                    hidden_hi(n, 1)
                    silu(n, 2)
                    hidden_hi(n, 2)
                    if not last:
                        act.wait_ge(gu_done, past(h * GU + n * 4 + 3))
                        split_gate_up(h, n + 1, 0)
                    silu(n, 3)
                    hidden_hi(n, 3)

                first = 0
                ffn_group(first, False)
                with act.Fori(1, GROUPS - 1) as n:
                    ffn_group(n, False)
                ffn_group(GROUPS - 1, True)

        @block.vector
        def _(dve):
            def norm_var(i):
                s = nv[:, i[1], :]
                dve.wait_ge(ssq_done, i[0] + 1)
                nc.vector.tensor_scalar(s[:, 1:2], s[:, 0:1], 1.0 / D, EPS, ALU.mult, ALU.add).then_inc(var_done, 1)
                dve.wait_ge(rstd0_done, i[0] + 1)
                nc.vector.tensor_tensor(s[:, 4:5], s[:, 3:4], s[:, 3:4], ALU.mult).then_inc(rstd_step, 1)
                dve.wait_ge(rstd_step, i[0] * 3 + 1)
                nc.vector.scalar_tensor_tensor(out=s[:, 5:6], in0=s[:, 4:5], scalar=-0.5, in1=s[:, 1:2],
                                               op0=ALU.mult, op1=ALU.mult).then_inc(rstd_step, 1)
                dve.wait_ge(rstd_step, i[0] * 3 + 2)
                nc.vector.scalar_tensor_tensor(out=s[:, 6:7], in0=s[:, 5:6], scalar=1.5, in1=s[:, 3:4],
                                               op0=ALU.add, op1=ALU.mult).then_inc(rstd_step, 1)
                dve.wait_ge(rstd_step, i[0] * 3 + 3)

            def norm_rows(i, src, gain, dst):
                norm_var(i)
                nc.vector.scalar_tensor_tensor(out=dst, in0=src, scalar=nv[:, i[1], 6:7], in1=gain,
                                               op0=ALU.mult, op1=ALU.mult).then_inc(xn_done, 1)

            def norm_lo(i, cols_, bank):
                dve.wait_ge(uhi_done, i + 1)
                nc.vector.tensor_tensor(u_lo[:, :, cols_], banks(bank, 2).rearrange("p (k t) -> p k t", k=KD),
                                        u_hi[:, :, cols_].bitcast(F32), ALU.subtract).then_inc(ulo_done, 1)

            def split_block(h, b):
                dve.wait_ge(split_hi, h * SP_ + b + 1)
                nc.vector.tensor_tensor(wp_lo[b % 2][:, :, :], raw[(b // 2) % 2][:, :, (b % 2) * P:(b % 2) * P + P],
                                        wp_hi[b % 2][:, :, :].bitcast(F32), ALU.subtract).then_inc(split_lo, 1)

            def split_piece(h, q):
                dve.wait_ge(split_hi, h * SP_ + OUT0 + q + 1)
                rows = slice(4 * (q % 2), 4 * (q % 2) + 4)
                nc.vector.tensor_tensor(wo[q // 2][1][:, rows, :], raw_wo[q % 2][:, :, :],
                                        wo[q // 2][0][:, rows, :].bitcast(F32), ALU.subtract).then_inc(split_lo, 1)

            def split_gate_up(h, n, f):
                for s in range(2):
                    dve.wait_ge(split_hi, h * SP_ + n * 4 + (FF0 + 2 * f + s + 1))
                    nc.vector.tensor_tensor(gu_lo[f][:, s, :, :], raw[s][:, :, f * P:f * P + P],
                                            gu_hi[f][:, s, :, :].bitcast(F32), ALU.subtract).then_inc(split_lo, 1)

            start_at_one(dve, glo_done, split_lo, if_lo_done, h_done, gf_done, ulo_done, dn_added, v_kept,
                         state_done, sd_done, hg_done)
            dve.wait_ge(const_pool, 11)
            dve.wait_ge(bias_loaded, 48)
            nc.vector.tensor_copy(pick[:, :, :], pick_src[:, :, :]).then_inc(const_dve, 1)
            nc.vector.tensor_copy(ident_b[:, :], ident[:, :]).then_inc(const_dve, 1)

            with dve.Fori(0, HALVES) as h:
                dve.wait_ge(gain_loaded, h * 32 + 16)
                dve.sem_inc(dve_passed, 1)
                with dve.Fori(0, TILES // 2) as j:
                    for s in range(2):
                        norm_rows((h * XT + j * 2 + s, s), x_in[s][:, :], gain1[:, :], xn1[s][:, :])
                    for s in range(2):
                        norm_lo(h * XT + j * 2 + s, bass.ds(j * (2 * P) + s * P, P), 2 * s)

                dve.wait_ge(if_hi_done, h + 1)
                nc.vector.tensor_tensor(if_lo[:, :, :].rearrange("p k (a c) -> p k a c", c=32)[:, :, 0:2, 0:HEADS],
                                        if_raw[:, :, :].rearrange("p k (a c) -> p k a c", a=2),
                                        if_hi[:, :, :].rearrange("p k (a c) -> p k a c", c=32)[:, :, 0:2, 0:HEADS]
                                        .bitcast(F32), ALU.subtract).then_inc(if_lo_done, 1)
                split_block(h, 0)

                def per_chunk(tile):
                    return tile[:, :].rearrange("p (c t) -> p c t", t=P)

                def gate_part(b):
                    g = h * 13
                    if b == 0:
                        dve.wait_ge(if_done, h * 2 + 2)
                        nc.vector.tensor_scalar(t0[:, :], ps[0:HEADS, 4:6, :].rearrange("p b n -> p (b n)"),
                                                bias_i[:, 0:1], None, ALU.add).then_inc(gate_dve, 1)
                        nc.vector.tensor_scalar(t1[:, :], ps[32:32 + HEADS, 4:6, :].rearrange("p b n -> p (b n)"),
                                                bias_f[32:32 + HEADS, 0:1], None, ALU.add).then_inc(gate_dve, 1)
                        dve.wait_ge(gate_dve, g + 2)
                        nc.vector.scalar_tensor_tensor(out=t2[:, :], in0=t1[:, :], scalar=-1.0, in1=t1[:, :],
                                                       op0=ALU.mult, op1=ALU.min).then_inc(gate_dve, 1)
                    if b == 2:
                        dve.wait_ge(gate_act, h * 7 + 2)
                        nc.vector.scalar_tensor_tensor(out=t1[:, :], in0=t1[:, :], scalar=0.0, in1=t2[:, :],
                                                       op0=ALU.min, op1=ALU.subtract).then_inc(gate_dve, 1)
                        dve.wait_ge(gate_dve, g + 4)
                        nc.vector.tensor_tensor_scan(t3[:, :], t1[:, :], t0[:, :], m_end[:, 0:1], ALU.add, ALU.max)\
                            .then_inc(gate_dve, 1)
                        nc.vector.tensor_tensor_scan(t4[:, :], not_first[:, :], t1[:, :], 0.0, ALU.mult, ALU.add)\
                            .then_inc(gate_dve, 1)
                        dve.wait_ge(gate_dve, g + 6)
                        dve.wait_ge(prep_done, h * 6 + 5)
                        nc.vector.tensor_tensor(cols[0:HEADS, :], t0[:, :], t4[:, :], ALU.subtract)\
                            .then_inc(gate_dve, 1)
                        dve.wait_ge(gate_dve, g + 7)
                        nc.vector.tensor_tensor(t4[:, :], t4[:, :], t3[:, :], ALU.subtract).then_inc(gate_dve, 1)
                        dve.wait_ge(gate_dve, g + 8)
                        nc.vector.tensor_copy(m_prev[:, 0:1], m_end[:, 0:1]).then_inc(gate_dve, 1)
                        nc.vector.tensor_copy(m_prev[:, 1:TILES], per_chunk(t3)[:, 0:TILES - 1, P - 1])
                        dve.drain()
                        nc.vector.tensor_copy(m_end[:, 0:1], t3[:, TOK - 1:TOK])
                        nc.vector.tensor_tensor(per_chunk(t2), per_chunk(t4),
                                                m_prev[:, :].unsqueeze(2).broadcast_to([HEADS, TILES, P]), ALU.add)\
                            .then_inc(gate_dve, 1)
                        nc.vector.tensor_copy(nm_end[:, :], per_chunk(t4)[:, :, P - 1])
                        dve.drain()
                        nc.vector.tensor_tensor(per_chunk(t0), cols[0:HEADS, :].rearrange("p (c t) -> p c t", t=P),
                                                nm_end[:, :].unsqueeze(2).broadcast_to([HEADS, TILES, P]), ALU.add)\
                            .then_inc(gate_dve, 1)
                    if b == 4:
                        dve.wait_ge(gate_act, h * 7 + 7)
                        nc.vector.tensor_tensor(negm[32:32 + HEADS, :], t4[:, :], negm[0:HEADS, :].bitcast(F32),
                                                ALU.subtract).then_inc(gate_dve, 1)
                        nc.vector.tensor_tensor(wint[32:32 + HEADS, :], t2[:, :], wint[0:HEADS, :].bitcast(F32),
                                                ALU.subtract).then_inc(gate_dve, 1)
                    if b == 6:
                        dve.wait_ge(colt_turned, h + 1)
                        nc.vector.tensor_copy(colt[:, :, :],
                                              ps[:, 6:8, :].rearrange("p b (c n) -> p (b c) n", n=P)[:, :, 0:72])\
                            .then_inc(colt_kept, 1)

                for b in range(QK_BLOCKS):
                    split_block(h, b + 1)
                    gate_part(b)

                dve.wait_ge(prep_done, h * 6 + 6)
                for b in range(QK_BLOCKS, V_END):
                    split_block(h, b + 1)
                    for t in range(TBS):
                        dve.wait_ge(vt_done, past(h * 16 + 2 * (b - QK_BLOCKS) + t + 1))
                        nc.vector.tensor_copy(v1[:, 4 * t:4 * t + 4, b - QK_BLOCKS, 0:DV],
                                              banks(4 + t).rearrange("p (c n) -> p c n", n=P)).then_inc(v_kept, 1)

                def weigh(c):
                    dve.wait_ge(wint_spread, h * 8 + c + 1)
                    nc.vector.tensor_copy(dec[:, :], banks(0).rearrange("p (g t) -> p g t", t=P)[:, :, P - 1])\
                        .then_inc(dec_done, 1)
                    dve.wait_ge(qkc_ready, h * 8 + c + 1)
                    nc.vector.tensor_tensor(qw[:, :, :], banks(0).rearrange("p (g t) -> p g t", t=P), qkc[:, 0:4, :],
                                            ALU.mult).then_inc(qw_done, 1)
                    dve.wait_ge(k_turned, h * 8 + c + 1)
                    nc.vector.tensor_tensor(kw[:, :, :], banks(3).rearrange("p (i n) -> p i n", n=DQK),
                                            colt[:, c, 32:32 + HEADS].unsqueeze(2).broadcast_to([P, HEADS, DQK]),
                                            ALU.mult).then_inc(kw_done, 1)

                def weigh_scores(c, q):
                    dve.wait_ge(s_done, h * 16 + c * 2 + q + 1)
                    dve.wait_ge(dmat_done, h * 64 + c * 8 + 4 * q + 4)
                    heads = dmat[:, 4 * q:4 * q + 4, :].rearrange("p (g a) t -> p g a t", a=2)
                    nc.vector.tensor_tensor(heads, ps[:, 6:8, 0:2 * P].rearrange("p a (g t) -> p g a t", g=2),
                                            heads, ALU.mult).then_inc(sd_done, 1)

                def update_state(c, g):
                    dve.wait_ge(n_done, h * 32 + c * 4 + g + 1)
                    dve.wait_ge(upd_done, h * 32 + c * 4 + g + 1)
                    for a in range(2):
                        r, w = slice(64 * a, 64 * a + 64), slice(VW * a, VW * a + VW)
                        nc.vector.scalar_tensor_tensor(out=state[r, g, w], in0=state[r, g, w],
                                                       scalar=dec[r, g:g + 1], in1=ps[r, 3 if g % 2 == 0 else 0, w],
                                                       op0=ALU.mult, op1=ALU.add).then_inc(state_done, 1)

                def head_scale_a(c):
                    p0 = h * 88 + c * 11
                    dve.wait_ge(num_kept, h * 32 + c * 4 + 4)
                    nc.vector.scalar_tensor_tensor(out=hv[:, 0, :], in0=num[:, :, DV], scalar=-1.0,
                                                   in1=colt[:, c, 64:64 + HEADS], op0=ALU.mult, op1=ALU.max)\
                        .then_inc(post_step, 1)
                    dve.wait_ge(post_step, p0 + 1)
                    nc.vector.tensor_tensor(hv[:, 0, :], hv[:, 0, :], num[:, :, DV], ALU.max).then_inc(post_step, 1)
                    dve.wait_ge(post_step, p0 + 2)
                    nc.vector.reciprocal(hv[:, 1, :], hv[:, 0, :]).then_inc(post_step, 1)
                    dve.wait_ge(sq_done, h * 8 + c + 1)
                    nc.vector.tensor_reduce(hv[:, 2, :], hrow[:, :, :], AX_X, ALU.add).then_inc(post_step, 1)
                    dve.wait_ge(post_step, p0 + 4)
                    nc.vector.tensor_tensor(hv[:, 3, :], hv[:, 1, :], hv[:, 1, :], ALU.mult).then_inc(post_step, 1)
                    dve.wait_ge(post_step, p0 + 5)
                    nc.vector.tensor_tensor(hv[:, 4, :], hv[:, 3, :], hv[:, 2, :], ALU.mult).then_inc(post_step, 1)
                    dve.wait_ge(post_step, p0 + 6)
                    nc.vector.tensor_scalar(hv[:, 5, :], hv[:, 4, :], 1.0 / DV, EPS, ALU.mult, ALU.add)\
                        .then_inc(post_step, 1)

                def head_scale_b(c):
                    p0 = h * 88 + c * 11
                    dve.wait_ge(hrs_done, h * 8 + c + 1)
                    nc.vector.tensor_tensor(hv[:, 8, :], hv[:, 7, :], hv[:, 7, :], ALU.mult).then_inc(post_step, 1)
                    dve.wait_ge(post_step, p0 + 8)
                    nc.vector.scalar_tensor_tensor(out=hv[:, 9, :], in0=hv[:, 8, :], scalar=-0.5, in1=hv[:, 5, :],
                                                   op0=ALU.mult, op1=ALU.mult).then_inc(post_step, 1)
                    dve.wait_ge(post_step, p0 + 9)
                    nc.vector.scalar_tensor_tensor(out=hv[:, 8, :], in0=hv[:, 9, :], scalar=1.5, in1=hv[:, 7, :],
                                                   op0=ALU.add, op1=ALU.mult).then_inc(post_step, 1)
                    dve.wait_ge(post_step, p0 + 10)
                    nc.vector.tensor_tensor(hv[:, 0, :], hv[:, 8, :], hv[:, 1, :], ALU.mult).then_inc(post_step, 1)
                    dve.wait_ge(post_step, p0 + 11)
                    nc.vector.tensor_tensor(hrow[:, :, :], num[:, :, 0:DV],
                                            hv[:, 0, :].unsqueeze(2).broadcast_to([P, HEADS, DV]), ALU.mult)\
                        .then_inc(h_done, 1)

                def chunk(c, before):
                    weigh(c)
                    weigh_scores(c, 0)
                    weigh_scores(c, 1)
                    if before is not None:
                        head_scale_a(before)
                    update_state(c, 0)
                    if before is not None:
                        head_scale_b(before)
                    update_state(c, 1)
                    update_state(c, 2)
                    update_state(c, 3)

                chunk(0, None)
                with dve.Fori(1, TILES) as c:
                    chunk(c, c - 1)
                head_scale_a(TILES - 1)
                head_scale_b(TILES - 1)

                for b in range(V_END, BLOCKS):
                    if b + 1 < BLOCKS:
                        split_block(h, b + 1)
                    if b >= BLOCKS - 2:
                        split_piece(h, b - (BLOCKS - 2))
                    i = b - V_END
                    if i == 0:
                        dve.wait_ge(ht_kept, past(h * 8 + 8))
                    for t in range(TBS):
                        bank = banks(2 * (b % 2) + t)
                        dve.wait_ge(oexp_done, h * 16 + 2 * i + t + 1)
                        nc.vector.tensor_scalar(bank, bank, 1.0, None, ALU.add).then_inc(o1_done, 1)
                        dve.wait_ge(o1_done, h * 32 + 4 * i + 2 * t + 1)
                        nc.vector.reciprocal(bank, bank).then_inc(o1_done, 1)
                        dve.wait_ge(o1_done, h * 32 + 4 * i + 2 * t + 2)
                        nc.vector.scalar_tensor_tensor(
                            out=hg[:, i, t * NB:t * NB + NB].rearrange("p (c n) -> p c n", n=P),
                            in0=v1[:, 4 * t:4 * t + 4, i, 0:DV], scalar=head_g[:, i:i + 1],
                            in1=bank.rearrange("p (c n) -> p c n", n=P), op0=ALU.mult, op1=ALU.mult)\
                            .then_inc(hg_done, 1)

                for i in range(TILES):
                    dve.wait_ge(hghi_done, h * 8 + i + 1)
                    nc.vector.tensor_tensor(u_lo[:, :, i * P:i * P + P], hg[:, :, i * P:i * P + P],
                                            u_hi[:, :, i * P:i * P + P].bitcast(F32), ALU.subtract)\
                        .then_inc(hglo_done, 1)
                split_piece(h, 2)
                split_piece(h, 3)

                def add_out(i, jj):
                    m = jj * TILES + i
                    dve.wait_ge(res_loaded[i // 2], h * 16 + 16)
                    dve.wait_ge(outp_done, past(h * 16 + m + 1))
                    nc.vector.tensor_tensor(res[:, i, jj * NB:jj * NB + NB], banks(m % 4),
                                            res[:, i, jj * NB:jj * NB + NB], ALU.add).then_inc(res_added, 1)

                for i in range(TILES):
                    add_out(i, 0)
                split_gate_up(h, 0, 0)
                dve.wait_ge(gain_loaded, h * 32 + 32)
                for i in range(TILES):
                    add_out(i, 1)
                    norm_rows((h * XT + TILES + i, i % 2), res[:, i, :], gain2[:, :], xn2[i % 2][:, :])
                    if i >= 2:
                        norm_lo(h * XT + TILES + i - 2, slice((i - 2) * P, (i - 1) * P), 4 + 2 * (i % 2))
                for i in range(TILES - 2, TILES):
                    norm_lo(h * XT + TILES + i, slice(i * P, i * P + P), 4 + 2 * (i % 2))

                def hidden(n, o):
                    dve.wait_ge(silu_done, h * GU + n * 4 + o + 1)
                    nc.vector.tensor_tensor(sg[:, o % 2, :], banks(2 * (o % 2) + 1), sg[:, o % 2, :], ALU.mult)\
                        .then_inc(gf_done, 1)

                def hidden_lo(n, o):
                    dve.wait_ge(ghi_done, h * GU + n * 4 + o + 1)
                    nc.vector.tensor_tensor(g_lo[o % 2][o // 2][:, :], sg[:, o % 2, :],
                                            g_hi[o % 2][o // 2][:, :].bitcast(F32), ALU.subtract)\
                        .then_inc(glo_done, 1)

                def add_down(n, t, lo, hi):
                    for q in range(lo, hi):
                        i, jj = 4 * t + q // 2, q % 2
                        dve.wait_ge(dn_done, past(h * DN + n * 16 + (8 * t + q + 1)))
                        nc.vector.tensor_tensor(res[:, i, jj * NB:jj * NB + NB], banks(4 + q % 4),
                                                res[:, i, jj * NB:jj * NB + NB], ALU.add).then_inc(dn_added, 1)

                def ffn_group(n, is_first, is_last):
                    split_gate_up(h, n, 1)
                    hidden(n, 0)
                    hidden_lo(n, 0)
                    if not is_first:
                        add_down(n - 1, 1, 0, 8)
                    for f in range(2):
                        dve.wait_ge(dn_hi_done, h * (2 * GROUPS) + n * 2 + f + 1)
                        nc.vector.tensor_tensor(dn_lo[:, f, :], dn_raw[:, f, :], dn_hi[:, f, :].bitcast(F32),
                                                ALU.subtract).then_inc(dn_lo_done, 1)
                    hidden(n, 1)
                    hidden_lo(n, 1)
                    hidden(n, 2)
                    hidden_lo(n, 2)
                    add_down(n, 0, 0, 4)
                    if not is_last:
                        split_gate_up(h, n + 1, 0)
                    add_down(n, 0, 4, 8)
                    hidden(n, 3)
                    hidden_lo(n, 3)

                ffn_group(0, True, False)
                with dve.Fori(1, GROUPS - 1) as n:
                    ffn_group(n, False, False)
                ffn_group(GROUPS - 1, False, True)
                add_down(GROUPS - 1, 1, 0, 8)

        @block.tensor
        def _(pe):
            def three_passes(out_, steps):
                n = len(steps)
                for k, (wh, wl, mh, ml) in enumerate(steps):
                    pe.matmul(out_, wh, ml, start=(k == 0), stop=False)
                    pe.matmul(out_, wh, mh, start=False, stop=False)
                    last = pe.matmul(out_, wl, mh, start=False, stop=(k == n - 1))
                return last

            def turn_rows(src, bank):
                for k in range(KD):
                    last = pe.transpose(ps[:, bank + k // 4, (k % 4) * P:(k % 4) * P + P], src[:, k * P:k * P + P],
                                        ident[:, :])
                last.then_inc(xt_done, 1)

            def project(h, b, s, t):
                three_passes(banks(2 * s + t),
                             [(wp_hi[s][:, k, :], wp_lo[s][:, k, :], u_hi[:, k, t * NB:t * NB + NB],
                               u_lo[:, k, t * NB:t * NB + NB]) for k in range(KD)]).then_inc(proj_done, 1)

            start_at_one(pe, outp_done, gu_done, h_turned, proj_done, xt_done, dn_done, vt_done)
            pe.wait_ge(const_dve, 2)

            with pe.Fori(0, HALVES) as h:
                pe.wait_ge(gf_done, past(h * GU))
                pe.sem_inc(pe_passed, 1)
                with pe.Fori(0, TILES // 2) as j:
                    for s in range(2):
                        pe.wait_ge(xn_done, h * XT + j * 2 + s + 1)
                        pe.wait_ge(ulo_done, past(h * XT + j * 2))
                        turn_rows(xn1[s], 2 * s)

                pe.wait_ge(if_lo_done, past(h + 1))
                pe.wait_ge(ulo_done, past(h * XT + TILES))
                pe.wait_ge(dn_added, past(h * DN))
                for t in range(TBS):
                    three_passes(banks(4 + t),
                                 [(if_hi[:, k, :], if_lo[:, k, :], u_hi[:, k, t * NB:t * NB + NB],
                                   u_lo[:, k, t * NB:t * NB + NB]) for k in range(KD)]).then_inc(if_done, 1)

                with pe.Fori(0, QK_BLOCKS // 2) as j:
                    for s in range(2):
                        pe.wait_ge(split_lo, past(h * SP_ + j * 2 + s + 1))
                        pe.wait_ge(qk_kept, past(h * 16 + j * 4))
                        for t in range(TBS):
                            project(h, None, s, t)

                pe.wait_ge(gate_act, h * 7 + 7)
                for c in range(TILES):
                    last = pe.transpose(ps[:, 6 + c // 4, (c % 4) * P:(c % 4) * P + P], cols[:, c * P:c * P + P],
                                        ident[:, :])
                last.then_inc(colt_turned, 1)

                pe.wait_ge(qk_kept, past(h * 16 + 16))
                pe.wait_ge(gate_dve, h * 13 + 3)
                pe.sem_inc(pe_passed, 1)

                def turn_v(j, s, t):
                    n = j * 4 + 2 * s + t
                    pe.wait_ge(v_staged, past(h * 16 + n + 1))
                    if s > 0:
                        pe.wait_ge(v_kept, past(h * 16 + n - 1))
                    else:
                        pe.wait_ge(v_kept, past(h * 16 + j * 4))
                    for q in range(4):
                        last = pe.transpose(ps[:, 4 + t, q * P:q * P + P], v_st[:, t, q * P:q * P + P], ident[:, :])
                    last.then_inc(vt_done, 1)

                with pe.Fori(0, (V_END - QK_BLOCKS) // 2) as j:
                    pe.wait_ge(split_lo, past(h * SP_ + j * 2 + (QK_BLOCKS + 1)))
                    pe.wait_ge(v_staged, past(h * 16 + j * 4))
                    project(h, None, 0, 0)
                    project(h, None, 0, 1)
                    turn_v(j, 0, 0)
                    pe.wait_ge(split_lo, past(h * SP_ + j * 2 + (QK_BLOCKS + 2)))
                    project(h, None, 1, 0)
                    turn_v(j, 0, 1)
                    project(h, None, 1, 1)
                    turn_v(j, 1, 0)
                    turn_v(j, 1, 1)

                def spread(c):
                    now = bass.ds(c * P, P)
                    pe.wait_ge(state_done, past(h * 64 + c * 8))
                    for g in range(4):
                        pair = pick[:, :, :].rearrange("p h c -> p (h c)")[:, 2 * g * P + DQK:2 * g * P + DQK + P]
                        last = pe.matmul(ps[:, 0, g * P:g * P + P], pair, wint[:, now],
                                         start=(g == 0), stop=(g == 3), skip_group_check=True)
                    last.then_inc(wint_spread, 1)
                    for half in range(2):
                        pe.matmul(banks(1 + half), ident_b[:, :], mask[:, :, :].rearrange("p a t -> p (a t)"),
                                  start=True, stop=False, skip_group_check=True)
                        for i in range(4):
                            last = pe.matmul(ps[:, 1 + half, i * P:i * P + P], pick[:, 4 * half + i, :], negm[:, now],
                                             start=False, stop=(i == 3), skip_group_check=True)
                    last.then_inc(darg_done, 1)
                    pe.wait_ge(qkc_ready, h * 8 + c + 1)
                    for g in range(4):
                        last = pe.transpose(ps[:, 3, g * P:g * P + P], qkc[:, 4 + g, :], ident[:, :])
                    last.then_inc(k_turned, 1)

                def scores(c, q):
                    pe.wait_ge(sd_done, past(h * 16 + c * 2 + q))
                    for g in (2 * q, 2 * q + 1):
                        for a in range(2):
                            r = slice(64 * a, 64 * a + 64)
                            last = pe.matmul(ps[:, 6 + a, (g % 2) * P:(g % 2) * P + P], qkc[r, 4 + g, :],
                                             qkc[r, g, :], start=True, stop=True, skip_group_check=True)
                    last.then_inc(s_done, 1)

                def state_sum(c, g):
                    if g == 0:
                        pe.wait_ge(kw_done, h * 8 + c + 1)
                    elif g == 1:
                        pe.wait_ge(qw_done, h * 8 + c + 1)
                        pe.wait_ge(dec_done, h * 8 + c + 1)
                    else:
                        pe.wait_ge(state_done, past(h * 64 + c * 8 + 2 * (g - 1)))
                    pe.matmul(ps[:, 3 if g % 2 == 0 else 0, 0:2 * VW],
                              kw[:, 2 * g:2 * g + 2, :], v1[:, c, 2 * g:2 * g + 2, :],
                              start=True, stop=True).then_inc(upd_done, 1)

                def outputs(c, g, is_first):
                    if g >= 2 or not is_first:
                        pe.wait_ge(num_kept, h * 32 + c * 4 + g - 1)
                    pe.wait_ge(sd_done, past(h * 16 + c * 2 + g // 2 + 1))
                    pe.matmul(ps[:, 4 + g % 2, 0:2 * VW], qw[:, g, :], state[:, g, :], start=True, stop=False,
                              skip_group_check=True)
                    for a in range(2):
                        last = pe.matmul(ps[:, 4 + g % 2, a * VW:a * VW + VW], dmat[:, 2 * g + a, :],
                                         v1[:, c, 2 * g + a, :], start=False, stop=(a == 1), skip_group_check=True)
                    last.then_inc(n_done, 1)

                def turn_heads(c):
                    pe.wait_ge(h_done, past(h * 8 + c + 1))
                    for i in range(HEADS):
                        last = pe.transpose(ps[:, 1 + i // 4, (i % 4) * P:(i % 4) * P + P], hrow[:, i, :],
                                            ident[:, :])
                    last.then_inc(h_turned, 1)

                def chunk(c, before):
                    if before is not None:
                        pe.wait_ge(ht_kept, past(h * 8 + before))
                    spread(c)
                    scores(c, 0)
                    state_sum(c, 0)
                    state_sum(c, 1)
                    scores(c, 1)
                    outputs(c, 0, before is None)
                    outputs(c, 1, before is None)
                    state_sum(c, 2)
                    outputs(c, 2, before is None)
                    state_sum(c, 3)
                    outputs(c, 3, before is None)
                    if before is not None:
                        pe.wait_ge(dmat_done, h * 64 + c * 8 + 8)
                        turn_heads(before)

                pe.wait_ge(v_staged, past(h * 16 + 16))
                pe.wait_ge(v_kept, past(h * 16 + 16))
                pe.wait_ge(gate_dve, h * 13 + 13)
                pe.wait_ge(colt_kept, h + 1)
                chunk(0, None)
                with pe.Fori(1, TILES) as c:
                    chunk(c, c - 1)
                pe.wait_ge(ht_kept, past(h * 8 + TILES - 1))
                turn_heads(TILES - 1)

                pe.wait_ge(state_done, past(h * 64 + 64))
                pe.wait_ge(ht_kept, past(h * 8 + 8))
                pe.sem_inc(pe_passed, 1)
                with pe.Fori(0, (BLOCKS - V_END) // 2) as j:
                    for s in range(2):
                        pe.wait_ge(split_lo, past(h * SP_ + j * 2 + (V_END + s + 1)))
                        for t in range(TBS):
                            if s == 0 and t == 0:
                                pe.wait_ge(hg_done, past(h * 16 + j * 4))
                            project(h, None, s, t)

                def out_group(i, jj):
                    m = jj * TILES + i
                    rows = slice(i * P, i * P + P)
                    if jj == 0:
                        pe.wait_ge(hglo_done, h * 8 + i + 1)
                    if m >= 4:
                        pe.wait_ge(res_added, h * 16 + m - 3)
                    three_passes(banks(m % 4), [(u_hi[:, k, rows], u_lo[:, k, rows], wo[jj][0][:, k, :],
                                                 wo[jj][1][:, k, :]) for k in range(KD)]).then_inc(outp_done, 1)

                def turn_norm2(i):
                    pe.wait_ge(xn_done, h * XT + TILES + i + 1)
                    if i >= 2:
                        pe.wait_ge(ulo_done, past(h * XT + TILES + i - 1))
                    turn_rows(xn2[i % 2], 4 + 2 * (i % 2))

                pe.wait_ge(hg_done, past(h * 16 + 16))
                pe.wait_ge(split_lo, past(h * SP_ + OUT0 + 2))
                for i in range(TILES):
                    out_group(i, 0)
                pe.wait_ge(split_lo, past(h * SP_ + OUT0 + 4))
                for i in range(TILES):
                    out_group(i, 1)
                    if i >= 2:
                        turn_norm2(i - 2)

                def gate_up(n, o):
                    f, t = o % 2, o // 2
                    pe.wait_ge(split_lo, past(h * SP_ + n * 4 + (FF0 + 2 * f + 2)))
                    pe.wait_ge(gf_done, past(h * GU + n * 4 + o - 1 if o >= 2 else h * GU + n * 4))
                    for s in range(2):
                        last = three_passes(banks(2 * (o % 2) + s),
                                            [(gu_hi[f][:, s, k, :], gu_lo[f][:, s, k, :],
                                              u_hi[:, k, t * NB:t * NB + NB], u_lo[:, k, t * NB:t * NB + NB])
                                             for k in range(KD)])
                    last.then_inc(gu_done, 1)

                def down(n, t):
                    pe.wait_ge(glo_done, past(h * GU + n * 4 + (2 * t + 2)))
                    pe.wait_ge(dn_lo_done, h * (2 * GROUPS) + n * 2 + 2)
                    for q in range(8):
                        i, jj = q // 2, q % 2
                        c = slice(i * P, i * P + P)
                        w = slice(jj * NB, jj * NB + NB)
                        if q >= 4:
                            pe.wait_ge(dn_added, past(h * DN + n * 16 + (8 * t + q - 3)))
                        elif q == 0:
                            pe.wait_ge(dn_added, past(h * DN + n * 16 + 8 * t))
                        three_passes(banks(4 + q % 4), [(g_hi[f][t][:, c], g_lo[f][t][:, c], dn_hi[:, f, w],
                                                         dn_lo[:, f, w]) for f in range(2)]).then_inc(dn_done, 1)

                def ffn_group(n, is_first):
                    gate_up(n, 0)
                    if is_first:
                        turn_norm2(TILES - 2)
                        turn_norm2(TILES - 1)
                    else:
                        down(n - 1, 1)
                    gate_up(n, 1)
                    if is_first:
                        pe.wait_ge(ulo_done, past(h * XT + XT))
                    gate_up(n, 2)
                    down(n, 0)
                    gate_up(n, 3)

                pe.wait_ge(res_added, h * 16 + 16)
                pe.wait_ge(ulo_done, past(h * XT + TILES + 4))
                ffn_group(0, True)
                with pe.Fori(1, GROUPS) as n:
                    ffn_group(n, False)
                down(GROUPS - 1, 1)


_INS = ['x', 'mix_norm_g', 'ffn_norm_g', 'ffn_w_gate', 'ffn_w_up', 'ffn_w_down', 'ml_w_in', 'ml_b_if', 'ml_norm_g',
        'ml_w_out']
_OUTS = [((1, SEQ, D), 'float32')]


def kernel(**inputs):
    import numpy as _np
    import concourse.bacc as _bacc
    from concourse import mybir as _mybir
    from concourse.bass_utils import run_bass_kernel_spmd as _run

    nc = _bacc.Bacc("TRN2", target_bir_lowering=False, num_devices=1)
    arrays, args = {}, []
    for name in _INS:
        a = _np.ascontiguousarray(inputs[name])
        arrays[f"in_{name}_dram"] = a
        args.append(nc.dram_tensor(f"in_{name}_dram", a.shape, _mybir.dt.from_np(a.dtype), kind="ExternalInput").ap())
    for i, (shape, dtype) in enumerate(_OUTS):
        dt = _mybir.dt.from_np(_np.dtype(dtype))
        args.append(nc.dram_tensor(f"out_{i}_dram", shape, dt, kind="ExternalOutput").ap())
    mlstm_layer(nc, *args)
    r = _run(nc, [arrays], core_ids=[0])
    got = tuple(r.results[0][f"out_{i}_dram"] for i in range(len(_OUTS)))
    return got[0]
```

```python
from contextlib import ExitStack

import concourse.bass as bass
from concourse import mybir

F32 = mybir.dt.float32
F32R = mybir.dt.float32r
BF16 = mybir.dt.bfloat16
ALU = mybir.AluOpType
ACT = mybir.ActivationFunctionType
AX_X = mybir.AxisListType.X

P = 128
D = 1024
SEQ = 2048
HEADS = 8
DV = D // HEADS
DQK = D // (2 * HEADS)
FF = 2816
EPS = 1e-6
KD = D // P
HALVES = 2
TOK = SEQ // HALVES
TILES = TOK // P
NB = 512
TBS = TOK // NB
VW = DV + 1
QK_BLOCKS = 8
V_BLOCKS = 8
O_BLOCKS = 8
BLOCKS = QK_BLOCKS + V_BLOCKS + O_BLOCKS
VA, VB, OA, OB, UNITS = 8, 16, 24, 32, 40
GROUPS = FF // (2 * P)
MASKED = -1e30

XT = 2 * TILES
PJ = TBS * BLOCKS
SP_ = UNITS + 4 * GROUPS
GU = 4 * GROUPS
DN = 16 * GROUPS
RAW_VB = VB // 4
RAW_OB = RAW_VB + (OB - VB) // 2
RAW_FF = RAW_OB + (UNITS - OB) // 4
RAW = RAW_FF + GROUPS
FF0 = UNITS


def groups_until(u):
    return TBS * u if u <= QK_BLOCKS else QK_BLOCKS + u


def raw_of(u):
    if VB <= u < OB:
        return u % 2, 0, RAW_VB + (u - VB) // 2
    first, pair = (RAW_OB, (u - OB) // 2) if u >= OB else (0, u // 2)
    return pair % 2, (u % 2) * P, first + pair // 2


def mlstm_layer(nc, x, mix_norm_g, ffn_norm_g, w_gate, w_up, w_down, w_in, b_if, norm_g, w_out, out):
    x_rows = x[0].rearrange("(t p) d -> t p d", p=P)
    out_rows = out[0].rearrange("(t p) d -> t p d", p=P)
    w_in_k = w_in[0].rearrange("(k p) n -> p k n", p=P)
    w_out_k = w_out[0].rearrange("(k p) n -> p k n", p=P)
    w_gate_k = w_gate[0].rearrange("(k p) n -> p k n", p=P)
    w_up_k = w_up[0].rearrange("(k p) n -> p k n", p=P)
    w_down_k = w_down[0].rearrange("(k p) n -> k p n", p=P)

    with ExitStack() as ctx:
        def sem(name):
            return ctx.enter_context(nc.semaphore(name))

        base = -(-nc.sbuf_base // 32) * 32
        top = [base]

        def region(nbytes):
            at = top[0]
            top[0] += -(-nbytes // 32) * 32
            return at

        def place(name, at, shape, dt):
            return nc.alloc_sbuf_tensor_at(name, shape, dt, offset=at)

        def small(name, shape, dt=F32):
            n = 1
            for s in shape[1:]:
                n *= s
            return place(name, region(n * (2 if dt == BF16 else 4)), shape, dt)

        KB = 1024
        r_u = region(64 * KB)
        u_hi = place("u_hi", r_u, [P, KD, TOK], F32R)
        u_lo = place("u_lo", r_u + 32 * KB, [P, KD, TOK], F32R)

        r_v = region(TILES * HEADS * VW * 4)
        v1 = place("v1", r_v, [P, TILES, HEADS, VW], F32)
        res = place("res", r_v, [P, TILES, D], F32)

        r_q = region(32 * KB)
        qk = place("qk", r_q, [P, QK_BLOCKS, TOK], F32)
        hg = place("hg", r_q, [P, KD, TOK], F32)
        wo1 = [place("wo1_hi", r_q, [P, KD, NB], F32R), place("wo1_lo", r_q + 16 * KB, [P, KD, NB], F32R)]
        dn_hi = place("dn_hi", r_q, [P, 2, D], F32R)
        dn_lo = place("dn_lo", r_q + 8 * KB, [P, 2, D], F32R)
        dn_raw = place("dn_raw", r_q + 16 * KB, [P, 2, D], F32)
        sg = place("sg", r_q + 24 * KB, [P, 2, NB], F32)
        x_in = [place("x_in0", r_q + 28 * KB, [P, D], F32), place("x_in1", r_q + 24 * KB, [P, D], F32)]

        r_a = region(16 * KB)
        wp_hi = [place(f"wp_hi{s}", r_a + 8 * KB * s, [P, KD, P], F32R) for s in range(2)]
        wp_lo = [place(f"wp_lo{s}", r_a + 8 * KB * s + 4 * KB, [P, KD, P], F32R) for s in range(2)]
        gain2 = place("gain2", r_a, [P, D], F32)
        xn2 = [place(f"xn2_{s}", r_a + 4 * KB * (s + 1), [P, D], F32) for s in range(2)]
        g_hi = [[place(f"g_hi{f}{t}", r_a + 2 * KB * (2 * f + t), [P, NB], F32R) for t in range(2)] for f in range(2)]
        g_lo = [[place(f"g_lo{f}{t}", r_a + 2 * KB * (4 + 2 * f + t), [P, NB], F32R) for t in range(2)] for f in range(2)]

        r_b = region(16 * KB)
        raw = [place(f"raw{s}", r_b + 8 * KB * s, [P, KD, 2 * P], F32) for s in range(2)]

        r_c = region(28 * KB + HEADS * VW * 4)
        cols = place("cols", r_c, [P, TOK], F32)
        negm = place("negm", r_c + 4 * KB, [P, TOK], F32R)
        wint = place("wint", r_c + 8 * KB, [P, TOK], F32R)
        t0 = place("t0", r_c + 12 * KB, [HEADS, TOK], F32)
        t1 = place("t1", r_c + 16 * KB, [HEADS, TOK], F32)
        t2 = place("t2", r_c + 20 * KB, [HEADS, TOK], F32)
        t3 = place("t3", r_c + 24 * KB, [HEADS, TOK], F32)
        t4 = place("t4", r_c + 28 * KB, [HEADS, TOK], F32)
        if_hi = place("if_hi", r_c + 12 * KB, [P, KD, P], F32R)
        if_lo = place("if_lo", r_c + 16 * KB, [P, KD, P], F32R)
        xn1 = [place(f"xn1_{s}", r_c + (20 + 4 * s) * KB, [P, D], F32) for s in range(2)]
        gain1 = place("gain1", r_c + 28 * KB, [P, D], F32)
        v_st = place("v_st", r_c, [P, 2, NB], F32)
        dmat = place("dmat", r_c + 12 * KB, [P, HEADS, P], F32)
        hrow = place("hrow", r_c + 16 * KB, [P, HEADS, DV], F32)
        qkc = place("qkc", r_c + 20 * KB, [P, QK_BLOCKS, P], F32)
        kw = place("kw", r_c + 24 * KB, [P, HEADS, DQK], F32)
        qw = place("qw", r_c + 26 * KB, [P, 4, P], F32)
        num = place("num", r_c + 28 * KB, [P, HEADS, VW], F32)
        wo0 = [place("wo0_hi", r_c, [P, KD, NB], F32R), place("wo0_lo", r_c + 16 * KB, [P, KD, NB], F32R)]
        gu_hi = [place(f"gu_hi{f}", r_c + 16 * KB * f, [P, 2, KD, P], F32R) for f in range(2)]
        gu_lo = [place(f"gu_lo{f}", r_c + 16 * KB * f + 8 * KB, [P, 2, KD, P], F32R) for f in range(2)]
        wo = [wo0, wo1]
        wo_raw = [place("wo0_raw", r_c + 16 * KB, [P, KD, NB], F32), place("wo1_raw", r_q + 16 * KB, [P, KD, NB], F32)]

        state = small("state", [P, 4, 2 * VW])
        colt = small("colt", [P, TILES, 72])
        ident = small("ident", [P, P])
        ident_b = small("ident_b", [P, P], BF16)
        pick = small("pick", [P, HEADS, P], F32R)
        mask = small("mask", [P, 4, P], BF16)
        not_first = small("not_first", [HEADS, TOK], BF16)
        if_raw = small("if_raw", [P, KD, 2 * HEADS])
        bias_i = small("bias_i", [HEADS, 1])
        bias_f = small("bias_f", [64, 1])
        head_g = small("head_g", [P, HEADS])
        m_end = small("m_end", [HEADS, 1])
        m_prev = small("m_prev", [HEADS, TILES])
        nm_end = small("nm_end", [HEADS, TILES])
        dec = small("dec", [P, 4])
        nv = small("nv", [P, 2, 8])
        hv = small("hv", [P, 10, HEADS])
        assert top[0] <= nc.sbuf_usable_end, (top[0], nc.sbuf_usable_end)
        pick_src = place("pick_src", r_q, [P, HEADS, P], F32)

        ps = ctx.enter_context(nc.psum_tensor("ps", [P, 8, NB], F32))

        def banks(b, n=1):
            return ps[:, b:b + n, :].rearrange("p b n -> p (b n)")

        x_loaded = [sem(f"x_loaded{s}") for s in range(2)]
        gain_loaded = sem("gain_loaded")
        if_loaded = sem("if_loaded")
        raw_loaded = [sem(f"raw_loaded{s}") for s in range(2)]
        wo_loaded = [sem(f"wo_loaded{s}") for s in range(2)]
        dn_loaded = [sem(f"dn_loaded{s}") for s in range(2)]
        res_loaded = [sem(f"res_loaded{s}") for s in range(4)]
        bias_loaded = sem("bias_loaded")
        out_stored = sem("out_stored")
        const_pool = sem("const_pool")
        const_dve = sem("const_dve")
        prep_done = sem("prep_done")
        pool_passed = sem("pool_passed")
        dve_passed = sem("dve_passed")
        pe_passed = sem("pe_passed")
        ssq_done = sem("ssq_done")
        var_done = sem("var_done")
        lnv_done = sem("lnv_done")
        rstd0_done = sem("rstd0_done")
        rstd_step = sem("rstd_step")
        xn_done = sem("xn_done")
        xt_done = sem("xt_done")
        uhi_done = sem("uhi_done")
        ulo_done = sem("ulo_done")
        split_hi = sem("split_hi")
        split_lo = sem("split_lo")
        if_hi_done = sem("if_hi_done")
        if_lo_done = sem("if_lo_done")
        dn_hi_done = sem("dn_hi_done")
        dn_lo_done = sem("dn_lo_done")
        if_done = sem("if_done")
        proj_done = sem("proj_done")
        qk_kept = sem("qk_kept")
        v_staged = sem("v_staged")
        vt_done = sem("vt_done")
        v_kept = sem("v_kept")
        gate_dve = sem("gate_dve")
        gate_act = sem("gate_act")
        colt_turned = sem("colt_turned")
        colt_kept = sem("colt_kept")
        qkc_ready = sem("qkc_ready")
        wint_spread = sem("wint_spread")
        darg_done = sem("darg_done")
        k_turned = sem("k_turned")
        dmat_done = sem("dmat_done")
        dec_done = sem("dec_done")
        qw_done = sem("qw_done")
        kw_done = sem("kw_done")
        s_done = sem("s_done")
        sd_done = sem("sd_done")
        upd_done = sem("upd_done")
        n_done = sem("n_done")
        num_kept = sem("num_kept")
        state_done = sem("state_done")
        sq_done = sem("sq_done")
        post_step = sem("post_step")
        hln_done = sem("hln_done")
        hrs_done = sem("hrs_done")
        h_done = sem("h_done")
        h_turned = sem("h_turned")
        ht_kept = sem("ht_kept")
        o_step = sem("o_step")
        o_gated = sem("o_gated")
        hg0_done = sem("hg0_done")
        hg1_done = sem("hg1_done")
        wohi_done = sem("wohi_done")
        wolo_done = sem("wolo_done")
        hghi_done = sem("hghi_done")
        hglo_done = sem("hglo_done")
        outp_done = sem("outp_done")
        res_added = sem("res_added")
        gu_done = sem("gu_done")
        silu_done = sem("silu_done")
        gf_done = sem("gf_done")
        ghi_done = sem("ghi_done")
        glo_done = sem("glo_done")
        dn_done = sem("dn_done")
        dn_added = sem("dn_added")

        def past(count):
            return count + 1

        def start_at_one(engine, *counters):
            for counter in counters:
                engine.sem_inc(counter, 1)

        block = ctx.enter_context(nc.Block())

        def head_values(c):
            return v1[:, c, :, 0:DV]

        @block.sync
        def _(sp):
            sp.dma_start(bias_i[:, :], b_if[0, 0:HEADS].rearrange("(p a) -> p a", a=1)).then_inc(bias_loaded, 16)
            sp.dma_start(bias_f[32:32 + HEADS, :], b_if[0, HEADS:2 * HEADS].rearrange("(p a) -> p a", a=1))\
                .then_inc(bias_loaded, 16)
            sp.dma_start(head_g[:, :], norm_g[0].rearrange("(h p) -> p h", p=P),
                         allow_slow_non_contiguous=True).then_inc(bias_loaded, 16)

            def load_out(jj):
                for s in range(2):
                    rows = slice(4 * s, 4 * s + 4)
                    sp.dma_start(wo_raw[jj][:, rows, :], w_out_k[:, rows, NB * jj:NB * jj + NB])\
                        .then_inc(wo_loaded[s], 16)

            def load_pair(p, s):
                sp.dma_start(raw[s][:, :, :], w_in_k[:, :, bass.ds(p * 2 * P, 2 * P)]).then_inc(raw_loaded[s], 16)

            def load_down(n, f):
                sp.dma_start(dn_raw[:, f, :], w_down_k[2 * n + f]).then_inc(dn_loaded[f], 16)

            def load_gate_up(n, s):
                w = w_gate_k if s == 0 else w_up_k
                sp.dma_start(raw[s][:, :, :], w[:, :, bass.ds(n * 2 * P, 2 * P)]).then_inc(raw_loaded[s], 16)

            with sp.Fori(0, HALVES) as h:
                sp.wait_ge(outp_done, past(h * 16))
                sp.dma_start(x_in[0][:, :], x_rows[h * TILES]).then_inc(x_loaded[0], 16)
                sp.wait_ge(glo_done, past(h * GU))
                sp.dma_start(x_in[1][:, :], x_rows[h * TILES + 1]).then_inc(x_loaded[1], 16)
                sp.wait_ge(gu_done, past(h * GU))
                sp.dma_start(gain1[:, :], mix_norm_g[0:1, :].partition_broadcast(P)).then_inc(gain_loaded, 16)
                sp.wait_ge(if_lo_done, past(h))
                sp.wait_ge(split_lo, past(h * SP_))
                sp.dma_start(if_raw[:, :, :], w_in_k[:, :, BLOCKS * P:BLOCKS * P + 2 * HEADS]).then_inc(if_loaded, 16)
                with sp.Fori(1, TILES // 2) as j:
                    for s in range(2):
                        sp.wait_ge(xn_done, h * XT + 2 * j + s - 1)
                        sp.dma_start(x_in[s][:, :], x_rows[h * TILES + 2 * j + s]).then_inc(x_loaded[s], 16)
                load_pair(0, 0)
                load_pair(1, 1)
                with sp.Fori(1, VB // 4) as j:
                    for s in range(2):
                        sp.wait_ge(split_lo, past(h * SP_ + 4 * j + 2 * s - 2))
                        load_pair(2 * j + s, s)
                with sp.Fori(0, TILES) as c:
                    for s in range(2):
                        sp.wait_ge(split_lo, past(h * SP_ + 2 * c + (VB - 1 + s)))
                        sp.dma_start(raw[s][:, :, 0:P], w_in_k[:, :, bass.ds((QK_BLOCKS + s) * P + c * (2 * P), P)])\
                            .then_inc(raw_loaded[s], 16)
                for p in range(2):
                    sp.wait_ge(split_lo, past(h * SP_ + OB - 1 + p))
                    load_pair((BLOCKS - O_BLOCKS) // 2 + p, p)
                sp.wait_ge(h_turned, past(h * 8 + 8))
                load_out(0)
                for p in range(2, 4):
                    sp.wait_ge(split_lo, past(h * SP_ + OB + 2 * p - 2))
                    load_pair((BLOCKS - O_BLOCKS) // 2 + p, p % 2)
                for s in range(2):
                    sp.wait_ge(split_lo, past(h * SP_ + UNITS - 2 + 2 * s))
                    load_gate_up(0, s)
                sp.wait_ge(proj_done, past(h * PJ + PJ))
                sp.dma_start(gain2[:, :], ffn_norm_g[0:1, :].partition_broadcast(P)).then_inc(gain_loaded, 16)
                sp.wait_ge(hglo_done, h * 8 + 8)
                load_out(1)
                sp.wait_ge(outp_done, past(h * 16 + 16))
                load_down(0, 0)
                load_down(0, 1)
                with sp.Fori(1, GROUPS) as n:
                    for s in range(2):
                        sp.wait_ge(split_lo, past(h * SP_ + n * 4 + (FF0 - 1 + s)))
                        load_gate_up(n, s)
                    for f in range(2):
                        sp.wait_ge(dn_lo_done, h * (2 * GROUPS) + n * 2 + (f - 1))
                        load_down(n, f)

        @block.gpsimd
        def _(pool):
            nc.gpsimd.memset(ident[:, :], 0.0).then_inc(const_pool, 1)
            nc.gpsimd.memset(mask[:, :, :], 0.0).then_inc(const_pool, 1)
            nc.gpsimd.memset(pick_src[:, :, :], 0.0).then_inc(const_pool, 1)
            pool.wait_ge(const_pool, 3)
            nc.gpsimd.affine_select(out=ident[:, :], in_=ident[:, :], compare_op=ALU.not_equal, fill=1.0, base=0,
                                    pattern=[[-1, P]], channel_multiplier=1).then_inc(const_pool, 1)
            nc.gpsimd.affine_select(out=mask[:, :, :], in_=mask[:, :, :], compare_op=ALU.is_ge, fill=MASKED, base=0,
                                    pattern=[[0, 4], [1, P]], channel_multiplier=-1).then_inc(const_pool, 1)
            nc.gpsimd.affine_select(out=pick_src[:, :, :], in_=pick_src[:, :, :], compare_op=ALU.not_equal, fill=1.0,
                                    base=0, pattern=[[-1, HEADS], [0, P]], channel_multiplier=1)\
                .then_inc(const_pool, 1)
            pool.wait_ge(const_pool, 6)
            nc.gpsimd.affine_select(out=pick_src[:, :, :], in_=pick_src[:, :, :], compare_op=ALU.not_equal, fill=1.0,
                                    base=-32, pattern=[[-1, HEADS], [0, P]], channel_multiplier=1)\
                .then_inc(const_pool, 1)
            nc.gpsimd.memset(state[:, :, :], 0.0).then_inc(const_pool, 1)
            nc.gpsimd.memset(m_end[:, :], 0.0).then_inc(const_pool, 1)
            nc.gpsimd.memset(not_first[:, :], 1.0).then_inc(const_pool, 1)
            pool.wait_ge(const_pool, 10)
            nc.gpsimd.memset(not_first[:, :].rearrange("p (c t) -> p c t", t=P)[:, :, 0:1], 0.0)\
                .then_inc(const_pool, 1)

            def clear_rows():
                for tile in (if_hi, if_lo):
                    nc.gpsimd.memset(tile[:, :, :].bitcast(F32), 0.0).then_inc(prep_done, 1)
                nc.gpsimd.memset(cols[:, :], 0.0).then_inc(prep_done, 1)
                for tile in (negm, wint):
                    nc.gpsimd.memset(tile[:, :].bitcast(F32), 0.0).then_inc(prep_done, 1)

            def set_ones():
                nc.gpsimd.memset(v1[:, :, :, DV:VW], 1.0).then_inc(prep_done, 1)

            clear_rows()
            set_ones()
            with pool.Fori(0, HALVES) as h:
                def squares(c):
                    pool.wait_ge(num_kept, h * 32 + c * 4 + 4)
                    pool.wait_ge(h_turned, past(h * 8 + c))
                    nc.gpsimd.tensor_tensor(hrow[:, :, :], num[:, :, 0:DV], num[:, :, 0:DV], ALU.mult)\
                        .then_inc(sq_done, 1)

                with pool.Fori(0, TILES) as c:
                    squares(c)
                pool.wait_ge(hg1_done, past(h * 8 + 8))
                pool.sem_inc(pool_passed, 1)
                for q in range(4):
                    pool.dma_start(res[:, 2 * q:2 * q + 2, :],
                                   x_rows[bass.ds(h * TILES + 2 * q, 2)].rearrange("t p d -> p t d"))\
                        .then_inc(res_loaded[q], 16)
                for i in range(TILES):
                    pool.wait_ge(dn_added, past(h * DN + (DN - 16 + 2 * i + 2)))
                    pool.sem_inc(pool_passed, 1)
                    pool.dma_start(out_rows[h * TILES + i], res[:, i, :]).then_inc(out_stored, 16)
                pool.wait_ge(gu_done, past(h * GU + GU))
                pool.sem_inc(pool_passed, 1)
                clear_rows()
                pool.wait_ge(out_stored, h * (16 * TILES) + 16 * TILES)
                pool.sem_inc(pool_passed, 1)
                set_ones()
            pool.wait_ge(out_stored, HALVES * 16 * TILES)

        @block.scalar
        def _(act):
            def norm_sum(i, src, junk):
                s = nv[:, i[1], :]
                nc.scalar.activation(junk, src, ACT.Square, accum_out=s[:, 0:1]).then_inc(ssq_done, 1)
                act.wait_ge(var_done, i[0] + 1)
                nc.scalar.activation(s[:, 2:3], s[:, 1:2], ACT.Ln).then_inc(lnv_done, 1)
                act.wait_ge(lnv_done, i[0] + 1)
                nc.scalar.activation(s[:, 3:4], s[:, 2:3], ACT.Exp, scale=-0.5).then_inc(rstd0_done, 1)

            def norm_hi(i, cols_, bank):
                act.wait_ge(xt_done, past(i + 1))
                nc.scalar.copy(u_hi[:, :, cols_], banks(bank, 2).rearrange("p (k t) -> p k t", k=KD))\
                    .then_inc(uhi_done, 1)

            def split_block(h, b):
                act.wait_ge(proj_done, past(h * PJ + groups_until(max(0, b - 1))))
                s, at, n = raw_of(b)
                act.wait_ge(raw_loaded[s], h * (16 * RAW) + 16 * (n + 1))
                nc.scalar.copy(wp_hi[b % 2][:, :, :], raw[s][:, :, at:at + P]).then_inc(split_hi, 1)

            def split_beside(h, c, s):
                act.wait_ge(proj_done, past(h * PJ + c * 2 + (groups_until(VB) + 1 - s)))
                act.wait_ge(raw_loaded[s], h * (16 * RAW) + c * 16 + 16 * (RAW_VB + 2 - s))
                nc.scalar.copy(wp_hi[s][:, :, :], raw[s][:, :, 0:P]).then_inc(split_hi, 1)

            def split_out(h, jj, s):
                act.wait_ge(wo_loaded[s], h * 32 + 16 * (jj + 1))
                rows = slice(4 * s, 4 * s + 4)
                nc.scalar.copy(wo[jj][0][:, rows, :], wo_raw[jj][:, rows, :]).then_inc(wohi_done, 1)

            def split_gate_up(h, n, f):
                for s in range(2):
                    act.wait_ge(raw_loaded[s], h * (16 * RAW) + n * 16 + 16 * (RAW_FF + 1))
                    nc.scalar.copy(gu_hi[f][:, s, :, :], raw[s][:, :, f * P:f * P + P]).then_inc(split_hi, 1)

            start_at_one(act, qk_kept, v_staged, ht_kept, o_gated)
            act.wait_ge(const_pool, 11)
            act.wait_ge(bias_loaded, 48)

            with act.Fori(0, HALVES) as h:
                nc.scalar.preload_act_table_set("natural_log_exp_and_others")
                act.wait_ge(gu_done, past(h * GU))
                with act.Fori(0, TILES // 2) as j:
                    for s in range(2):
                        act.wait_ge(x_loaded[s], h * (8 * TILES) + j * 16 + 16)
                        act.wait_ge(xt_done, past(h * XT + j * 2))
                        norm_sum((h * XT + j * 2 + s, s), x_in[s][:, :], xn1[s][:, :])
                    for s in range(2):
                        norm_hi(h * XT + j * 2 + s, bass.ds(j * (2 * P) + s * P, P), 2 * s)

                act.wait_ge(if_loaded, h * 16 + 16)
                act.wait_ge(prep_done, h * 6 + 2)
                nc.scalar.copy(if_hi[:, :, :].rearrange("p k (a c) -> p k a c", c=32)[:, :, 0:2, 0:HEADS],
                               if_raw[:, :, :].rearrange("p k (a c) -> p k a c", a=2)).then_inc(if_hi_done, 1)
                act.wait_ge(dn_done, past(h * DN))
                split_block(h, 0)

                def gate_part(b):
                    if b == 1:
                        act.wait_ge(gate_dve, h * 13 + 3)
                        nc.scalar.activation(t2[:, :], t2[:, :], ACT.Exp).then_inc(gate_act, 1)
                        act.wait_ge(gate_act, h * 7 + 1)
                        nc.scalar.activation(t2[:, :], t2[:, :], ACT.Ln, bias=1.0).then_inc(gate_act, 1)
                    if b == 3:
                        act.wait_ge(gate_dve, h * 13 + 8)
                        nc.scalar.activation(cols[64:64 + HEADS, :], t3[:, :], ACT.Exp, scale=-1.0)\
                            .then_inc(gate_act, 1)
                        nc.scalar.copy(negm[0:HEADS, :], t4[:, :]).then_inc(gate_act, 1)
                        act.wait_ge(gate_dve, h * 13 + 11)
                        nc.scalar.activation(t2[:, :], t2[:, :], ACT.Exp).then_inc(gate_act, 1)
                        nc.scalar.activation(cols[32:32 + HEADS, :], t0[:, :], ACT.Exp).then_inc(gate_act, 1)
                        act.wait_ge(gate_act, h * 7 + 5)
                        nc.scalar.copy(wint[0:HEADS, :], t2[:, :]).then_inc(gate_act, 1)

                for b in range(QK_BLOCKS):
                    split_block(h, b + 1)
                    gate_part(b)
                    for t in range(TBS):
                        act.wait_ge(proj_done, past(h * PJ + 2 * b + t + 1))
                        nc.scalar.mul(qk[:, b, t * NB:t * NB + NB], banks(2 * (b % 2) + t),
                                      1.0 if b < 4 else float(DQK) ** -0.5).then_inc(qk_kept, 1)

                def stage_v(i, s):
                    act.wait_ge(proj_done, past(h * PJ + i + (groups_until(VA) + 1)))
                    if s is None:
                        act.wait_ge(vt_done, past(h * 16 + max(0, i - 1)))
                        s = i % 2
                    else:
                        act.wait_ge(vt_done, past(h * 16 + i - 1))
                    nc.scalar.copy(v_st[:, s, :], banks(s)).then_inc(v_staged, 1)

                def copy_qk(c):
                    nc.scalar.copy(qkc[:, :, :], qk[:, :, bass.ds(c * P, P)]).then_inc(qkc_ready, 1)

                act.wait_ge(colt_turned, h + 1)
                act.wait_ge(gate_dve, h * 13 + 13)
                act.wait_ge(gate_act, h * 7 + 7)
                act.wait_ge(qk_kept, past(h * 16 + 16))
                for b in range(VA, VB):
                    split_block(h, b + 1)
                    if b < VB - 1:
                        stage_v(b - VA, None)
                copy_qk(h * 0)

                def decay_matrix(c):
                    act.wait_ge(darg_done, h * 8 + c + 1)
                    for i in range(HEADS):
                        nc.scalar.activation(dmat[:, i, :], ps[:, 4 + i // 4, (i % 4) * P:(i % 4) * P + P], ACT.Exp,
                                             bias=colt[:, c, i:i + 1]).then_inc(dmat_done, 1)

                def head_rstd(c):
                    act.wait_ge(post_step, h * 88 + c * 11 + 7)
                    nc.scalar.activation(hv[:, 6, :], hv[:, 5, :], ACT.Ln).then_inc(hln_done, 1)
                    act.wait_ge(hln_done, h * 8 + c + 1)
                    nc.scalar.activation(hv[:, 7, :], hv[:, 6, :], ACT.Exp, scale=-0.5).then_inc(hrs_done, 1)

                def keep_num(c, pairs):
                    act.wait_ge(h_done, past(h * 8 + c))
                    for g in pairs:
                        act.wait_ge(n_done, h * 32 + c * 4 + g + 1)
                        nc.scalar.copy(num[:, 2 * g:2 * g + 2, :],
                                       ps[:, 6 + g % 2, 0:2 * VW].rearrange("p (a n) -> p a n", a=2))\
                            .then_inc(num_kept, 1)

                def keep_turned(c):
                    act.wait_ge(h_turned, past(h * 8 + c + 1))
                    nc.scalar.copy(head_values(c), banks(4, 2).rearrange("p (k t) -> p k t", k=HEADS))\
                        .then_inc(ht_kept, 1)

                def sigmoid(j, bank, dst):
                    act.wait_ge(proj_done, past(h * PJ + j + (groups_until(OA) + 1)))
                    nc.scalar.activation(banks(bank), banks(bank), ACT.Exp, scale=-1.0).then_inc(o_step, 1)
                    act.wait_ge(o_step, h * 32 + j * 2 + 1)
                    nc.scalar.activation(banks(bank), banks(bank), ACT.Ln, bias=1.0).then_inc(o_step, 1)
                    act.wait_ge(o_step, h * 32 + j * 2 + 2)
                    nc.scalar.activation(dst, banks(bank), ACT.Exp, scale=-1.0).then_inc(o_gated, 1)

                def sigmoid_kept(j, bank):
                    sigmoid(j, bank, qk[:, bass.ds(j, 1), 0:NB].rearrange("p a n -> p (a n)"))

                def chunk(c, is_first, v_before, v_beside, is_last=False):
                    if v_before:
                        stage_v(c * 2 + (V_BLOCKS - 1), 1)
                    decay_matrix(c)
                    if not v_before:
                        sigmoid_kept(c * 2 - 9, 1)
                    split_beside(h, c, 1)
                    keep_num(c, (0, 1))
                    if not is_first:
                        keep_turned(c - 1)
                    keep_num(c, (2, 3))
                    if not is_last:
                        act.wait_ge(s_done, h * 8 + c + 1)
                        act.wait_ge(qw_done, h * 8 + c + 1)
                        copy_qk(c + 1)
                    if v_beside:
                        stage_v(c * 2 + V_BLOCKS, 0)
                    else:
                        sigmoid_kept(c * 2 - 8, 0)
                    split_beside(h, c, 0)
                    head_rstd(c)

                act.wait_ge(colt_kept, h + 1)
                chunk(0, True, True, True)
                with act.Fori(1, TILES // 2) as c:
                    chunk(c, False, True, True)
                chunk(TILES // 2, False, True, False)
                with act.Fori(TILES // 2 + 1, TILES - 1) as c:
                    chunk(c, False, False, False)
                chunk(TILES - 1, False, False, False, True)

                sigmoid_kept(O_BLOCKS - 1, 1)
                keep_turned(TILES - 1)

                def split_gated(i):
                    nc.scalar.copy(u_hi[:, :, i * P:i * P + P], hg[:, :, i * P:i * P + P]).then_inc(hghi_done, 1)

                for u in range(OB, UNITS):
                    i = u - OB
                    if u + 1 < UNITS:
                        split_block(h, u + 1)
                    if i in (2, 3, 4, 5):
                        act.wait_ge(hg0_done, h * 8 + 8)
                        act.wait_ge(proj_done, past(h * PJ + groups_until(OB)))
                        split_gated(i - 2)
                    if i >= 6:
                        split_out(h, 0, i - 6)
                    sigmoid(O_BLOCKS + i, i % 2, banks(i % 2))

                act.wait_ge(hg1_done, past(h * 8 + 8))
                for i in range(TILES // 2, TILES):
                    split_gated(i)
                split_out(h, 1, 0)
                split_out(h, 1, 1)
                act.wait_ge(outp_done, past(h * 16 + 8))
                split_gate_up(h, 0, 0)
                for i in range(TILES):
                    act.wait_ge(res_added, h * 16 + 8 + i + 1)
                    if i >= 2:
                        act.wait_ge(xt_done, past(h * XT + TILES + i - 1))
                    norm_sum((h * XT + TILES + i, i % 2), res[:, i, :], xn2[i % 2][:, :])
                    if i >= 2:
                        norm_hi(h * XT + TILES + i - 2, slice((i - 2) * P, (i - 1) * P), 4 + 2 * (i % 2))
                for i in range(TILES - 2, TILES):
                    norm_hi(h * XT + TILES + i, slice(i * P, i * P + P), 4 + 2 * (i % 2))

                def silu(n, o):
                    act.wait_ge(gu_done, past(h * GU + n * 4 + o + 1))
                    act.wait_ge(glo_done, past(h * GU + n * 4 + o - 1 if o >= 2 else h * GU + n * 4))
                    nc.scalar.activation(sg[:, o % 2, :], banks(2 * (o % 2)), ACT.Silu).then_inc(silu_done, 1)

                def hidden_hi(n, o):
                    act.wait_ge(gf_done, past(h * GU + n * 4 + o + 1))
                    act.wait_ge(dn_done, past(h * DN + n * 16 + (-8 if o < 2 else 0) if n is not first else h * DN))
                    nc.scalar.copy(g_hi[o % 2][o // 2][:, :], sg[:, o % 2, :]).then_inc(ghi_done, 1)

                def ffn_group(n, last):
                    act.wait_ge(gu_done, past(h * GU + n * 4))
                    split_gate_up(h, n, 1)
                    silu(n, 0)
                    if n is first:
                        act.wait_ge(xt_done, past(h * XT + XT))
                    hidden_hi(n, 0)
                    act.wait_ge(dn_done, past(h * DN + n * 16))
                    for f in range(2):
                        act.wait_ge(dn_loaded[f], h * (16 * GROUPS) + n * 16 + 16)
                        nc.scalar.copy(dn_hi[:, f, :], dn_raw[:, f, :]).then_inc(dn_hi_done, 1)
                    silu(n, 1)
                    hidden_hi(n, 1)
                    silu(n, 2)
                    hidden_hi(n, 2)
                    if not last:
                        act.wait_ge(gu_done, past(h * GU + n * 4 + 3))
                        split_gate_up(h, n + 1, 0)
                    silu(n, 3)
                    hidden_hi(n, 3)

                first = 0
                ffn_group(first, False)
                with act.Fori(1, GROUPS - 1) as n:
                    ffn_group(n, False)
                ffn_group(GROUPS - 1, True)

        @block.vector
        def _(dve):
            def norm_var(i):
                s = nv[:, i[1], :]
                dve.wait_ge(ssq_done, i[0] + 1)
                nc.vector.tensor_scalar(s[:, 1:2], s[:, 0:1], 1.0 / D, EPS, ALU.mult, ALU.add).then_inc(var_done, 1)
                dve.wait_ge(rstd0_done, i[0] + 1)
                nc.vector.tensor_tensor(s[:, 4:5], s[:, 3:4], s[:, 3:4], ALU.mult).then_inc(rstd_step, 1)
                dve.wait_ge(rstd_step, i[0] * 3 + 1)
                nc.vector.scalar_tensor_tensor(out=s[:, 5:6], in0=s[:, 4:5], scalar=-0.5, in1=s[:, 1:2],
                                               op0=ALU.mult, op1=ALU.mult).then_inc(rstd_step, 1)
                dve.wait_ge(rstd_step, i[0] * 3 + 2)
                nc.vector.scalar_tensor_tensor(out=s[:, 6:7], in0=s[:, 5:6], scalar=1.5, in1=s[:, 3:4],
                                               op0=ALU.add, op1=ALU.mult).then_inc(rstd_step, 1)
                dve.wait_ge(rstd_step, i[0] * 3 + 3)

            def norm_rows(i, src, gain, dst):
                norm_var(i)
                nc.vector.scalar_tensor_tensor(out=dst, in0=src, scalar=nv[:, i[1], 6:7], in1=gain,
                                               op0=ALU.mult, op1=ALU.mult).then_inc(xn_done, 1)

            def norm_lo(i, cols_, bank):
                dve.wait_ge(uhi_done, i + 1)
                nc.vector.tensor_tensor(u_lo[:, :, cols_], banks(bank, 2).rearrange("p (k t) -> p k t", k=KD),
                                        u_hi[:, :, cols_].bitcast(F32), ALU.subtract).then_inc(ulo_done, 1)

            def split_block(h, b):
                dve.wait_ge(split_hi, h * SP_ + b + 1)
                s, at, _ = raw_of(b)
                nc.vector.tensor_tensor(wp_lo[b % 2][:, :, :], raw[s][:, :, at:at + P],
                                        wp_hi[b % 2][:, :, :].bitcast(F32), ALU.subtract).then_inc(split_lo, 1)

            def split_beside(h, c, s):
                dve.wait_ge(split_hi, h * SP_ + c * 2 + (VB + 3 - s))
                nc.vector.tensor_tensor(wp_lo[s][:, :, :], raw[s][:, :, 0:P], wp_hi[s][:, :, :].bitcast(F32),
                                        ALU.subtract).then_inc(split_lo, 1)

            def split_out(h, jj, s):
                dve.wait_ge(wohi_done, h * 4 + 2 * jj + s + 1)
                rows = slice(4 * s, 4 * s + 4)
                nc.vector.tensor_tensor(wo[jj][1][:, rows, :], wo_raw[jj][:, rows, :],
                                        wo[jj][0][:, rows, :].bitcast(F32), ALU.subtract).then_inc(wolo_done, 1)

            def split_gate_up(h, n, f):
                for s in range(2):
                    dve.wait_ge(split_hi, h * SP_ + n * 4 + (FF0 + 2 * f + s + 1))
                    nc.vector.tensor_tensor(gu_lo[f][:, s, :, :], raw[s][:, :, f * P:f * P + P],
                                            gu_hi[f][:, s, :, :].bitcast(F32), ALU.subtract).then_inc(split_lo, 1)

            start_at_one(dve, glo_done, split_lo, if_lo_done, h_done, gf_done, ulo_done, dn_added, v_kept,
                         state_done, sd_done, hg1_done)
            dve.wait_ge(const_pool, 11)
            dve.wait_ge(bias_loaded, 48)
            nc.vector.tensor_copy(pick[:, :, :], pick_src[:, :, :]).then_inc(const_dve, 1)
            nc.vector.tensor_copy(ident_b[:, :], ident[:, :]).then_inc(const_dve, 1)

            with dve.Fori(0, HALVES) as h:
                dve.wait_ge(gain_loaded, h * 32 + 16)
                dve.sem_inc(dve_passed, 1)
                with dve.Fori(0, TILES // 2) as j:
                    for s in range(2):
                        norm_rows((h * XT + j * 2 + s, s), x_in[s][:, :], gain1[:, :], xn1[s][:, :])
                    for s in range(2):
                        norm_lo(h * XT + j * 2 + s, bass.ds(j * (2 * P) + s * P, P), 2 * s)

                dve.wait_ge(if_hi_done, h + 1)
                nc.vector.tensor_tensor(if_lo[:, :, :].rearrange("p k (a c) -> p k a c", c=32)[:, :, 0:2, 0:HEADS],
                                        if_raw[:, :, :].rearrange("p k (a c) -> p k a c", a=2),
                                        if_hi[:, :, :].rearrange("p k (a c) -> p k a c", c=32)[:, :, 0:2, 0:HEADS]
                                        .bitcast(F32), ALU.subtract).then_inc(if_lo_done, 1)
                split_block(h, 0)

                def per_chunk(tile):
                    return tile[:, :].rearrange("p (c t) -> p c t", t=P)

                def gate_part(b):
                    g = h * 13
                    if b == 0:
                        dve.wait_ge(if_done, h * 2 + 2)
                        nc.vector.tensor_scalar(t0[:, :], ps[0:HEADS, 4:6, :].rearrange("p b n -> p (b n)"),
                                                bias_i[:, 0:1], None, ALU.add).then_inc(gate_dve, 1)
                        nc.vector.tensor_scalar(t1[:, :], ps[32:32 + HEADS, 4:6, :].rearrange("p b n -> p (b n)"),
                                                bias_f[32:32 + HEADS, 0:1], None, ALU.add).then_inc(gate_dve, 1)
                        dve.wait_ge(gate_dve, g + 2)
                        nc.vector.scalar_tensor_tensor(out=t2[:, :], in0=t1[:, :], scalar=-1.0, in1=t1[:, :],
                                                       op0=ALU.mult, op1=ALU.min).then_inc(gate_dve, 1)
                    if b == 2:
                        dve.wait_ge(gate_act, h * 7 + 2)
                        nc.vector.scalar_tensor_tensor(out=t1[:, :], in0=t1[:, :], scalar=0.0, in1=t2[:, :],
                                                       op0=ALU.min, op1=ALU.subtract).then_inc(gate_dve, 1)
                        dve.wait_ge(gate_dve, g + 4)
                        nc.vector.tensor_tensor_scan(t3[:, :], t1[:, :], t0[:, :], m_end[:, 0:1], ALU.add, ALU.max)\
                            .then_inc(gate_dve, 1)
                        nc.vector.tensor_tensor_scan(t4[:, :], not_first[:, :], t1[:, :], 0.0, ALU.mult, ALU.add)\
                            .then_inc(gate_dve, 1)
                        dve.wait_ge(gate_dve, g + 6)
                        dve.wait_ge(prep_done, h * 6 + 5)
                        nc.vector.tensor_tensor(cols[0:HEADS, :], t0[:, :], t4[:, :], ALU.subtract)\
                            .then_inc(gate_dve, 1)
                        dve.wait_ge(gate_dve, g + 7)
                        nc.vector.tensor_tensor(t4[:, :], t4[:, :], t3[:, :], ALU.subtract).then_inc(gate_dve, 1)
                        dve.wait_ge(gate_dve, g + 8)
                        nc.vector.tensor_copy(m_prev[:, 0:1], m_end[:, 0:1]).then_inc(gate_dve, 1)
                        nc.vector.tensor_copy(m_prev[:, 1:TILES], per_chunk(t3)[:, 0:TILES - 1, P - 1])
                        dve.drain()
                        nc.vector.tensor_copy(m_end[:, 0:1], t3[:, TOK - 1:TOK])
                        nc.vector.tensor_tensor(per_chunk(t2), per_chunk(t4),
                                                m_prev[:, :].unsqueeze(2).broadcast_to([HEADS, TILES, P]), ALU.add)\
                            .then_inc(gate_dve, 1)
                        nc.vector.tensor_copy(nm_end[:, :], per_chunk(t4)[:, :, P - 1])
                        dve.drain()
                        nc.vector.tensor_tensor(per_chunk(t0), cols[0:HEADS, :].rearrange("p (c t) -> p c t", t=P),
                                                nm_end[:, :].unsqueeze(2).broadcast_to([HEADS, TILES, P]), ALU.add)\
                            .then_inc(gate_dve, 1)
                    if b == 4:
                        dve.wait_ge(gate_act, h * 7 + 7)
                        nc.vector.tensor_tensor(negm[32:32 + HEADS, :], t4[:, :], negm[0:HEADS, :].bitcast(F32),
                                                ALU.subtract).then_inc(gate_dve, 1)
                        nc.vector.tensor_tensor(wint[32:32 + HEADS, :], t2[:, :], wint[0:HEADS, :].bitcast(F32),
                                                ALU.subtract).then_inc(gate_dve, 1)
                    if b == 6:
                        dve.wait_ge(colt_turned, h + 1)
                        nc.vector.tensor_copy(colt[:, :, :],
                                              ps[:, 6:8, :].rearrange("p b (c n) -> p (b c) n", n=P)[:, :, 0:72])\
                            .then_inc(colt_kept, 1)

                for b in range(QK_BLOCKS):
                    split_block(h, b + 1)
                    gate_part(b)

                dve.wait_ge(prep_done, h * 6 + 6)
                def keep_v(i, head, s, t):
                    dve.wait_ge(vt_done, past(h * 16 + i + 1))
                    where = v1[:, 4 * t:4 * t + 4, :, 0:DV]
                    if isinstance(head, int):
                        where = where[:, :, head, :]
                    else:
                        where = where[:, :, bass.ds(head, 1), :].rearrange("p c a n -> p (c a) n")
                    nc.vector.tensor_copy(where, banks(s).rearrange("p (c n) -> p c n", n=P)).then_inc(v_kept, 1)

                for b in range(VA, VB):
                    split_block(h, b + 1)
                    if b < VB - 1:
                        keep_v(b - VA, b - VA, b % 2, 0)

                def weigh(c):
                    dve.wait_ge(wint_spread, h * 8 + c + 1)
                    nc.vector.tensor_copy(dec[:, :], banks(2).rearrange("p (g t) -> p g t", t=P)[:, :, P - 1])\
                        .then_inc(dec_done, 1)
                    dve.wait_ge(qkc_ready, h * 8 + c + 1)
                    nc.vector.tensor_tensor(qw[:, :, :], banks(2).rearrange("p (g t) -> p g t", t=P), qkc[:, 0:4, :],
                                            ALU.mult).then_inc(qw_done, 1)
                    dve.wait_ge(k_turned, h * 8 + c + 1)
                    nc.vector.tensor_tensor(kw[:, :, :], banks(3).rearrange("p (i n) -> p i n", n=DQK),
                                            colt[:, c, 32:32 + HEADS].unsqueeze(2).broadcast_to([P, HEADS, DQK]),
                                            ALU.mult).then_inc(kw_done, 1)

                def weigh_scores(c, q):
                    dve.wait_ge(s_done, h * 8 + c + 1)
                    dve.wait_ge(dmat_done, h * 64 + c * 8 + 4 * q + 4)
                    heads = dmat[:, 4 * q:4 * q + 4, :].rearrange("p (g a) t -> p g a t", a=2)
                    nc.vector.tensor_tensor(heads, ps[:, 6:8, 2 * q * P:2 * q * P + 2 * P]
                                            .rearrange("p a (g t) -> p g a t", g=2),
                                            heads, ALU.mult).then_inc(sd_done, 1)

                def update_state(c, g):
                    dve.wait_ge(n_done, h * 32 + c * 4 + g + 1)
                    dve.wait_ge(upd_done, h * 32 + c * 4 + g + 1)
                    for a in range(2):
                        r, w = slice(64 * a, 64 * a + 64), slice(VW * a, VW * a + VW)
                        nc.vector.scalar_tensor_tensor(out=state[r, g, w], in0=state[r, g, w],
                                                       scalar=dec[r, g:g + 1], in1=ps[r, 3 if g % 2 == 0 else 2, w],
                                                       op0=ALU.mult, op1=ALU.add).then_inc(state_done, 1)

                def head_scale_a(c):
                    p0 = h * 88 + c * 11
                    dve.wait_ge(num_kept, h * 32 + c * 4 + 4)
                    nc.vector.scalar_tensor_tensor(out=hv[:, 0, :], in0=num[:, :, DV], scalar=-1.0,
                                                   in1=colt[:, c, 64:64 + HEADS], op0=ALU.mult, op1=ALU.max)\
                        .then_inc(post_step, 1)
                    dve.wait_ge(post_step, p0 + 1)
                    nc.vector.tensor_tensor(hv[:, 0, :], hv[:, 0, :], num[:, :, DV], ALU.max).then_inc(post_step, 1)
                    dve.wait_ge(post_step, p0 + 2)
                    nc.vector.reciprocal(hv[:, 1, :], hv[:, 0, :]).then_inc(post_step, 1)
                    dve.wait_ge(sq_done, h * 8 + c + 1)
                    nc.vector.tensor_reduce(hv[:, 2, :], hrow[:, :, :], AX_X, ALU.add).then_inc(post_step, 1)
                    dve.wait_ge(post_step, p0 + 4)
                    nc.vector.tensor_tensor(hv[:, 3, :], hv[:, 1, :], hv[:, 1, :], ALU.mult).then_inc(post_step, 1)
                    dve.wait_ge(post_step, p0 + 5)
                    nc.vector.tensor_tensor(hv[:, 4, :], hv[:, 3, :], hv[:, 2, :], ALU.mult).then_inc(post_step, 1)
                    dve.wait_ge(post_step, p0 + 6)
                    nc.vector.tensor_scalar(hv[:, 5, :], hv[:, 4, :], 1.0 / DV, EPS, ALU.mult, ALU.add)\
                        .then_inc(post_step, 1)

                def head_scale_b(c):
                    p0 = h * 88 + c * 11
                    dve.wait_ge(hrs_done, h * 8 + c + 1)
                    nc.vector.tensor_tensor(hv[:, 8, :], hv[:, 7, :], hv[:, 7, :], ALU.mult).then_inc(post_step, 1)
                    dve.wait_ge(post_step, p0 + 8)
                    nc.vector.scalar_tensor_tensor(out=hv[:, 9, :], in0=hv[:, 8, :], scalar=-0.5, in1=hv[:, 5, :],
                                                   op0=ALU.mult, op1=ALU.mult).then_inc(post_step, 1)
                    dve.wait_ge(post_step, p0 + 9)
                    nc.vector.scalar_tensor_tensor(out=hv[:, 8, :], in0=hv[:, 9, :], scalar=1.5, in1=hv[:, 7, :],
                                                   op0=ALU.add, op1=ALU.mult).then_inc(post_step, 1)
                    dve.wait_ge(post_step, p0 + 10)
                    nc.vector.tensor_tensor(hv[:, 0, :], hv[:, 8, :], hv[:, 1, :], ALU.mult).then_inc(post_step, 1)
                    dve.wait_ge(post_step, p0 + 11)
                    nc.vector.tensor_tensor(hrow[:, :, :], num[:, :, 0:DV],
                                            hv[:, 0, :].unsqueeze(2).broadcast_to([P, HEADS, DV]), ALU.mult)\
                        .then_inc(h_done, 1)

                def chunk(c, v_before, v_beside):
                    weigh(c)
                    if v_before:
                        if isinstance(c, int):
                            keep_v(2 * c + 7, (2 * c + 7) % V_BLOCKS, 1, 0 if c == 0 else 1)
                        else:
                            keep_v(c * 2 + 7, c * 2 - 1, 1, 1)
                    weigh_scores(c, 0)
                    weigh_scores(c, 1)
                    split_beside(h, c, 1)
                    for g in range(4):
                        update_state(c, g)
                    head_scale_a(c)
                    split_beside(h, c, 0)
                    head_scale_b(c)
                    if v_beside:
                        keep_v(c * 2 + 8, c * 2, 0, 1)

                chunk(0, True, True)
                with dve.Fori(1, TILES // 2) as c:
                    chunk(c, True, True)
                chunk(TILES // 2, True, False)
                with dve.Fori(TILES // 2 + 1, TILES) as c:
                    chunk(c, False, False)

                def gate_heads(i, t, sig):
                    return nc.vector.scalar_tensor_tensor(
                        out=hg[:, i, t * NB:t * NB + NB].rearrange("p (c n) -> p c n", n=P),
                        in0=v1[:, 4 * t:4 * t + 4, i, 0:DV], scalar=head_g[:, i:i + 1],
                        in1=sig.rearrange("p (c n) -> p c n", n=P), op0=ALU.mult, op1=ALU.mult)

                def split_gated(i):
                    dve.wait_ge(hghi_done, h * 8 + i + 1)
                    nc.vector.tensor_tensor(u_lo[:, :, i * P:i * P + P], hg[:, :, i * P:i * P + P],
                                            u_hi[:, :, i * P:i * P + P].bitcast(F32), ALU.subtract)\
                        .then_inc(hglo_done, 1)

                for u in range(OB, UNITS):
                    i = u - OB
                    if u + 1 < UNITS:
                        split_block(h, u + 1)
                    if i in (0, 1):
                        if i == 0:
                            dve.wait_ge(ht_kept, past(h * 8 + 8))
                        for head in range(4 * i, 4 * i + 4):
                            dve.wait_ge(o_gated, past(h * 16 + head + 1))
                            gate_heads(head, 0, qk[:, head, 0:NB]).then_inc(hg0_done, 1)
                    if i in (2, 3, 4, 5):
                        split_gated(i - 2)
                    if i >= 6:
                        split_out(h, 0, i - 6)
                    dve.wait_ge(o_gated, past(h * 16 + O_BLOCKS + i + 1))
                    gate_heads(i, 1, banks(i % 2)).then_inc(hg1_done, 1)

                for i in range(TILES // 2, TILES):
                    split_gated(i)
                split_out(h, 1, 0)
                split_out(h, 1, 1)

                def add_out(i, jj):
                    m = jj * TILES + i
                    dve.wait_ge(res_loaded[i // 2], h * 16 + 16)
                    dve.wait_ge(outp_done, past(h * 16 + m + 1))
                    nc.vector.tensor_tensor(res[:, i, jj * NB:jj * NB + NB], banks((m + 2) % 4),
                                            res[:, i, jj * NB:jj * NB + NB], ALU.add).then_inc(res_added, 1)

                for i in range(TILES):
                    add_out(i, 0)
                split_gate_up(h, 0, 0)
                dve.wait_ge(gain_loaded, h * 32 + 32)
                for i in range(TILES):
                    add_out(i, 1)
                    norm_rows((h * XT + TILES + i, i % 2), res[:, i, :], gain2[:, :], xn2[i % 2][:, :])
                    if i >= 2:
                        norm_lo(h * XT + TILES + i - 2, slice((i - 2) * P, (i - 1) * P), 4 + 2 * (i % 2))
                for i in range(TILES - 2, TILES):
                    norm_lo(h * XT + TILES + i, slice(i * P, i * P + P), 4 + 2 * (i % 2))

                def hidden(n, o):
                    dve.wait_ge(silu_done, h * GU + n * 4 + o + 1)
                    nc.vector.tensor_tensor(sg[:, o % 2, :], banks(2 * (o % 2) + 1), sg[:, o % 2, :], ALU.mult)\
                        .then_inc(gf_done, 1)

                def hidden_lo(n, o):
                    dve.wait_ge(ghi_done, h * GU + n * 4 + o + 1)
                    nc.vector.tensor_tensor(g_lo[o % 2][o // 2][:, :], sg[:, o % 2, :],
                                            g_hi[o % 2][o // 2][:, :].bitcast(F32), ALU.subtract)\
                        .then_inc(glo_done, 1)

                def add_down(n, t, lo, hi):
                    for q in range(lo, hi):
                        i, jj = 4 * t + q // 2, q % 2
                        dve.wait_ge(dn_done, past(h * DN + n * 16 + (8 * t + q + 1)))
                        nc.vector.tensor_tensor(res[:, i, jj * NB:jj * NB + NB], banks(4 + q % 4),
                                                res[:, i, jj * NB:jj * NB + NB], ALU.add).then_inc(dn_added, 1)

                def ffn_group(n, is_first, is_last):
                    split_gate_up(h, n, 1)
                    hidden(n, 0)
                    hidden_lo(n, 0)
                    if not is_first:
                        add_down(n - 1, 1, 0, 8)
                    for f in range(2):
                        dve.wait_ge(dn_hi_done, h * (2 * GROUPS) + n * 2 + f + 1)
                        nc.vector.tensor_tensor(dn_lo[:, f, :], dn_raw[:, f, :], dn_hi[:, f, :].bitcast(F32),
                                                ALU.subtract).then_inc(dn_lo_done, 1)
                    hidden(n, 1)
                    hidden_lo(n, 1)
                    hidden(n, 2)
                    hidden_lo(n, 2)
                    add_down(n, 0, 0, 4)
                    if not is_last:
                        split_gate_up(h, n + 1, 0)
                    add_down(n, 0, 4, 8)
                    hidden(n, 3)
                    hidden_lo(n, 3)

                ffn_group(0, True, False)
                with dve.Fori(1, GROUPS - 1) as n:
                    ffn_group(n, False, False)
                ffn_group(GROUPS - 1, False, True)
                add_down(GROUPS - 1, 1, 0, 8)

        @block.tensor
        def _(pe):
            def three_passes(out_, steps):
                n = len(steps)
                for k, (wh, wl, mh, ml) in enumerate(steps):
                    pe.matmul(out_, wh, ml, start=(k == 0), stop=False)
                    pe.matmul(out_, wh, mh, start=False, stop=False)
                    last = pe.matmul(out_, wl, mh, start=False, stop=(k == n - 1))
                return last

            def turn_rows(src, bank):
                for k in range(KD):
                    last = pe.transpose(ps[:, bank + k // 4, (k % 4) * P:(k % 4) * P + P], src[:, k * P:k * P + P],
                                        ident[:, :])
                last.then_inc(xt_done, 1)

            def project(s, bank, t, k0=0, k1=KD):
                now = slice(t * NB, t * NB + NB)
                for k in range(k0, k1):
                    wh, wl = wp_hi[s][:, k, :], wp_lo[s][:, k, :]
                    pe.matmul(banks(bank), wh, u_lo[:, k, now], start=(k == 0), stop=False, skip_group_check=True)
                    pe.matmul(banks(bank), wh, u_hi[:, k, now], start=False, stop=False, skip_group_check=True)
                    last = pe.matmul(banks(bank), wl, u_hi[:, k, now], start=False, stop=(k == KD - 1),
                                     skip_group_check=True)
                if k1 == KD:
                    last.then_inc(proj_done, 1)

            start_at_one(pe, outp_done, gu_done, h_turned, proj_done, xt_done, dn_done, vt_done)
            pe.wait_ge(const_dve, 2)

            with pe.Fori(0, HALVES) as h:
                pe.wait_ge(gf_done, past(h * GU))
                pe.sem_inc(pe_passed, 1)
                with pe.Fori(0, TILES // 2) as j:
                    for s in range(2):
                        pe.wait_ge(xn_done, h * XT + j * 2 + s + 1)
                        pe.wait_ge(ulo_done, past(h * XT + j * 2))
                        turn_rows(xn1[s], 2 * s)

                pe.wait_ge(if_lo_done, past(h + 1))
                pe.wait_ge(ulo_done, past(h * XT + TILES))
                pe.wait_ge(dn_added, past(h * DN))
                for t in range(TBS):
                    three_passes(banks(4 + t),
                                 [(if_hi[:, k, :], if_lo[:, k, :], u_hi[:, k, t * NB:t * NB + NB],
                                   u_lo[:, k, t * NB:t * NB + NB]) for k in range(KD)]).then_inc(if_done, 1)

                with pe.Fori(0, QK_BLOCKS // 2) as j:
                    for s in range(2):
                        pe.wait_ge(split_lo, past(h * SP_ + j * 2 + s + 1))
                        pe.wait_ge(qk_kept, past(h * 16 + j * 4))
                        for t in range(TBS):
                            project(s, 2 * s + t, t)

                pe.wait_ge(gate_act, h * 7 + 7)
                for c in range(TILES):
                    last = pe.transpose(ps[:, 6 + c // 4, (c % 4) * P:(c % 4) * P + P], cols[:, c * P:c * P + P],
                                        ident[:, :])
                last.then_inc(colt_turned, 1)

                pe.wait_ge(qk_kept, past(h * 16 + 16))

                def turn_v(i, s):
                    pe.wait_ge(v_staged, past(h * 16 + i + 1))
                    for q in range(4):
                        last = pe.transpose(ps[:, s, q * P:q * P + P], v_st[:, s, q * P:q * P + P], ident[:, :])
                    last.then_inc(vt_done, 1)

                def v_unit(j, s, is_first):
                    pe.wait_ge(split_lo, past(h * SP_ + j * 2 + (VA + s + 1)))
                    if not is_first:
                        pe.wait_ge(v_kept, past(h * 16 + j * 2 + s - 1))
                    project(s, s, 0, 0, KD // 2)
                    if s == 1 or not is_first:
                        turn_v(j * 2 + s - 1, 1 - s)
                    project(s, s, 0, KD // 2, KD)

                v_unit(0, 0, True)
                v_unit(0, 1, True)
                with pe.Fori(1, V_BLOCKS // 2) as j:
                    v_unit(j, 0, False)
                    v_unit(j, 1, False)

                def spread(c):
                    now = bass.ds(c * P, P)
                    pe.wait_ge(state_done, past(h * 64 + c * 8))
                    for g in range(4):
                        pair = pick[:, :, :].rearrange("p h c -> p (h c)")[:, 2 * g * P + DQK:2 * g * P + DQK + P]
                        last = pe.matmul(ps[:, 2, g * P:g * P + P], pair, wint[:, now],
                                         start=(g == 0), stop=(g == 3), skip_group_check=True)
                    last.then_inc(wint_spread, 1)
                    for half in range(2):
                        pe.matmul(banks(4 + half), ident_b[:, :], mask[:, :, :].rearrange("p a t -> p (a t)"),
                                  start=True, stop=False, skip_group_check=True)
                        for i in range(4):
                            last = pe.matmul(ps[:, 4 + half, i * P:i * P + P], pick[:, 4 * half + i, :], negm[:, now],
                                             start=False, stop=(i == 3), skip_group_check=True)
                    last.then_inc(darg_done, 1)
                    pe.wait_ge(qkc_ready, h * 8 + c + 1)
                    for g in range(4):
                        last = pe.transpose(ps[:, 3, g * P:g * P + P], qkc[:, 4 + g, :], ident[:, :])
                    last.then_inc(k_turned, 1)

                def scores(c, is_first):
                    if not is_first:
                        pe.wait_ge(num_kept, h * 32 + c * 4)
                    for g in range(4):
                        for a in range(2):
                            r = slice(64 * a, 64 * a + 64)
                            last = pe.matmul(ps[:, 6 + a, g * P:g * P + P], qkc[r, 4 + g, :],
                                             qkc[r, g, :], start=True, stop=True, skip_group_check=True)
                    last.then_inc(s_done, 1)

                def state_sum(c, g):
                    if g == 0:
                        pe.wait_ge(kw_done, h * 8 + c + 1)
                    elif g == 1:
                        pe.wait_ge(qw_done, h * 8 + c + 1)
                        pe.wait_ge(dec_done, h * 8 + c + 1)
                    else:
                        pe.wait_ge(state_done, past(h * 64 + c * 8 + 2 * (g - 1)))
                    pe.matmul(ps[:, 3 if g % 2 == 0 else 2, 0:2 * VW],
                              kw[:, 2 * g:2 * g + 2, :], v1[:, c, 2 * g:2 * g + 2, :],
                              start=True, stop=True).then_inc(upd_done, 1)

                def outputs(c, g):
                    if g >= 2:
                        pe.wait_ge(num_kept, h * 32 + c * 4 + g - 1)
                    else:
                        pe.wait_ge(sd_done, past(h * 16 + c * 2 + 2))
                    pe.matmul(ps[:, 6 + g % 2, 0:2 * VW], qw[:, g, :], state[:, g, :], start=True, stop=False,
                              skip_group_check=True)
                    for a in range(2):
                        last = pe.matmul(ps[:, 6 + g % 2, a * VW:a * VW + VW], dmat[:, 2 * g + a, :],
                                         v1[:, c, 2 * g + a, :], start=False, stop=(a == 1), skip_group_check=True)
                    last.then_inc(n_done, 1)

                def turn_heads(c):
                    pe.wait_ge(h_done, past(h * 8 + c + 1))
                    for i in range(HEADS):
                        last = pe.transpose(ps[:, 4 + i // 4, (i % 4) * P:(i % 4) * P + P], hrow[:, i, :],
                                            ident[:, :])
                    last.then_inc(h_turned, 1)

                def beside(c, s, k0, k1, v_before, v_beside):
                    if k0 == 0:
                        pe.wait_ge(split_lo, past(h * SP_ + c * 2 + (VB + s + 1)))
                        if v_before:
                            pe.wait_ge(v_kept, past(h * 16 + c * 2 + (V_BLOCKS - 1 + s)))
                        else:
                            pe.wait_ge(o_gated, past(h * 16 + c * 2 - 9 + s))
                    project(s, s, 1 if v_beside else 0, k0, k1)

                def chunk(c, is_first, v_before, v_beside):
                    if not is_first:
                        pe.wait_ge(ht_kept, past(h * 8 + c - 1))
                    spread(c)
                    scores(c, is_first)
                    if v_before:
                        turn_v(c * 2 + (V_BLOCKS - 1), 1)
                    if not isinstance(c, int):
                        beside(c, 0, 0, 3, v_before, v_beside)
                        state_sum(c, 0)
                        state_sum(c, 1)
                    else:
                        beside(c, 0, 0, 3, v_before, v_beside)
                        pe.wait_ge(v_kept, past(h * 16 + c * 2 + V_BLOCKS))
                        state_sum(c, 0)
                        state_sum(c, 1)
                    outputs(c, 0)
                    outputs(c, 1)
                    if not is_first:
                        pe.wait_ge(dmat_done, h * 64 + c * 8 + 8)
                        turn_heads(c - 1)
                    beside(c, 0, 3, 5, v_before, v_beside)
                    state_sum(c, 2)
                    outputs(c, 2)
                    state_sum(c, 3)
                    outputs(c, 3)
                    beside(c, 0, 5, KD, v_before, v_beside)
                    beside(c, 1, 0, 4, v_before, v_beside)
                    if v_beside:
                        turn_v(c * 2 + V_BLOCKS, 0)
                    beside(c, 1, 4, KD, v_before, v_beside)

                pe.wait_ge(gate_dve, h * 13 + 13)
                pe.wait_ge(colt_kept, h + 1)
                chunk(0, True, True, True)
                with pe.Fori(1, TILES // 2) as c:
                    chunk(c, False, True, True)
                chunk(TILES // 2, False, True, False)
                with pe.Fori(TILES // 2 + 1, TILES) as c:
                    chunk(c, False, False, False)
                pe.wait_ge(ht_kept, past(h * 8 + TILES - 1))
                turn_heads(TILES - 1)

                def o_unit(j, s, is_first):
                    pe.wait_ge(split_lo, past(h * SP_ + j * 2 + (OB + s + 1)))
                    if is_first:
                        pe.wait_ge(o_gated, past(h * 16 + O_BLOCKS - 1 + s))
                    else:
                        pe.wait_ge(hg1_done, past(h * 8 + j * 2 - 1 + s))
                    project(s, s, 1)

                o_unit(0, 0, True)
                o_unit(0, 1, True)
                with pe.Fori(1, O_BLOCKS // 2) as j:
                    o_unit(j, 0, False)
                    o_unit(j, 1, False)

                def out_group(i, jj):
                    m = jj * TILES + i
                    rows = slice(i * P, i * P + P)
                    if jj == 0:
                        pe.wait_ge(hglo_done, h * 8 + i + 1)
                    if m >= 4:
                        pe.wait_ge(res_added, h * 16 + m - 3)
                    elif m >= 2:
                        pe.wait_ge(hg1_done, past(h * 8 + 8))
                    three_passes(banks((m + 2) % 4), [(u_hi[:, k, rows], u_lo[:, k, rows], wo[jj][0][:, k, :],
                                                 wo[jj][1][:, k, :]) for k in range(KD)]).then_inc(outp_done, 1)

                def turn_norm2(i):
                    pe.wait_ge(xn_done, h * XT + TILES + i + 1)
                    if i >= 2:
                        pe.wait_ge(ulo_done, past(h * XT + TILES + i - 1))
                    turn_rows(xn2[i % 2], 4 + 2 * (i % 2))

                pe.wait_ge(state_done, past(h * 64 + 64))
                pe.wait_ge(ht_kept, past(h * 8 + 8))
                pe.wait_ge(wolo_done, h * 4 + 2)
                for i in range(TILES):
                    out_group(i, 0)
                pe.wait_ge(wolo_done, h * 4 + 4)
                for i in range(TILES):
                    out_group(i, 1)
                    if i >= 2:
                        turn_norm2(i - 2)

                def gate_up(n, o):
                    f, t = o % 2, o // 2
                    pe.wait_ge(split_lo, past(h * SP_ + n * 4 + (FF0 + 2 * f + 2)))
                    pe.wait_ge(gf_done, past(h * GU + n * 4 + o - 1 if o >= 2 else h * GU + n * 4))
                    for s in range(2):
                        last = three_passes(banks(2 * (o % 2) + s),
                                            [(gu_hi[f][:, s, k, :], gu_lo[f][:, s, k, :],
                                              u_hi[:, k, t * NB:t * NB + NB], u_lo[:, k, t * NB:t * NB + NB])
                                             for k in range(KD)])
                    last.then_inc(gu_done, 1)

                def down(n, t):
                    pe.wait_ge(glo_done, past(h * GU + n * 4 + (2 * t + 2)))
                    pe.wait_ge(dn_lo_done, h * (2 * GROUPS) + n * 2 + 2)
                    for q in range(8):
                        i, jj = q // 2, q % 2
                        c = slice(i * P, i * P + P)
                        w = slice(jj * NB, jj * NB + NB)
                        if q >= 4:
                            pe.wait_ge(dn_added, past(h * DN + n * 16 + (8 * t + q - 3)))
                        elif q == 0:
                            pe.wait_ge(dn_added, past(h * DN + n * 16 + 8 * t))
                        three_passes(banks(4 + q % 4), [(g_hi[f][t][:, c], g_lo[f][t][:, c], dn_hi[:, f, w],
                                                         dn_lo[:, f, w]) for f in range(2)]).then_inc(dn_done, 1)

                def ffn_group(n, is_first):
                    gate_up(n, 0)
                    if is_first:
                        turn_norm2(TILES - 2)
                        turn_norm2(TILES - 1)
                    else:
                        down(n - 1, 1)
                    gate_up(n, 1)
                    if is_first:
                        pe.wait_ge(ulo_done, past(h * XT + XT))
                    gate_up(n, 2)
                    down(n, 0)
                    gate_up(n, 3)

                pe.wait_ge(res_added, h * 16 + 16)
                pe.wait_ge(ulo_done, past(h * XT + TILES + 4))
                ffn_group(0, True)
                with pe.Fori(1, GROUPS) as n:
                    ffn_group(n, False)
                down(GROUPS - 1, 1)


_INS = ['x', 'mix_norm_g', 'ffn_norm_g', 'ffn_w_gate', 'ffn_w_up', 'ffn_w_down', 'ml_w_in', 'ml_b_if', 'ml_norm_g',
        'ml_w_out']
_OUTS = [((1, SEQ, D), 'float32')]


def kernel(**inputs):
    import numpy as _np
    import concourse.bacc as _bacc
    from concourse import mybir as _mybir
    from concourse.bass_utils import run_bass_kernel_spmd as _run

    nc = _bacc.Bacc("TRN2", target_bir_lowering=False, num_devices=1)
    arrays, args = {}, []
    for name in _INS:
        a = _np.ascontiguousarray(inputs[name])
        arrays[f"in_{name}_dram"] = a
        args.append(nc.dram_tensor(f"in_{name}_dram", a.shape, _mybir.dt.from_np(a.dtype), kind="ExternalInput").ap())
    for i, (shape, dtype) in enumerate(_OUTS):
        dt = _mybir.dt.from_np(_np.dtype(dtype))
        args.append(nc.dram_tensor(f"out_{i}_dram", shape, dt, kind="ExternalOutput").ap())
    mlstm_layer(nc, *args)
    r = _run(nc, [arrays], core_ids=[0])
    got = tuple(r.results[0][f"out_{i}_dram"] for i in range(len(_OUTS)))
    return got[0]
```

```python
from contextlib import ExitStack

import concourse.bass as bass
from concourse import mybir

F32 = mybir.dt.float32
F32R = mybir.dt.float32r
BF16 = mybir.dt.bfloat16
ALU = mybir.AluOpType
ACT = mybir.ActivationFunctionType
AX_X = mybir.AxisListType.X

P = 128
D = 1024
SEQ = 2048
HEADS = 8
DV = D // HEADS
DQK = D // (2 * HEADS)
FF = 2816
EPS = 1e-6
KD = D // P
HALVES = 2
TOK = SEQ // HALVES
TILES = TOK // P
NB = 512
TBS = TOK // NB
VW = DV + 1
QK_BLOCKS = 8
V_BLOCKS = 8
O_BLOCKS = 8
BLOCKS = QK_BLOCKS + V_BLOCKS + O_BLOCKS
VA, VB, OA, OB, UNITS = 8, 16, 24, 32, 40
GROUPS = FF // (2 * P)
MASKED = -1e30

XT = 2 * TILES
PJ = TBS * BLOCKS
SP_ = UNITS + 4 * GROUPS
GU = 4 * GROUPS
DN = 16 * GROUPS
RAW_VB = VB // 4
RAW_OB = RAW_VB + (OB - VB) // 2
RAW_FF = RAW_OB + (UNITS - OB) // 4
RAW = RAW_FF + GROUPS
FF0 = UNITS


def groups_until(u):
    return 3 if u == 1 else TBS * u if u <= QK_BLOCKS else QK_BLOCKS + u


def raw_of(u):
    if VB <= u < OB:
        return u % 2, 0, RAW_VB + (u - VB) // 2
    first, pair = (RAW_OB, (u - OB) // 2) if u >= OB else (0, u // 2)
    return pair % 2, (u % 2) * P, first + pair // 2


def mlstm_layer(nc, x, mix_norm_g, ffn_norm_g, w_gate, w_up, w_down, w_in, b_if, norm_g, w_out, out):
    x_rows = x[0].rearrange("(t p) d -> t p d", p=P)
    out_rows = out[0].rearrange("(t p) d -> t p d", p=P)
    w_in_k = w_in[0].rearrange("(k p) n -> p k n", p=P)
    w_out_k = w_out[0].rearrange("(k p) n -> p k n", p=P)
    w_gate_k = w_gate[0].rearrange("(k p) n -> p k n", p=P)
    w_up_k = w_up[0].rearrange("(k p) n -> p k n", p=P)
    w_down_k = w_down[0].rearrange("(k p) n -> k p n", p=P)

    with ExitStack() as ctx:
        def sem(name):
            return ctx.enter_context(nc.semaphore(name))

        base = -(-nc.sbuf_base // 32) * 32
        top = [base]

        def region(nbytes):
            at = top[0]
            top[0] += -(-nbytes // 32) * 32
            return at

        def place(name, at, shape, dt):
            return nc.alloc_sbuf_tensor_at(name, shape, dt, offset=at)

        def small(name, shape, dt=F32):
            n = 1
            for s in shape[1:]:
                n *= s
            return place(name, region(n * (2 if dt == BF16 else 4)), shape, dt)

        KB = 1024
        r_u = region(64 * KB)
        u_hi = place("u_hi", r_u, [P, KD, TOK], F32R)
        u_lo = place("u_lo", r_u + 32 * KB, [P, KD, TOK], F32R)

        r_v = region(TILES * HEADS * VW * 4)
        v1 = place("v1", r_v, [P, TILES, HEADS, VW], F32)
        res = place("res", r_v, [P, TILES, D], F32)

        r_q = region(32 * KB)
        qk = place("qk", r_q, [P, QK_BLOCKS, TOK], F32)
        hg = place("hg", r_q, [P, KD, TOK], F32)
        wo1 = [place("wo1_hi", r_q, [P, KD, NB], F32R), place("wo1_lo", r_q + 16 * KB, [P, KD, NB], F32R)]
        dn_hi = place("dn_hi", r_q, [P, 2, D], F32R)
        dn_lo = place("dn_lo", r_q + 8 * KB, [P, 2, D], F32R)
        dn_raw = place("dn_raw", r_q + 16 * KB, [P, 2, D], F32)
        sg = place("sg", r_q + 24 * KB, [P, 2, NB], F32)
        x_in = [place(f"x_in{s}", r_q + (28 - 4 * s) * KB, [P, D], F32) for s in range(4)]

        r_a = region(16 * KB)
        wp_hi = [place(f"wp_hi{s}", r_a + 8 * KB * s, [P, KD, P], F32R) for s in range(2)]
        wp_lo = [place(f"wp_lo{s}", r_a + 8 * KB * s + 4 * KB, [P, KD, P], F32R) for s in range(2)]
        gain2 = place("gain2", r_a, [P, D], F32)
        xn2 = [place(f"xn2_{s}", r_a + 4 * KB * (s + 1), [P, D], F32) for s in range(2)]
        g_hi = [[place(f"g_hi{f}{t}", r_a + 2 * KB * (2 * f + t), [P, NB], F32R) for t in range(2)] for f in range(2)]
        g_lo = [[place(f"g_lo{f}{t}", r_a + 2 * KB * (4 + 2 * f + t), [P, NB], F32R) for t in range(2)] for f in range(2)]

        r_b = region(16 * KB)
        raw = [place(f"raw{s}", r_b + 8 * KB * s, [P, KD, 2 * P], F32) for s in range(2)]

        r_c = region(28 * KB + HEADS * VW * 4)
        cols = place("cols", r_c, [P, TOK], F32)
        negm = place("negm", r_c + 4 * KB, [P, TOK], F32R)
        wint = place("wint", r_c + 8 * KB, [P, TOK], F32R)
        t0 = place("t0", r_c + 12 * KB, [HEADS, TOK], F32)
        t1 = place("t1", r_c + 16 * KB, [HEADS, TOK], F32)
        t2 = place("t2", r_c + 20 * KB, [HEADS, TOK], F32)
        t3 = place("t3", r_c + 24 * KB, [HEADS, TOK], F32)
        t4 = place("t4", r_c + 28 * KB, [HEADS, TOK], F32)
        if_w = place("if_w", r_c + 12 * KB, [P, KD, P], F32R)
        xn1 = [place(f"xn1_{s}", r_c + (20 + 4 * s) * KB, [P, D], F32) for s in range(2)]
        gain1 = place("gain1", r_c + 28 * KB, [P, D], F32)
        v_st = place("v_st", r_c, [P, 2, NB], F32)
        dmat = place("dmat", r_c + 12 * KB, [P, HEADS, P], F32)
        hrow = place("hrow", r_c + 16 * KB, [P, HEADS, DV], F32)
        qkc = place("qkc", r_c + 20 * KB, [P, QK_BLOCKS, P], F32)
        kw = place("kw", r_c + 24 * KB, [P, HEADS, DQK], F32)
        qw = place("qw", r_c + 26 * KB, [P, 4, P], F32)
        num = place("num", r_c + 28 * KB, [P, HEADS, VW], F32)
        wo0 = [place("wo0_hi", r_c, [P, KD, NB], F32R), place("wo0_lo", r_c + 16 * KB, [P, KD, NB], F32R)]
        gu_hi = [place(f"gu_hi{f}", r_c + 16 * KB * f, [P, 2, KD, P], F32R) for f in range(2)]
        gu_lo = [place(f"gu_lo{f}", r_c + 16 * KB * f + 8 * KB, [P, 2, KD, P], F32R) for f in range(2)]
        wo = [wo0, wo1]
        wo_raw = [place("wo0_raw", r_c + 16 * KB, [P, KD, NB], F32), place("wo1_raw", r_q + 16 * KB, [P, KD, NB], F32)]

        state = small("state", [P, 4, VW])
        colt = small("colt", [P, TILES, 72])
        ident = small("ident", [P, P])
        ident_b = small("ident_b", [P, P], BF16)
        pick = small("pick", [P, HEADS, P], F32R)
        mask = small("mask", [P, 4, P], BF16)
        not_first = small("not_first", [HEADS, TOK], BF16)
        if_raw = small("if_raw", [P, KD, 2 * HEADS])
        bias = small("bias", [P, 1])
        head_g = small("head_g", [P, HEADS])
        m_end = small("m_end", [HEADS, 1])
        m_prev = small("m_prev", [HEADS, TILES])
        nm_end = small("nm_end", [HEADS, TILES])
        dec = small("dec", [P, 4])
        nv = small("nv", [P, 2, 8])
        eps = small("eps", [P, 1])
        hv = small("hv", [P, 10, HEADS])
        assert top[0] <= nc.sbuf_usable_end, (top[0], nc.sbuf_usable_end)
        pick_src = place("pick_src", r_q, [P, HEADS, P], F32)

        ps = ctx.enter_context(nc.psum_tensor("ps", [P, 8, NB], F32))

        def banks(b, n=1):
            return ps[:, b:b + n, :].rearrange("p b n -> p (b n)")

        EPS_SET, IDENT_SET, PICK_SET, CONST_SET = 1, 3, 6, 12

        x_loaded = [sem(f"x_loaded{s}") for s in range(4)]
        gain_loaded = sem("gain_loaded")
        if_loaded = sem("if_loaded")
        raw_loaded = [sem(f"raw_loaded{s}") for s in range(2)]
        wo_loaded = [sem(f"wo_loaded{s}") for s in range(2)]
        dn_loaded = [sem(f"dn_loaded{s}") for s in range(2)]
        res_loaded = [sem(f"res_loaded{s}") for s in range(4)]
        bias_loaded = sem("bias_loaded")
        out_stored = sem("out_stored")
        const_pool = sem("const_pool")
        const_dve = sem("const_dve")
        prep_done = sem("prep_done")
        pool_passed = sem("pool_passed")
        dve_passed = sem("dve_passed")
        ssq_done = sem("ssq_done")
        var_done = sem("var_done")
        lnv_done = sem("lnv_done")
        rstd0_done = sem("rstd0_done")
        rstd_step = sem("rstd_step")
        xn_done = sem("xn_done")
        xt_done = sem("xt_done")
        uhi_done = sem("uhi_done")
        ulo_done = sem("ulo_done")
        split_hi = sem("split_hi")
        split_lo = sem("split_lo")
        if_hi_done = sem("if_hi_done")
        if_lo_done = sem("if_lo_done")
        dn_hi_done = sem("dn_hi_done")
        dn_lo_done = sem("dn_lo_done")
        if_done = sem("if_done")
        proj_done = sem("proj_done")
        qk_kept = sem("qk_kept")
        v_staged = sem("v_staged")
        vt_done = sem("vt_done")
        v_kept = sem("v_kept")
        gate_dve = sem("gate_dve")
        gate_act = sem("gate_act")
        colt_turned = sem("colt_turned")
        colt_kept = sem("colt_kept")
        qkc_ready = sem("qkc_ready")
        wint_spread = sem("wint_spread")
        darg_done = sem("darg_done")
        k_turned = sem("k_turned")
        dmat_done = sem("dmat_done")
        dec_done = sem("dec_done")
        qw_done = sem("qw_done")
        kw_done = sem("kw_done")
        s_done = sem("s_done")
        sd_done = sem("sd_done")
        upd_done = sem("upd_done")
        n_done = sem("n_done")
        num_kept = sem("num_kept")
        state_done = sem("state_done")
        sq_done = sem("sq_done")
        post_step = sem("post_step")
        hln_done = sem("hln_done")
        hrs_done = sem("hrs_done")
        h_done = sem("h_done")
        h_turned = sem("h_turned")
        ht_kept = sem("ht_kept")
        o_step = sem("o_step")
        o_gated = sem("o_gated")
        hg0_done = sem("hg0_done")
        hg1_done = sem("hg1_done")
        wohi_done = sem("wohi_done")
        wolo_done = sem("wolo_done")
        hghi_done = sem("hghi_done")
        hglo_done = sem("hglo_done")
        outp_done = sem("outp_done")
        res_added = sem("res_added")
        gu_done = sem("gu_done")
        silu_done = sem("silu_done")
        gf_done = sem("gf_done")
        ghi_done = sem("ghi_done")
        glo_done = sem("glo_done")
        dn_done = sem("dn_done")
        dn_added = sem("dn_added")

        def past(count):
            return count + 1

        def start_at_one(engine, *counters):
            for counter in counters:
                engine.sem_inc(counter, 1)

        block = ctx.enter_context(nc.Block())

        def head_values(c):
            return v1[:, c, :, 0:DV]

        @block.sync
        def _(sp):
            def load_out(jj):
                for s in range(2):
                    rows = slice(4 * s, 4 * s + 4)
                    sp.dma_start(wo_raw[jj][:, rows, :], w_out_k[:, rows, NB * jj:NB * jj + NB])\
                        .then_inc(wo_loaded[s], 16)

            def load_pair(p, s):
                sp.dma_start(raw[s][:, :, :], w_in_k[:, :, bass.ds(p * 2 * P, 2 * P)]).then_inc(raw_loaded[s], 16)

            def load_down(n, f):
                sp.dma_start(dn_raw[:, f, :], w_down_k[2 * n + f]).then_inc(dn_loaded[f], 16)

            def load_gate_up(n, s):
                w = w_gate_k if s == 0 else w_up_k
                sp.dma_start(raw[s][:, :, :], w[:, :, bass.ds(n * 2 * P, 2 * P)]).then_inc(raw_loaded[s], 16)

            with sp.Fori(0, HALVES) as h:
                def load_x(i):
                    sp.dma_start(x_in[i % 4][:, :], x_rows[h * TILES + i]).then_inc(x_loaded[i % 4], 16)

                sp.wait_ge(outp_done, past(h * 16))
                load_x(0)
                sp.wait_ge(gu_done, past(h * GU))
                sp.dma_start(gain1[:, :], mix_norm_g[0:1, :].partition_broadcast(P)).then_inc(gain_loaded, 16)
                sp.wait_ge(glo_done, past(h * GU))
                load_x(1)
                load_x(2)
                load_x(3)
                sp.wait_ge(split_lo, past(h * SP_))
                load_pair(0, 0)
                for i in range(4, TILES):
                    sp.wait_ge(xn_done, h * XT + i - 3)
                    load_x(i)
                sp.wait_ge(if_lo_done, past(h))
                sp.dma_start(if_raw[:, :, :], w_in_k[:, :, BLOCKS * P:BLOCKS * P + 2 * HEADS]).then_inc(if_loaded, 16)
                load_pair(1, 1)
                with sp.Fori(1, VB // 4) as j:
                    for s in range(2):
                        sp.wait_ge(split_lo, past(h * SP_ + 4 * j + 2 * s - 2))
                        load_pair(2 * j + s, s)
                with sp.Fori(0, TILES) as c:
                    for s in range(2):
                        sp.wait_ge(split_lo, past(h * SP_ + 2 * c + (VB - 1 + s)))
                        sp.dma_start(raw[s][:, :, 0:P], w_in_k[:, :, bass.ds((QK_BLOCKS + s) * P + c * (2 * P), P)])\
                            .then_inc(raw_loaded[s], 16)
                for p in range(2):
                    sp.wait_ge(split_lo, past(h * SP_ + OB - 1 + p))
                    load_pair((BLOCKS - O_BLOCKS) // 2 + p, p)
                sp.wait_ge(h_turned, past(h * 8 + 8))
                load_out(0)
                for p in range(2, 4):
                    sp.wait_ge(split_lo, past(h * SP_ + OB + 2 * p - 2))
                    load_pair((BLOCKS - O_BLOCKS) // 2 + p, p % 2)
                for s in range(2):
                    sp.wait_ge(split_lo, past(h * SP_ + UNITS - 2 + 2 * s))
                    load_gate_up(0, s)
                sp.wait_ge(proj_done, past(h * PJ + PJ))
                sp.dma_start(gain2[:, :], ffn_norm_g[0:1, :].partition_broadcast(P)).then_inc(gain_loaded, 16)
                sp.wait_ge(hglo_done, h * 8 + 8)
                load_out(1)
                sp.wait_ge(outp_done, past(h * 16 + 16))
                load_down(0, 0)
                load_down(0, 1)
                with sp.Fori(1, GROUPS) as n:
                    for s in range(2):
                        sp.wait_ge(split_lo, past(h * SP_ + n * 4 + (FF0 - 1 + s)))
                        load_gate_up(n, s)
                    for f in range(2):
                        sp.wait_ge(dn_lo_done, h * (2 * GROUPS) + n * 2 + (f - 1))
                        load_down(n, f)

        @block.gpsimd
        def _(pool):
            nc.gpsimd.memset(eps[:, :], EPS).then_inc(const_pool, 1)
            nc.gpsimd.memset(ident[:, :], 0.0).then_inc(const_pool, 1)
            pool.wait_ge(const_pool, 2)
            nc.gpsimd.affine_select(out=ident[:, :], in_=ident[:, :], compare_op=ALU.not_equal, fill=1.0, base=0,
                                    pattern=[[-1, P]], channel_multiplier=1).then_inc(const_pool, 1)
            nc.gpsimd.memset(pick_src[:, :, :], 0.0).then_inc(const_pool, 1)
            for row in (0, 32):
                pool.wait_ge(const_pool, 4 + (1 if row else 0))
                nc.gpsimd.affine_select(out=pick_src[:, :, :], in_=pick_src[:, :, :], compare_op=ALU.not_equal,
                                        fill=1.0, base=-row, pattern=[[-1, HEADS], [0, P]], channel_multiplier=1)\
                    .then_inc(const_pool, 1)
            nc.gpsimd.memset(mask[:, :, :], 0.0).then_inc(const_pool, 1)
            nc.gpsimd.memset(not_first[:, :], 1.0).then_inc(const_pool, 1)
            nc.gpsimd.memset(m_end[:, :], 0.0).then_inc(const_pool, 1)
            nc.gpsimd.memset(state[:, :, :], 0.0).then_inc(const_pool, 1)
            pool.wait_ge(const_pool, 10)
            nc.gpsimd.affine_select(out=mask[:, :, :], in_=mask[:, :, :], compare_op=ALU.is_ge, fill=MASKED, base=0,
                                    pattern=[[0, 4], [1, P]], channel_multiplier=-1).then_inc(const_pool, 1)
            nc.gpsimd.memset(not_first[:, :].rearrange("p (c t) -> p c t", t=P)[:, :, 0:1], 0.0)\
                .then_inc(const_pool, 1)

            def clear_rows():
                nc.gpsimd.memset(if_w[:, :, :].bitcast(F32), 0.0).then_inc(prep_done, 1)
                nc.gpsimd.memset(cols[:, :], 0.0).then_inc(prep_done, 1)
                for tile in (negm, wint):
                    nc.gpsimd.memset(tile[:, :].bitcast(F32), 0.0).then_inc(prep_done, 1)

            def set_ones():
                nc.gpsimd.memset(v1[:, :, :, DV:VW], 1.0).then_inc(prep_done, 1)

            clear_rows()
            set_ones()
            for row, first in ((0, 0), (32, HEADS)):
                pool.dma_start(bias[row:row + HEADS, :], b_if[0, first:first + HEADS].rearrange("(p a) -> p a", a=1))\
                    .then_inc(bias_loaded, 16)
            pool.dma_start(head_g[:, :], norm_g[0].rearrange("(h p) -> p h", p=P),
                           allow_slow_non_contiguous=True).then_inc(bias_loaded, 16)
            with pool.Fori(0, HALVES) as h:
                def squares(c):
                    pool.wait_ge(num_kept, h * 16 + c * 2 + 2)
                    pool.wait_ge(h_turned, past(h * 8 + c))
                    nc.gpsimd.tensor_tensor(hrow[:, :, :], num[:, :, 0:DV], num[:, :, 0:DV], ALU.mult)\
                        .then_inc(sq_done, 1)

                with pool.Fori(0, TILES) as c:
                    squares(c)
                pool.wait_ge(hg1_done, past(h * 8 + 8))
                pool.sem_inc(pool_passed, 1)
                for q in range(4):
                    pool.dma_start(res[:, 2 * q:2 * q + 2, :],
                                   x_rows[bass.ds(h * TILES + 2 * q, 2)].rearrange("t p d -> p t d"))\
                        .then_inc(res_loaded[q], 16)
                for i in range(TILES):
                    pool.wait_ge(dn_added, past(h * DN + (DN - 16 + 2 * i + 2)))
                    pool.sem_inc(pool_passed, 1)
                    pool.dma_start(out_rows[h * TILES + i], res[:, i, :]).then_inc(out_stored, 16)
                pool.wait_ge(gu_done, past(h * GU + GU))
                pool.sem_inc(pool_passed, 1)
                clear_rows()
                pool.wait_ge(out_stored, h * (16 * TILES) + 16 * TILES)
                pool.sem_inc(pool_passed, 1)
                set_ones()
            pool.wait_ge(out_stored, HALVES * 16 * TILES)

        @block.scalar
        def _(act):
            def norm_sum(i, src, junk):
                s = nv[:, i[1], :]
                nc.scalar.activation(junk, src, ACT.Square, accum_out=s[:, 0:1]).then_inc(ssq_done, 1)
                act.wait_ge(ssq_done, i[0] + 1)
                nc.scalar.activation(s[:, 2:3], s[:, 0:1], ACT.Ln, scale=1.0 / D, bias=eps[:, 0:1])\
                    .then_inc(lnv_done, 1)
                act.wait_ge(lnv_done, i[0] + 1)
                nc.scalar.activation(s[:, 3:4], s[:, 2:3], ACT.Exp, scale=-0.5).then_inc(rstd0_done, 1)

            def norm_hi(i, cols_, bank):
                act.wait_ge(xt_done, past(i + 1))
                nc.scalar.copy(u_hi[:, :, cols_], banks(bank, 2).rearrange("p (k t) -> p k t", k=KD))\
                    .then_inc(uhi_done, 1)

            def split_block(h, b):
                act.wait_ge(proj_done, past(h * PJ + groups_until(max(0, b - 1))))
                s, at, n = raw_of(b)
                act.wait_ge(raw_loaded[s], h * (16 * RAW) + 16 * (n + 1))
                nc.scalar.copy(wp_hi[b % 2][:, :, :], raw[s][:, :, at:at + P]).then_inc(split_hi, 1)

            def split_beside(h, c, s):
                act.wait_ge(proj_done, past(h * PJ + c * 2 + (groups_until(VB) + 1 - s)))
                act.wait_ge(raw_loaded[s], h * (16 * RAW) + c * 16 + 16 * (RAW_VB + 2 - s))
                nc.scalar.copy(wp_hi[s][:, :, :], raw[s][:, :, 0:P]).then_inc(split_hi, 1)

            def split_out(h, jj, s):
                act.wait_ge(wo_loaded[s], h * 32 + 16 * (jj + 1))
                rows = slice(4 * s, 4 * s + 4)
                nc.scalar.copy(wo[jj][0][:, rows, :], wo_raw[jj][:, rows, :]).then_inc(wohi_done, 1)

            def split_gate_up(h, n, f):
                for s in range(2):
                    act.wait_ge(raw_loaded[s], h * (16 * RAW) + n * 16 + 16 * (RAW_FF + 1))
                    nc.scalar.copy(gu_hi[f][:, s, :, :], raw[s][:, :, f * P:f * P + P]).then_inc(split_hi, 1)

            start_at_one(act, qk_kept, v_staged, ht_kept, o_gated)
            act.wait_ge(const_pool, EPS_SET)

            with act.Fori(0, HALVES) as h:
                nc.scalar.preload_act_table_set("natural_log_exp_and_others")
                act.wait_ge(gu_done, past(h * GU))
                for i in range(TILES):
                    act.wait_ge(x_loaded[i % 4], h * (4 * TILES) + 16 * (i // 4) + 16)
                    act.wait_ge(xt_done, past(h * XT + max(0, i - 1)))
                    norm_sum((h * XT + i, i % 2), x_in[i % 4][:, :], xn1[i % 2][:, :])
                    if i == 3:
                        act.wait_ge(dn_done, past(h * DN))
                        split_block(h, 0)
                    if i == 5:
                        split_block(h, 1)
                    if i >= 1:
                        norm_hi(h * XT + i - 1, slice((i - 1) * P, i * P), 4 + 2 * ((i - 1) % 2))
                norm_hi(h * XT + TILES - 1, slice(TOK - P, TOK), 4 + 2 * ((TILES - 1) % 2))

                act.wait_ge(if_loaded, h * 16 + 16)
                act.wait_ge(prep_done, h * 5 + 1)
                nc.scalar.copy(if_w[:, :, :].rearrange("p k (a c) -> p k a c", c=32)[:, :, 0:2, 0:HEADS],
                               if_raw[:, :, :].rearrange("p k (a c) -> p k a c", a=2)).then_inc(if_hi_done, 1)

                def gate_part(b):
                    if b == 1:
                        act.wait_ge(gate_dve, h * 13 + 3)
                        nc.scalar.activation(t2[:, :], t2[:, :], ACT.Exp).then_inc(gate_act, 1)
                        act.wait_ge(gate_act, h * 7 + 1)
                        nc.scalar.activation(t2[:, :], t2[:, :], ACT.Ln, bias=1.0).then_inc(gate_act, 1)
                    if b == 3:
                        act.wait_ge(gate_dve, h * 13 + 8)
                        nc.scalar.activation(cols[64:64 + HEADS, :], t3[:, :], ACT.Exp, scale=-1.0)\
                            .then_inc(gate_act, 1)
                        nc.scalar.copy(negm[0:HEADS, :], t4[:, :]).then_inc(gate_act, 1)
                        act.wait_ge(gate_dve, h * 13 + 11)
                        nc.scalar.activation(t2[:, :], t2[:, :], ACT.Exp).then_inc(gate_act, 1)
                        nc.scalar.activation(cols[32:32 + HEADS, :], t0[:, :], ACT.Exp).then_inc(gate_act, 1)
                        act.wait_ge(gate_act, h * 7 + 5)
                        nc.scalar.copy(wint[0:HEADS, :], t2[:, :]).then_inc(gate_act, 1)

                def keep_qk(b, t, n):
                    act.wait_ge(proj_done, past(h * PJ + n + 1))
                    nc.scalar.mul(qk[:, b, t * NB:t * NB + NB], banks(2 * (b % 2) + t),
                                  1.0 if b < 4 else float(DQK) ** -0.5).then_inc(qk_kept, 1)

                act.wait_ge(const_dve, 1)
                keep_qk(0, 0, 0)
                keep_qk(1, 0, 1)
                keep_qk(0, 1, 2)
                split_block(h, 2)
                gate_part(1)
                keep_qk(1, 1, 3)
                for b in range(2, QK_BLOCKS):
                    split_block(h, b + 1)
                    gate_part(b)
                    for t in range(TBS):
                        keep_qk(b, t, 2 * b + t)

                def stage_v(i, s):
                    act.wait_ge(proj_done, past(h * PJ + i + (groups_until(VA) + 1)))
                    if s is None:
                        act.wait_ge(vt_done, past(h * 16 + max(0, i - 1)))
                        s = i % 2
                    else:
                        act.wait_ge(vt_done, past(h * 16 + i - 1))
                    nc.scalar.copy(v_st[:, s, :], banks(s)).then_inc(v_staged, 1)

                def copy_qk(c):
                    nc.scalar.copy(qkc[:, :, :], qk[:, :, bass.ds(c * P, P)]).then_inc(qkc_ready, 1)

                act.wait_ge(colt_turned, h + 1)
                act.wait_ge(gate_dve, h * 13 + 13)
                act.wait_ge(gate_act, h * 7 + 7)
                act.wait_ge(qk_kept, past(h * 16 + 16))
                split_block(h, VA + 1)
                for b in range(VA, VB - 1):
                    stage_v(b - VA, None)
                    split_block(h, b + 2)
                copy_qk(h * 0)

                def decay_matrix(c):
                    act.wait_ge(darg_done, h * 8 + c + 1)
                    for i in range(HEADS):
                        nc.scalar.activation(dmat[:, i, :], ps[:, 4 + i // 4, (i % 4) * P:(i % 4) * P + P], ACT.Exp,
                                             bias=colt[:, c, i:i + 1]).then_inc(dmat_done, 1)

                def head_rstd(c):
                    act.wait_ge(post_step, h * 88 + c * 11 + 7)
                    nc.scalar.activation(hv[:, 6, :], hv[:, 5, :], ACT.Ln).then_inc(hln_done, 1)
                    act.wait_ge(hln_done, h * 8 + c + 1)
                    nc.scalar.activation(hv[:, 7, :], hv[:, 6, :], ACT.Exp, scale=-0.5).then_inc(hrs_done, 1)

                def keep_num(c, q):
                    act.wait_ge(h_done, past(h * 8 + c))
                    act.wait_ge(n_done, h * 16 + c * 2 + q + 1)
                    nc.scalar.copy(num[:, 4 * q:4 * q + 4, :].rearrange("p (g a) n -> p a g n", a=2),
                                   ps[:, 6:8, 0:2 * VW].rearrange("p a (g n) -> p a g n", g=2)).then_inc(num_kept, 1)

                def keep_turned(c):
                    act.wait_ge(h_turned, past(h * 8 + c + 1))
                    nc.scalar.copy(head_values(c), banks(4, 2).rearrange("p (k t) -> p k t", k=HEADS))\
                        .then_inc(ht_kept, 1)

                def sigmoid(j, bank, dst):
                    act.wait_ge(proj_done, past(h * PJ + j + (groups_until(OA) + 1)))
                    nc.scalar.activation(banks(bank), banks(bank), ACT.Exp, scale=-1.0).then_inc(o_step, 1)
                    act.wait_ge(o_step, h * 32 + j * 2 + 1)
                    nc.scalar.activation(banks(bank), banks(bank), ACT.Ln, bias=1.0).then_inc(o_step, 1)
                    act.wait_ge(o_step, h * 32 + j * 2 + 2)
                    nc.scalar.activation(dst, banks(bank), ACT.Exp, scale=-1.0).then_inc(o_gated, 1)

                def sigmoid_kept(j, bank):
                    sigmoid(j, bank, qk[:, bass.ds(j, 1), 0:NB].rearrange("p a n -> p (a n)"))

                def chunk(c, is_first, v_before, v_beside, is_last=False):
                    if v_before:
                        stage_v(c * 2 + (V_BLOCKS - 1), 1)
                    decay_matrix(c)
                    if not v_before:
                        sigmoid_kept(c * 2 - 9, 1)
                    split_beside(h, c, 1)
                    keep_num(c, 0)
                    if not is_first:
                        keep_turned(c - 1)
                    keep_num(c, 1)
                    if not is_last:
                        act.wait_ge(s_done, h * 8 + c + 1)
                        act.wait_ge(qw_done, h * 8 + c + 1)
                        copy_qk(c + 1)
                    if v_beside:
                        stage_v(c * 2 + V_BLOCKS, 0)
                    else:
                        sigmoid_kept(c * 2 - 8, 0)
                    split_beside(h, c, 0)
                    head_rstd(c)

                act.wait_ge(colt_kept, h + 1)
                chunk(0, True, True, True)
                with act.Fori(1, TILES // 2) as c:
                    chunk(c, False, True, True)
                chunk(TILES // 2, False, True, False)
                with act.Fori(TILES // 2 + 1, TILES - 1) as c:
                    chunk(c, False, False, False)
                chunk(TILES - 1, False, False, False, True)

                sigmoid_kept(O_BLOCKS - 1, 1)
                keep_turned(TILES - 1)

                def split_gated(i):
                    nc.scalar.copy(u_hi[:, :, i * P:i * P + P], hg[:, :, i * P:i * P + P]).then_inc(hghi_done, 1)

                for u in range(OB, UNITS):
                    i = u - OB
                    if u + 1 < UNITS:
                        split_block(h, u + 1)
                    if i in (1, 2, 3, 4):
                        act.wait_ge(hg0_done, h * 8 + 8)
                        act.wait_ge(proj_done, past(h * PJ + groups_until(OB)))
                        split_gated(i - 1)
                    if i in (5, 6):
                        split_out(h, 0, i - 5)
                    sigmoid(O_BLOCKS + i, i % 2, banks(i % 2))

                act.wait_ge(hg1_done, past(h * 8 + 8))
                for i in range(TILES // 2, TILES):
                    split_gated(i)
                split_out(h, 1, 0)
                split_out(h, 1, 1)
                act.wait_ge(outp_done, past(h * 16 + 8))
                split_gate_up(h, 0, 0)
                split_gate_up(h, 0, 1)
                for i in range(TILES):
                    act.wait_ge(res_added, h * 16 + 8 + i + 1)
                    if i >= 2:
                        act.wait_ge(xt_done, past(h * XT + TILES + i - 1))
                    norm_sum((h * XT + TILES + i, i % 2), res[:, i, :], xn2[i % 2][:, :])
                    if i >= 2:
                        norm_hi(h * XT + TILES + i - 2, slice((i - 2) * P, (i - 1) * P), 4 + 2 * (i % 2))
                for i in range(TILES - 2, TILES):
                    norm_hi(h * XT + TILES + i, slice(i * P, i * P + P), 4 + 2 * (i % 2))

                def silu(n, o):
                    act.wait_ge(gu_done, past(h * GU + n * 4 + o + 1))
                    act.wait_ge(glo_done, past(h * GU + n * 4 + o - 1 if o >= 2 else h * GU + n * 4))
                    nc.scalar.activation(sg[:, o % 2, :], banks(2 * (o % 2)), ACT.Silu).then_inc(silu_done, 1)

                def hidden_hi(n, o):
                    act.wait_ge(gf_done, past(h * GU + n * 4 + o + 1))
                    act.wait_ge(dn_done, past(h * DN + n * 16 + (-8 if o < 2 else 0) if n is not first else h * DN))
                    nc.scalar.copy(g_hi[o % 2][o // 2][:, :], sg[:, o % 2, :]).then_inc(ghi_done, 1)

                def ffn_group(n, last):
                    if n is not first:
                        act.wait_ge(gu_done, past(h * GU + n * 4))
                        split_gate_up(h, n, 1)
                    silu(n, 0)
                    if n is first:
                        act.wait_ge(xt_done, past(h * XT + XT))
                    hidden_hi(n, 0)
                    act.wait_ge(dn_done, past(h * DN + n * 16))
                    for f in range(2):
                        act.wait_ge(dn_loaded[f], h * (16 * GROUPS) + n * 16 + 16)
                        nc.scalar.copy(dn_hi[:, f, :], dn_raw[:, f, :]).then_inc(dn_hi_done, 1)
                    silu(n, 1)
                    hidden_hi(n, 1)
                    silu(n, 2)
                    hidden_hi(n, 2)
                    if not last:
                        act.wait_ge(gu_done, past(h * GU + n * 4 + 3))
                        split_gate_up(h, n + 1, 0)
                    silu(n, 3)
                    hidden_hi(n, 3)

                first = 0
                ffn_group(first, False)
                with act.Fori(1, GROUPS - 1) as n:
                    ffn_group(n, False)
                ffn_group(GROUPS - 1, True)

        @block.vector
        def _(dve):
            def norm_var(i):
                s = nv[:, i[1], :]
                dve.wait_ge(ssq_done, i[0] + 1)
                nc.vector.tensor_scalar(s[:, 1:2], s[:, 0:1], -0.5 / D, -0.5 * EPS, ALU.mult, ALU.add)\
                    .then_inc(var_done, 1)
                dve.wait_ge(var_done, i[0] + 1)
                dve.wait_ge(rstd0_done, i[0] + 1)
                nc.vector.tensor_scalar(s[:, 5:6], s[:, 1:2], s[:, 3:4], s[:, 3:4], ALU.mult, ALU.mult)\
                    .then_inc(rstd_step, 1)
                dve.wait_ge(rstd_step, i[0] * 2 + 1)
                nc.vector.scalar_tensor_tensor(out=s[:, 6:7], in0=s[:, 5:6], scalar=1.5, in1=s[:, 3:4],
                                               op0=ALU.add, op1=ALU.mult).then_inc(rstd_step, 1)
                dve.wait_ge(rstd_step, i[0] * 2 + 2)

            def norm_rows(i, src, gain, dst):
                norm_var(i)
                nc.vector.scalar_tensor_tensor(out=dst, in0=src, scalar=nv[:, i[1], 6:7], in1=gain,
                                               op0=ALU.mult, op1=ALU.mult).then_inc(xn_done, 1)

            def norm_lo(i, cols_, bank):
                dve.wait_ge(uhi_done, i + 1)
                nc.vector.tensor_tensor(u_lo[:, :, cols_], banks(bank, 2).rearrange("p (k t) -> p k t", k=KD),
                                        u_hi[:, :, cols_].bitcast(F32), ALU.subtract).then_inc(ulo_done, 1)

            def split_block(h, b):
                dve.wait_ge(split_hi, h * SP_ + b + 1)
                s, at, _ = raw_of(b)
                nc.vector.tensor_tensor(wp_lo[b % 2][:, :, :], raw[s][:, :, at:at + P],
                                        wp_hi[b % 2][:, :, :].bitcast(F32), ALU.subtract).then_inc(split_lo, 1)

            def split_beside(h, c, s):
                dve.wait_ge(split_hi, h * SP_ + c * 2 + (VB + 3 - s))
                nc.vector.tensor_tensor(wp_lo[s][:, :, :], raw[s][:, :, 0:P], wp_hi[s][:, :, :].bitcast(F32),
                                        ALU.subtract).then_inc(split_lo, 1)

            def split_out(h, jj, s):
                dve.wait_ge(wohi_done, h * 4 + 2 * jj + s + 1)
                rows = slice(4 * s, 4 * s + 4)
                nc.vector.tensor_tensor(wo[jj][1][:, rows, :], wo_raw[jj][:, rows, :],
                                        wo[jj][0][:, rows, :].bitcast(F32), ALU.subtract).then_inc(wolo_done, 1)

            def split_gate_up(h, n, f):
                for s in range(2):
                    dve.wait_ge(split_hi, h * SP_ + n * 4 + (FF0 + 2 * f + s + 1))
                    nc.vector.tensor_tensor(gu_lo[f][:, s, :, :], raw[s][:, :, f * P:f * P + P],
                                            gu_hi[f][:, s, :, :].bitcast(F32), ALU.subtract).then_inc(split_lo, 1)

            start_at_one(dve, glo_done, split_lo, if_lo_done, h_done, gf_done, ulo_done, dn_added, v_kept,
                         state_done, sd_done, hg1_done)
            dve.wait_ge(const_pool, PICK_SET)
            nc.vector.tensor_copy(pick[:, :, :], pick_src[:, :, :]).then_inc(const_dve, 1)
            nc.vector.tensor_copy(ident_b[:, :], ident[:, :]).then_inc(const_dve, 1)

            with dve.Fori(0, HALVES) as h:
                dve.wait_ge(gain_loaded, h * 32 + 16)
                dve.sem_inc(dve_passed, 1)
                for i in range(TILES):
                    norm_rows((h * XT + i, i % 2), x_in[i % 4][:, :], gain1[:, :], xn1[i % 2][:, :])
                    if i == 3:
                        split_block(h, 0)
                    if i == 5:
                        split_block(h, 1)
                    if i >= 1:
                        norm_lo(h * XT + i - 1, slice((i - 1) * P, i * P), 4 + 2 * ((i - 1) % 2))
                norm_lo(h * XT + TILES - 1, slice(TOK - P, TOK), 4 + 2 * ((TILES - 1) % 2))

                dve.wait_ge(if_hi_done, h + 1)
                if_parts = if_w[:, :, :].rearrange("p k (a c) -> p k a c", c=32)
                nc.vector.tensor_tensor(if_parts[:, :, 2:4, 0:HEADS],
                                        if_raw[:, :, :].rearrange("p k (a c) -> p k a c", a=2),
                                        if_parts[:, :, 0:2, 0:HEADS].bitcast(F32), ALU.subtract)\
                    .then_inc(if_lo_done, 1)

                def per_chunk(tile):
                    return tile[:, :].rearrange("p (c t) -> p c t", t=P)

                def gate_part(b):
                    g = h * 13
                    if b == 0:
                        dve.wait_ge(bias_loaded, 48)
                        dve.wait_ge(const_pool, CONST_SET)
                        dve.wait_ge(if_done, h + 1)
                        pre = banks(4, 2)
                        for row, tile in ((0, t0), (32, t1)):
                            nc.vector.tensor_scalar(tile[:, :], pre[row:row + HEADS, :], bias[row:row + HEADS, 0:1],
                                                    None, ALU.add)
                        dve.drain()
                        for row, tile in ((64, t0), (96, t1)):
                            nc.vector.tensor_tensor(tile[:, :], pre[row:row + HEADS, :], tile[:, :], ALU.add)\
                                .then_inc(gate_dve, 1)
                        dve.wait_ge(gate_dve, g + 2)
                        nc.vector.scalar_tensor_tensor(out=t2[:, :], in0=t1[:, :], scalar=-1.0, in1=t1[:, :],
                                                       op0=ALU.mult, op1=ALU.min).then_inc(gate_dve, 1)
                    if b == 2:
                        dve.wait_ge(gate_act, h * 7 + 2)
                        nc.vector.scalar_tensor_tensor(out=t1[:, :], in0=t1[:, :], scalar=0.0, in1=t2[:, :],
                                                       op0=ALU.min, op1=ALU.subtract).then_inc(gate_dve, 1)
                        dve.wait_ge(gate_dve, g + 4)
                        nc.vector.tensor_tensor_scan(t3[:, :], t1[:, :], t0[:, :], m_end[:, 0:1], ALU.add, ALU.max)\
                            .then_inc(gate_dve, 1)
                        nc.vector.tensor_tensor_scan(t4[:, :], not_first[:, :], t1[:, :], 0.0, ALU.mult, ALU.add)\
                            .then_inc(gate_dve, 1)
                        dve.wait_ge(gate_dve, g + 6)
                        dve.wait_ge(prep_done, h * 5 + 4)
                        nc.vector.tensor_tensor(cols[0:HEADS, :], t0[:, :], t4[:, :], ALU.subtract)\
                            .then_inc(gate_dve, 1)
                        dve.wait_ge(gate_dve, g + 7)
                        nc.vector.tensor_tensor(t4[:, :], t4[:, :], t3[:, :], ALU.subtract).then_inc(gate_dve, 1)
                        dve.wait_ge(gate_dve, g + 8)
                        nc.vector.tensor_copy(m_prev[:, 0:1], m_end[:, 0:1]).then_inc(gate_dve, 1)
                        nc.vector.tensor_copy(m_prev[:, 1:TILES], per_chunk(t3)[:, 0:TILES - 1, P - 1])
                        dve.drain()
                        nc.vector.tensor_copy(m_end[:, 0:1], t3[:, TOK - 1:TOK])
                        nc.vector.tensor_tensor(per_chunk(t2), per_chunk(t4),
                                                m_prev[:, :].unsqueeze(2).broadcast_to([HEADS, TILES, P]), ALU.add)\
                            .then_inc(gate_dve, 1)
                        nc.vector.tensor_copy(nm_end[:, :], per_chunk(t4)[:, :, P - 1])
                        dve.drain()
                        nc.vector.tensor_tensor(per_chunk(t0), cols[0:HEADS, :].rearrange("p (c t) -> p c t", t=P),
                                                nm_end[:, :].unsqueeze(2).broadcast_to([HEADS, TILES, P]), ALU.add)\
                            .then_inc(gate_dve, 1)
                    if b == 4:
                        dve.wait_ge(gate_act, h * 7 + 7)
                        nc.vector.tensor_tensor(negm[32:32 + HEADS, :], t4[:, :], negm[0:HEADS, :].bitcast(F32),
                                                ALU.subtract).then_inc(gate_dve, 1)
                        nc.vector.tensor_tensor(wint[32:32 + HEADS, :], t2[:, :], wint[0:HEADS, :].bitcast(F32),
                                                ALU.subtract).then_inc(gate_dve, 1)
                    if b == 7:
                        dve.wait_ge(colt_turned, h + 1)
                        nc.vector.tensor_copy(colt[:, :, :],
                                              ps[:, 6:8, :].rearrange("p b (c n) -> p (b c) n", n=P)[:, :, 0:72])\
                            .then_inc(colt_kept, 1)

                for b in range(QK_BLOCKS):
                    if b > 0:
                        split_block(h, b + 1)
                    gate_part(b)

                dve.wait_ge(prep_done, h * 5 + 5)
                def keep_v(i, head, s, t):
                    dve.wait_ge(vt_done, past(h * 16 + i + 1))
                    where = v1[:, 4 * t:4 * t + 4, :, 0:DV]
                    if isinstance(head, int):
                        where = where[:, :, head, :]
                    else:
                        where = where[:, :, bass.ds(head, 1), :].rearrange("p c a n -> p (c a) n")
                    nc.vector.tensor_copy(where, banks(s).rearrange("p (c n) -> p c n", n=P)).then_inc(v_kept, 1)

                split_block(h, VA + 1)
                for b in range(VA, VB - 1):
                    split_block(h, b + 2)
                    keep_v(b - VA, b - VA, b % 2, 0)

                def weigh(c):
                    dve.wait_ge(wint_spread, h * 8 + c + 1)
                    nc.vector.tensor_copy(dec[:, :], banks(2).rearrange("p (g t) -> p g t", t=P)[:, :, P - 1])\
                        .then_inc(dec_done, 1)
                    dve.wait_ge(qkc_ready, h * 8 + c + 1)
                    nc.vector.tensor_tensor(qw[:, :, :], banks(2).rearrange("p (g t) -> p g t", t=P), qkc[:, 0:4, :],
                                            ALU.mult).then_inc(qw_done, 1)
                    dve.wait_ge(k_turned, h * 8 + c + 1)
                    nc.vector.tensor_tensor(kw[:, :, :], banks(3).rearrange("p (i n) -> p i n", n=DQK),
                                            colt[:, c, 32:32 + HEADS].unsqueeze(2).broadcast_to([P, HEADS, DQK]),
                                            ALU.mult).then_inc(kw_done, 1)

                def weigh_scores(c, q):
                    dve.wait_ge(s_done, h * 8 + c + 1)
                    dve.wait_ge(dmat_done, h * 64 + c * 8 + 4 * q + 4)
                    heads = dmat[:, 4 * q:4 * q + 4, :].rearrange("p (g a) t -> p g a t", a=2)
                    nc.vector.tensor_tensor(heads, ps[:, 6:8, 2 * q * P:2 * q * P + 2 * P]
                                            .rearrange("p a (g t) -> p g a t", g=2),
                                            heads, ALU.mult).then_inc(sd_done, 1)

                def update_state(c, g):
                    dve.wait_ge(n_done, h * 16 + c * 2 + g // 2 + 1)
                    dve.wait_ge(upd_done, h * 32 + c * 4 + g + 1)
                    for a in range(2):
                        r = slice(64 * a, 64 * a + 64)
                        nc.vector.scalar_tensor_tensor(out=state[r, g, :], in0=state[r, g, :], scalar=dec[r, g:g + 1],
                                                       in1=ps[r, 3 - g % 2, VW * a:VW * a + VW],
                                                       op0=ALU.mult, op1=ALU.add).then_inc(state_done, 1)

                def head_scale_a(c):
                    p0 = h * 88 + c * 11
                    dve.wait_ge(num_kept, h * 16 + c * 2 + 2)
                    nc.vector.scalar_tensor_tensor(out=hv[:, 0, :], in0=num[:, :, DV], scalar=-1.0,
                                                   in1=colt[:, c, 64:64 + HEADS], op0=ALU.mult, op1=ALU.max)\
                        .then_inc(post_step, 1)
                    dve.wait_ge(post_step, p0 + 1)
                    nc.vector.tensor_tensor(hv[:, 0, :], hv[:, 0, :], num[:, :, DV], ALU.max).then_inc(post_step, 1)
                    dve.wait_ge(post_step, p0 + 2)
                    nc.vector.reciprocal(hv[:, 1, :], hv[:, 0, :]).then_inc(post_step, 1)
                    dve.wait_ge(sq_done, h * 8 + c + 1)
                    nc.vector.tensor_reduce(hv[:, 2, :], hrow[:, :, :], AX_X, ALU.add).then_inc(post_step, 1)
                    dve.wait_ge(post_step, p0 + 4)
                    nc.vector.tensor_tensor(hv[:, 3, :], hv[:, 1, :], hv[:, 1, :], ALU.mult).then_inc(post_step, 1)
                    dve.wait_ge(post_step, p0 + 5)
                    nc.vector.tensor_tensor(hv[:, 4, :], hv[:, 3, :], hv[:, 2, :], ALU.mult).then_inc(post_step, 1)
                    dve.wait_ge(post_step, p0 + 6)
                    nc.vector.tensor_scalar(hv[:, 5, :], hv[:, 4, :], 1.0 / DV, EPS, ALU.mult, ALU.add)\
                        .then_inc(post_step, 1)

                def head_scale_b(c):
                    p0 = h * 88 + c * 11
                    dve.wait_ge(hrs_done, h * 8 + c + 1)
                    nc.vector.tensor_tensor(hv[:, 8, :], hv[:, 7, :], hv[:, 7, :], ALU.mult).then_inc(post_step, 1)
                    dve.wait_ge(post_step, p0 + 8)
                    nc.vector.scalar_tensor_tensor(out=hv[:, 9, :], in0=hv[:, 8, :], scalar=-0.5, in1=hv[:, 5, :],
                                                   op0=ALU.mult, op1=ALU.mult).then_inc(post_step, 1)
                    dve.wait_ge(post_step, p0 + 9)
                    nc.vector.scalar_tensor_tensor(out=hv[:, 8, :], in0=hv[:, 9, :], scalar=1.5, in1=hv[:, 7, :],
                                                   op0=ALU.add, op1=ALU.mult).then_inc(post_step, 1)
                    dve.wait_ge(post_step, p0 + 10)
                    nc.vector.tensor_tensor(hv[:, 0, :], hv[:, 8, :], hv[:, 1, :], ALU.mult).then_inc(post_step, 1)
                    dve.wait_ge(post_step, p0 + 11)
                    nc.vector.tensor_tensor(hrow[:, :, :], num[:, :, 0:DV],
                                            hv[:, 0, :].unsqueeze(2).broadcast_to([P, HEADS, DV]), ALU.mult)\
                        .then_inc(h_done, 1)

                def chunk(c, v_before, v_beside):
                    weigh(c)
                    if v_before:
                        if isinstance(c, int):
                            keep_v(2 * c + 7, (2 * c + 7) % V_BLOCKS, 1, 0 if c == 0 else 1)
                        else:
                            keep_v(c * 2 + 7, c * 2 - 1, 1, 1)
                    weigh_scores(c, 0)
                    weigh_scores(c, 1)
                    split_beside(h, c, 1)
                    for g in range(4):
                        update_state(c, g)
                    head_scale_a(c)
                    split_beside(h, c, 0)
                    head_scale_b(c)
                    if v_beside:
                        keep_v(c * 2 + 8, c * 2, 0, 1)

                chunk(0, True, True)
                with dve.Fori(1, TILES // 2) as c:
                    chunk(c, True, True)
                chunk(TILES // 2, True, False)
                with dve.Fori(TILES // 2 + 1, TILES) as c:
                    chunk(c, False, False)

                def gate_heads(i, t, sig):
                    return nc.vector.scalar_tensor_tensor(
                        out=hg[:, i, t * NB:t * NB + NB].rearrange("p (c n) -> p c n", n=P),
                        in0=v1[:, 4 * t:4 * t + 4, i, 0:DV], scalar=head_g[:, i:i + 1],
                        in1=sig.rearrange("p (c n) -> p c n", n=P), op0=ALU.mult, op1=ALU.mult)

                def split_gated(i):
                    dve.wait_ge(hghi_done, h * 8 + i + 1)
                    nc.vector.tensor_tensor(u_lo[:, :, i * P:i * P + P], hg[:, :, i * P:i * P + P],
                                            u_hi[:, :, i * P:i * P + P].bitcast(F32), ALU.subtract)\
                        .then_inc(hglo_done, 1)

                def gate_first(head):
                    dve.wait_ge(o_gated, past(h * 16 + head + 1))
                    gate_heads(head, 0, qk[:, head, 0:NB]).then_inc(hg0_done, 1)

                dve.wait_ge(ht_kept, past(h * 8 + 4))
                for head in range(HEADS - 1):
                    gate_first(head)
                for u in range(OB, UNITS):
                    i = u - OB
                    if u + 1 < UNITS:
                        split_block(h, u + 1)
                    if i == 0:
                        gate_first(HEADS - 1)
                        dve.wait_ge(ht_kept, past(h * 8 + 8))
                    if i in (1, 2, 3, 4):
                        split_gated(i - 1)
                    if i in (5, 6):
                        split_out(h, 0, i - 5)
                    dve.wait_ge(o_gated, past(h * 16 + O_BLOCKS + i + 1))
                    gate_heads(i, 1, banks(i % 2)).then_inc(hg1_done, 1)

                for i in range(TILES // 2, TILES):
                    split_gated(i)

                def add_out(i, jj):
                    m = jj * TILES + i
                    dve.wait_ge(res_loaded[i // 2], h * 16 + 16)
                    dve.wait_ge(outp_done, past(h * 16 + m + 1))
                    nc.vector.tensor_tensor(res[:, i, jj * NB:jj * NB + NB], banks((m + 2) % 4),
                                            res[:, i, jj * NB:jj * NB + NB], ALU.add).then_inc(res_added, 1)

                for i in range(TILES):
                    add_out(i, 0)
                    if i in (3, 4):
                        split_out(h, 1, i - 3)
                split_gate_up(h, 0, 0)
                split_gate_up(h, 0, 1)
                dve.wait_ge(gain_loaded, h * 32 + 32)
                for i in range(TILES):
                    add_out(i, 1)
                    norm_rows((h * XT + TILES + i, i % 2), res[:, i, :], gain2[:, :], xn2[i % 2][:, :])
                    if i >= 2:
                        norm_lo(h * XT + TILES + i - 2, slice((i - 2) * P, (i - 1) * P), 4 + 2 * (i % 2))
                for i in range(TILES - 2, TILES):
                    norm_lo(h * XT + TILES + i, slice(i * P, i * P + P), 4 + 2 * (i % 2))

                def hidden(n, o):
                    dve.wait_ge(silu_done, h * GU + n * 4 + o + 1)
                    nc.vector.tensor_tensor(sg[:, o % 2, :], banks(2 * (o % 2) + 1), sg[:, o % 2, :], ALU.mult)\
                        .then_inc(gf_done, 1)

                def hidden_lo(n, o):
                    dve.wait_ge(ghi_done, h * GU + n * 4 + o + 1)
                    nc.vector.tensor_tensor(g_lo[o % 2][o // 2][:, :], sg[:, o % 2, :],
                                            g_hi[o % 2][o // 2][:, :].bitcast(F32), ALU.subtract)\
                        .then_inc(glo_done, 1)

                def add_down(n, t, lo, hi):
                    for q in range(lo, hi):
                        i, jj = 4 * t + q // 2, q % 2
                        dve.wait_ge(dn_done, past(h * DN + n * 16 + (8 * t + q + 1)))
                        nc.vector.tensor_tensor(res[:, i, jj * NB:jj * NB + NB], banks(4 + q % 4),
                                                res[:, i, jj * NB:jj * NB + NB], ALU.add).then_inc(dn_added, 1)

                def ffn_group(n, is_first, is_last):
                    if not is_first:
                        split_gate_up(h, n, 1)
                    hidden(n, 0)
                    hidden_lo(n, 0)
                    if not is_first:
                        add_down(n - 1, 1, 0, 8)
                    for f in range(2):
                        dve.wait_ge(dn_hi_done, h * (2 * GROUPS) + n * 2 + f + 1)
                        nc.vector.tensor_tensor(dn_lo[:, f, :], dn_raw[:, f, :], dn_hi[:, f, :].bitcast(F32),
                                                ALU.subtract).then_inc(dn_lo_done, 1)
                    hidden(n, 1)
                    hidden_lo(n, 1)
                    hidden(n, 2)
                    hidden_lo(n, 2)
                    if not is_last:
                        add_down(n, 0, 0, 4)
                        split_gate_up(h, n + 1, 0)
                        add_down(n, 0, 4, 8)
                    hidden(n, 3)
                    hidden_lo(n, 3)
                    if is_last:
                        add_down(n, 0, 0, 8)

                ffn_group(0, True, False)
                with dve.Fori(1, GROUPS - 1) as n:
                    ffn_group(n, False, False)
                ffn_group(GROUPS - 1, False, True)
                add_down(GROUPS - 1, 1, 0, 8)

        @block.tensor
        def _(pe):
            def three_passes(out_, steps):
                n = len(steps)
                for k, (wh, wl, mh, ml) in enumerate(steps):
                    pe.matmul(out_, wh, ml, start=(k == 0), stop=False)
                    pe.matmul(out_, wh, mh, start=False, stop=False)
                    last = pe.matmul(out_, wl, mh, start=False, stop=(k == n - 1))
                return last

            def turn_rows(src, bank):
                for k in range(KD):
                    last = pe.transpose(ps[:, bank + k // 4, (k % 4) * P:(k % 4) * P + P], src[:, k * P:k * P + P],
                                        ident[:, :])
                last.then_inc(xt_done, 1)

            def project(s, bank, t, k0=0, k1=KD):
                now = slice(t * NB, t * NB + NB)
                for k in range(k0, k1):
                    wh, wl = wp_hi[s][:, k, :], wp_lo[s][:, k, :]
                    pe.matmul(banks(bank), wh, u_lo[:, k, now], start=(k == 0), stop=False, skip_group_check=True)
                    pe.matmul(banks(bank), wh, u_hi[:, k, now], start=False, stop=False, skip_group_check=True)
                    last = pe.matmul(banks(bank), wl, u_hi[:, k, now], start=False, stop=(k == KD - 1),
                                     skip_group_check=True)
                if k1 == KD:
                    last.then_inc(proj_done, 1)

            start_at_one(pe, outp_done, gu_done, h_turned, proj_done, xt_done, dn_done, vt_done)
            pe.wait_ge(const_pool, IDENT_SET)

            with pe.Fori(0, HALVES) as h:
                def turn_norm1(i):
                    pe.wait_ge(xn_done, h * XT + i + 1)
                    if i >= 2:
                        pe.wait_ge(ulo_done, past(h * XT + i - 1))
                    turn_rows(xn1[i % 2], 4 + 2 * (i % 2))

                pe.wait_ge(dn_added, past(h * DN))
                for i in range(5):
                    turn_norm1(i)
                pe.wait_ge(gf_done, past(h * GU))
                pe.wait_ge(ulo_done, past(h * XT + 4))
                pe.wait_ge(split_lo, past(h * SP_ + 1))
                project(0, 0, 0, 0, 3)
                turn_norm1(5)
                project(0, 0, 0, 3, KD)
                turn_norm1(6)
                pe.wait_ge(split_lo, past(h * SP_ + 2))
                project(1, 2, 0, 0, 3)
                turn_norm1(7)
                project(1, 2, 0, 3, KD)

                pe.wait_ge(if_lo_done, past(h + 1))
                for t in range(TBS):
                    pe.wait_ge(ulo_done, past(h * XT + TILES - 1 + t))
                    for k in range(KD):
                        for u in (u_lo, u_hi):
                            last = pe.matmul(banks(4 + t), if_w[:, k, :], u[:, k, t * NB:t * NB + NB],
                                             start=(k == 0 and u is u_lo), stop=(k == KD - 1 and u is u_hi))
                last.then_inc(if_done, 1)

                project(0, 1, 1)
                project(1, 3, 1)
                with pe.Fori(1, QK_BLOCKS // 2) as j:
                    for s in range(2):
                        pe.wait_ge(split_lo, past(h * SP_ + j * 2 + s + 1))
                        pe.wait_ge(qk_kept, past(h * 16 + j * 4 + (s - 1)))
                        for t in range(TBS):
                            project(s, 2 * s + t, t)

                pe.wait_ge(gate_act, h * 7 + 7)
                for c in range(TILES):
                    last = pe.transpose(ps[:, 6 + c // 4, (c % 4) * P:(c % 4) * P + P], cols[:, c * P:c * P + P],
                                        ident[:, :])
                last.then_inc(colt_turned, 1)

                pe.wait_ge(qk_kept, past(h * 16 + 14))

                def turn_v(i, s):
                    pe.wait_ge(v_staged, past(h * 16 + i + 1))
                    for q in range(4):
                        last = pe.transpose(ps[:, s, q * P:q * P + P], v_st[:, s, q * P:q * P + P], ident[:, :])
                    last.then_inc(vt_done, 1)

                def v_unit(j, s, is_first):
                    pe.wait_ge(split_lo, past(h * SP_ + j * 2 + (VA + s + 1)))
                    if not is_first:
                        pe.wait_ge(v_kept, past(h * 16 + j * 2 + s - 1))
                    project(s, s, 0, 0, KD // 2)
                    if s == 1 or not is_first:
                        turn_v(j * 2 + s - 1, 1 - s)
                    project(s, s, 0, KD // 2, KD)

                v_unit(0, 0, True)
                v_unit(0, 1, True)
                with pe.Fori(1, V_BLOCKS // 2) as j:
                    v_unit(j, 0, False)
                    v_unit(j, 1, False)

                def spread(c):
                    now = bass.ds(c * P, P)
                    pe.wait_ge(state_done, past(h * 64 + c * 8))
                    for g in range(4):
                        pair = pick[:, :, :].rearrange("p h c -> p (h c)")[:, 2 * g * P + DQK:2 * g * P + DQK + P]
                        last = pe.matmul(ps[:, 2, g * P:g * P + P], pair, wint[:, now],
                                         start=(g == 0), stop=(g == 3), skip_group_check=True)
                    last.then_inc(wint_spread, 1)
                    for half in range(2):
                        pe.matmul(banks(4 + half), ident_b[:, :], mask[:, :, :].rearrange("p a t -> p (a t)"),
                                  start=True, stop=False, skip_group_check=True)
                        for i in range(4):
                            last = pe.matmul(ps[:, 4 + half, i * P:i * P + P], pick[:, 4 * half + i, :], negm[:, now],
                                             start=False, stop=(i == 3), skip_group_check=True)
                    last.then_inc(darg_done, 1)
                    pe.wait_ge(qkc_ready, h * 8 + c + 1)
                    for g in range(4):
                        last = pe.transpose(ps[:, 3, g * P:g * P + P], qkc[:, 4 + g, :], ident[:, :])
                    last.then_inc(k_turned, 1)

                def scores(c, is_first):
                    if not is_first:
                        pe.wait_ge(num_kept, h * 16 + c * 2)
                    for g in range(4):
                        for a in range(2):
                            r = slice(64 * a, 64 * a + 64)
                            last = pe.matmul(ps[:, 6 + a, g * P:g * P + P], qkc[r, 4 + g, :],
                                             qkc[r, g, :], start=True, stop=True, skip_group_check=True)
                    last.then_inc(s_done, 1)

                def state_sum(c, g):
                    if g == 0:
                        pe.wait_ge(kw_done, h * 8 + c + 1)
                    elif g == 1:
                        pe.wait_ge(qw_done, h * 8 + c + 1)
                        pe.wait_ge(dec_done, h * 8 + c + 1)
                    else:
                        pe.wait_ge(state_done, past(h * 64 + c * 8 + 2 * (g - 1)))
                    pe.matmul(ps[:, 3 - g % 2, 0:2 * VW], kw[:, 2 * g:2 * g + 2, :], v1[:, c, 2 * g:2 * g + 2, :],
                              start=True, stop=True).then_inc(upd_done, 1)

                def outputs(c, q):
                    if q == 1:
                        pe.wait_ge(num_kept, h * 16 + c * 2 + 1)
                    else:
                        pe.wait_ge(sd_done, past(h * 16 + c * 2 + 2))
                        pe.wait_ge(qw_done, h * 8 + c + 1)
                    for g in (2 * q, 2 * q + 1):
                        w = slice((g % 2) * VW, (g % 2) * VW + VW)
                        for a in range(2):
                            r = slice(64 * a, 64 * a + 64)
                            pe.matmul(ps[:, 6 + a, w], qw[r, g, :], state[r, g, :], start=(g % 2 == 0), stop=False,
                                      skip_group_check=True)
                    for g in (2 * q, 2 * q + 1):
                        w = slice((g % 2) * VW, (g % 2) * VW + VW)
                        for a in range(2):
                            last = pe.matmul(ps[:, 6 + a, w], dmat[:, 2 * g + a, :], v1[:, c, 2 * g + a, :],
                                             start=False, stop=(g % 2 == 1), skip_group_check=True)
                    last.then_inc(n_done, 1)

                def turn_heads(c):
                    pe.wait_ge(h_done, past(h * 8 + c + 1))
                    for i in range(HEADS):
                        last = pe.transpose(ps[:, 4 + i // 4, (i % 4) * P:(i % 4) * P + P], hrow[:, i, :],
                                            ident[:, :])
                    last.then_inc(h_turned, 1)

                def beside(c, s, k0, k1, v_before, v_beside):
                    if k0 == 0:
                        pe.wait_ge(split_lo, past(h * SP_ + c * 2 + (VB + s + 1)))
                        if v_before:
                            pe.wait_ge(v_kept, past(h * 16 + c * 2 + (V_BLOCKS - 1 + s)))
                        else:
                            pe.wait_ge(o_gated, past(h * 16 + c * 2 - 9 + s))
                    project(s, s, 1 if v_beside else 0, k0, k1)

                def chunk(c, is_first, v_before, v_beside):
                    if not is_first:
                        pe.wait_ge(ht_kept, past(h * 8 + c - 1))
                    spread(c)
                    scores(c, is_first)
                    if v_before:
                        turn_v(c * 2 + (V_BLOCKS - 1), 1)
                    beside(c, 0, 0, 3, v_before, v_beside)
                    if isinstance(c, int):
                        pe.wait_ge(v_kept, past(h * 16 + c * 2 + V_BLOCKS))
                    state_sum(c, 0)
                    state_sum(c, 1)
                    outputs(c, 0)
                    if not is_first:
                        pe.wait_ge(dmat_done, h * 64 + c * 8 + 8)
                        turn_heads(c - 1)
                    beside(c, 0, 3, 5, v_before, v_beside)
                    state_sum(c, 2)
                    state_sum(c, 3)
                    outputs(c, 1)
                    beside(c, 0, 5, KD, v_before, v_beside)
                    beside(c, 1, 0, 4, v_before, v_beside)
                    if v_beside:
                        turn_v(c * 2 + V_BLOCKS, 0)
                    beside(c, 1, 4, KD, v_before, v_beside)

                pe.wait_ge(qk_kept, past(h * 16 + 16))
                pe.wait_ge(gate_dve, h * 13 + 13)
                pe.wait_ge(colt_kept, h + 1)
                pe.wait_ge(const_pool, CONST_SET)
                pe.wait_ge(const_dve, 2)
                chunk(0, True, True, True)
                with pe.Fori(1, TILES // 2) as c:
                    chunk(c, False, True, True)
                chunk(TILES // 2, False, True, False)
                with pe.Fori(TILES // 2 + 1, TILES) as c:
                    chunk(c, False, False, False)
                def o_unit(j, s, is_first):
                    pe.wait_ge(split_lo, past(h * SP_ + j * 2 + (OB + s + 1)))
                    if is_first:
                        pe.wait_ge(o_gated, past(h * 16 + O_BLOCKS - 1 + s))
                    else:
                        pe.wait_ge(hg1_done, past(h * 8 + j * 2 - 1 + s))
                    project(s, s, 1, 0, KD // 2)
                    if is_first and s == 0:
                        pe.wait_ge(ht_kept, past(h * 8 + TILES - 1))
                        turn_heads(TILES - 1)
                    project(s, s, 1, KD // 2, KD)

                o_unit(0, 0, True)
                o_unit(0, 1, True)
                with pe.Fori(1, O_BLOCKS // 2) as j:
                    o_unit(j, 0, False)
                    o_unit(j, 1, False)

                def out_group(i, jj):
                    m = jj * TILES + i
                    rows = slice(i * P, i * P + P)
                    if jj == 0:
                        pe.wait_ge(hglo_done, h * 8 + i + 1)
                    if m >= 4:
                        pe.wait_ge(res_added, h * 16 + m - 3)
                    elif m >= 2:
                        pe.wait_ge(hg1_done, past(h * 8 + 8))
                    three_passes(banks((m + 2) % 4), [(u_hi[:, k, rows], u_lo[:, k, rows], wo[jj][0][:, k, :],
                                                 wo[jj][1][:, k, :]) for k in range(KD)]).then_inc(outp_done, 1)

                def turn_norm2(i):
                    pe.wait_ge(xn_done, h * XT + TILES + i + 1)
                    if i >= 2:
                        pe.wait_ge(ulo_done, past(h * XT + TILES + i - 1))
                    turn_rows(xn2[i % 2], 4 + 2 * (i % 2))

                pe.wait_ge(state_done, past(h * 64 + 64))
                pe.wait_ge(ht_kept, past(h * 8 + 8))
                pe.wait_ge(wolo_done, h * 4 + 2)
                for i in range(TILES):
                    out_group(i, 0)
                pe.wait_ge(wolo_done, h * 4 + 4)
                for i in range(TILES):
                    out_group(i, 1)
                    if i >= 2:
                        turn_norm2(i - 2)

                def gate_up(n, o):
                    f, t = o % 2, o // 2
                    pe.wait_ge(split_lo, past(h * SP_ + n * 4 + (FF0 + 2 * f + 2)))
                    if o < 2 and isinstance(n, int) and n == 0:
                        pe.wait_ge(gf_done, past(h * GU))
                    else:
                        pe.wait_ge(gf_done, past(h * GU + n * 4 + o - 1))
                    for s in range(2):
                        last = three_passes(banks(2 * (o % 2) + s),
                                            [(gu_hi[f][:, s, k, :], gu_lo[f][:, s, k, :],
                                              u_hi[:, k, t * NB:t * NB + NB], u_lo[:, k, t * NB:t * NB + NB])
                                             for k in range(KD)])
                    last.then_inc(gu_done, 1)

                def down(n, t):
                    pe.wait_ge(glo_done, past(h * GU + n * 4 + (2 * t + 2)))
                    pe.wait_ge(dn_lo_done, h * (2 * GROUPS) + n * 2 + 2)
                    for q in range(8):
                        i, jj = q // 2, q % 2
                        c = slice(i * P, i * P + P)
                        w = slice(jj * NB, jj * NB + NB)
                        if q >= 4 or not (isinstance(n, int) and n == 0 and t == 0):
                            pe.wait_ge(dn_added, past(h * DN + n * 16 + (8 * t + q - 3)))
                        elif q == 0:
                            pe.wait_ge(dn_added, past(h * DN))
                        three_passes(banks(4 + q % 4), [(g_hi[f][t][:, c], g_lo[f][t][:, c], dn_hi[:, f, w],
                                                         dn_lo[:, f, w]) for f in range(2)]).then_inc(dn_done, 1)

                def ffn_group(n, is_first, is_last=False):
                    gate_up(n, 0)
                    if is_first:
                        turn_norm2(TILES - 2)
                        turn_norm2(TILES - 1)
                    else:
                        down(n - 1, 1)
                    gate_up(n, 1)
                    if is_first:
                        pe.wait_ge(ulo_done, past(h * XT + XT))
                    gate_up(n, 2)
                    if not is_last:
                        down(n, 0)
                    gate_up(n, 3)
                    if is_last:
                        down(n, 0)

                pe.wait_ge(res_added, h * 16 + 16)
                pe.wait_ge(ulo_done, past(h * XT + TILES + 4))
                ffn_group(0, True)
                with pe.Fori(1, GROUPS - 1) as n:
                    ffn_group(n, False)
                ffn_group(GROUPS - 1, False, True)
                down(GROUPS - 1, 1)


_INS = ['x', 'mix_norm_g', 'ffn_norm_g', 'ffn_w_gate', 'ffn_w_up', 'ffn_w_down', 'ml_w_in', 'ml_b_if', 'ml_norm_g',
        'ml_w_out']
_OUTS = [((1, SEQ, D), 'float32')]


def kernel(**inputs):
    import numpy as _np
    import concourse.bacc as _bacc
    from concourse import mybir as _mybir
    from concourse.bass_utils import run_bass_kernel_spmd as _run

    nc = _bacc.Bacc("TRN2", target_bir_lowering=False, num_devices=1)
    arrays, args = {}, []
    for name in _INS:
        a = _np.ascontiguousarray(inputs[name])
        arrays[f"in_{name}_dram"] = a
        args.append(nc.dram_tensor(f"in_{name}_dram", a.shape, _mybir.dt.from_np(a.dtype), kind="ExternalInput").ap())
    for i, (shape, dtype) in enumerate(_OUTS):
        dt = _mybir.dt.from_np(_np.dtype(dtype))
        args.append(nc.dram_tensor(f"out_{i}_dram", shape, dt, kind="ExternalOutput").ap())
    mlstm_layer(nc, *args)
    r = _run(nc, [arrays], core_ids=[0])
    got = tuple(r.results[0][f"out_{i}_dram"] for i in range(len(_OUTS)))
    return got[0]
```
